# Optimizing a Trainium2 kernel written in Bass

```python
import math
import jax, jax.numpy as jnp
from jax import lax
import numpy as np

D_MODEL = 1024
BATCH = 1
SEQ = 256
DEPTH = 2

GRID_W = 64
CTX_LEN = 256
EPS = 1e-6

A_HEADS = 4
A_HEAD_DIM = 128
A_WIDTH = A_HEADS * A_HEAD_DIM
SHORT_CONV_W = 5
DELTA_CHUNK = 64
B_Q_HEADS = 8
B_KV_HEADS = 2
B_HEAD_DIM = 64
B_GROUP = B_Q_HEADS // B_KV_HEADS
B_WIDTH = B_Q_HEADS * B_HEAD_DIM
B_KV_WIDTH = B_KV_HEADS * B_HEAD_DIM
ROPE_AXIS_PAIRS = B_HEAD_DIM // 4
ROPE_THETA = 10000.0
Q_BLOCK = 128
OFF_Z_A = 3 * A_WIDTH
OFF_BA_A = OFF_Z_A + A_WIDTH
OFF_Q_B = OFF_BA_A + 4 * A_HEADS
OFF_K_B = OFF_Q_B + B_WIDTH
OFF_V_B = OFF_K_B + B_KV_WIDTH
HYB_IN_WIDTH = OFF_V_B + B_KV_WIDTH
MIX_WIDTH = A_WIDTH + B_WIDTH
CONF_WIDTH = D_MODEL
CONF_KERNEL = 31
FFN_HIDDEN = ((8 * D_MODEL + 3 * 256 - 1) // (3 * 256)) * 256
N_EVEN = (DEPTH + 1) // 2
N_ODD = DEPTH // 2


F32 = jnp.float32

def rms_norm(x, gain):
    xf = x.astype(F32)
    y = xf * lax.rsqrt(jnp.mean(jnp.square(xf), axis=-1, keepdims=True) + EPS)
    return (y * gain.astype(F32)).astype(x.dtype)

def layer_norm(x, gain, bias):
    xf = x.astype(F32)
    mu = jnp.mean(xf, axis=-1, keepdims=True)
    var = jnp.mean(jnp.square(xf - mu), axis=-1, keepdims=True)
    return ((xf - mu) * lax.rsqrt(var + EPS) * gain.astype(F32) + bias.astype(F32)).astype(x.dtype)

def l2_normalize(x):
    return x * lax.rsqrt(jnp.sum(jnp.square(x), axis=-1, keepdims=True) + EPS)

def depthwise_conv_centred(x, w):
    pad = w.shape[0] // 2
    return lax.conv_general_dilated(
        x, w[:, None, :].astype(x.dtype), window_strides=(1,), padding=[(pad, pad)],
        dimension_numbers=("NWC", "WIO", "NWC"), feature_group_count=x.shape[-1])

def ada_terms(cond, w_mod, b_mod):
    m = jax.nn.silu(cond) @ w_mod + b_mod
    return jnp.split(m, 6, axis=-1)

def modulate(h, shift, scale):
    return h * (1.0 + scale) + shift

def axial_rope_tables(n_tokens):
    rows = n_tokens // GRID_W
    row = jnp.broadcast_to(jnp.arange(rows, dtype=F32)[:, None], (rows, GRID_W)).reshape(n_tokens)
    col = jnp.broadcast_to(jnp.arange(GRID_W, dtype=F32)[None, :], (rows, GRID_W)).reshape(n_tokens)
    inv_freq = ROPE_THETA ** (-jnp.arange(ROPE_AXIS_PAIRS, dtype=F32) / ROPE_AXIS_PAIRS)
    ang_r = row[:, None] * inv_freq
    ang_c = col[:, None] * inv_freq
    ang = jnp.concatenate([ang_r, ang_r, ang_c, ang_c], axis=-1)
    return jnp.cos(ang), jnp.sin(ang)

def apply_axial_rope(x, cos, sin):
    xf = x.astype(F32)
    xr = xf.reshape(*x.shape[:-1], 2, 2, ROPE_AXIS_PAIRS)
    rot = jnp.stack([-xr[..., 1, :], xr[..., 0, :]], axis=-2).reshape(x.shape)
    return (xf * cos[None, :, None, :] + rot * sin[None, :, None, :]).astype(x.dtype)

def gated_delta_chunked(q, k, v, g, beta, s0, need_out):
    bsz, n_tok, n_h, _ = q.shape
    dv = v.shape[-1]
    n_ch = n_tok // DELTA_CHUNK

    def chunks(t):
        return t.reshape(bsz, n_ch, DELTA_CHUNK, n_h, -1).transpose(1, 0, 3, 2, 4)

    qc, kc, vc = chunks(q), chunks(k), chunks(v)
    gcum = jnp.cumsum(chunks(g[..., None])[..., 0], axis=-1)
    bc = chunks(beta[..., None])
    idx = jnp.arange(DELTA_CHUNK)
    incl = idx[:, None] >= idx[None, :]
    strict = idx[:, None] > idx[None, :]
    decay = jnp.exp(jnp.where(incl, gcum[..., :, None] - gcum[..., None, :], -jnp.inf))
    kb = kc * bc
    lower = jnp.where(strict, jnp.einsum("nbhcd,nbhsd->nbhcs", kb, kc) * decay, 0.0)
    eye = jnp.eye(DELTA_CHUNK, dtype=F32)
    rhs = jnp.concatenate([vc * bc, kb * jnp.exp(gcum)[..., None]], axis=-1)
    sol = lax.linalg.triangular_solve(lower + eye, rhs, left_side=True, lower=True, unit_diagonal=True)
    u, w = sol[..., :dv], sol[..., dv:]
    g_last = gcum[..., -1]
    k_tail = kc * jnp.exp(g_last[..., None] - gcum)[..., None]
    xs = (u, w, k_tail, g_last)
    if need_out:
        intra = jnp.einsum("nbhcd,nbhsd->nbhcs", qc, kc) * decay
        q_dec = qc * jnp.exp(gcum)[..., None]
        xs = xs + (q_dec, intra)

    def step(state, xs_i):
        u_i, w_i, kt_i, gl_i = xs_i[:4]
        v_new = u_i - jnp.einsum("bhcd,bhde->bhce", w_i, state)
        new_state = state * jnp.exp(gl_i)[..., None, None] + jnp.einsum("bhcd,bhce->bhde", kt_i, v_new)
        if need_out:
            qd_i, a_i = xs_i[4:]
            o_i = jnp.einsum("bhcd,bhde->bhce", qd_i, state) + jnp.einsum("bhcs,bhse->bhce", a_i, v_new)
            return new_state, o_i
        return new_state, None

    s_fin, o = lax.scan(step, s0, xs)
    if need_out:
        o = o.transpose(1, 0, 3, 2, 4).reshape(bsz, n_tok, n_h, dv)
    return o, s_fin

def bidirectional_delta(q, k, v, g, beta, s0_fwd, s0_bwd, need_out):
    o_f, s_f = gated_delta_chunked(q, k, v, g[:, :, 0], beta[:, :, 0], s0_fwd, need_out)
    rev = lambda t: jnp.flip(t, axis=1)
    o_b, s_b = gated_delta_chunked(rev(q), rev(k), rev(v), rev(g[:, :, 1]), rev(beta[:, :, 1]), s0_bwd, need_out)
    o = o_f + rev(o_b) if need_out else None
    return o, s_f, s_b

def split_hybrid_projection(p, conv_w, a_log, dt_bias, q_norm, k_norm):
    bsz, n_tok, _ = p.shape
    qkv = jax.nn.silu(depthwise_conv_centred(p[..., :OFF_Z_A], conv_w))
    qkv = qkv.astype(F32).reshape(bsz, n_tok, 3, A_HEADS, A_HEAD_DIM)
    qa = l2_normalize(qkv[:, :, 0]) * (A_HEAD_DIM ** -0.5)
    ka = l2_normalize(qkv[:, :, 1])
    va = qkv[:, :, 2]
    za = p[..., OFF_Z_A:OFF_BA_A].reshape(bsz, n_tok, A_HEADS, A_HEAD_DIM)
    ba = p[..., OFF_BA_A:OFF_Q_B].astype(F32).reshape(bsz, n_tok, 2, 2, A_HEADS)
    beta = jax.nn.sigmoid(ba[:, :, 0])
    g = -jnp.exp(a_log.astype(F32)) * jax.nn.softplus(ba[:, :, 1] + dt_bias.astype(F32))
    qb = rms_norm(p[..., OFF_Q_B:OFF_K_B].reshape(bsz, n_tok, B_Q_HEADS, B_HEAD_DIM), q_norm)
    kb = rms_norm(p[..., OFF_K_B:OFF_V_B].reshape(bsz, n_tok, B_KV_HEADS, B_HEAD_DIM), k_norm)
    vb = p[..., OFF_V_B:].reshape(bsz, n_tok, B_KV_HEADS, B_HEAD_DIM)
    return qa, ka, va, za, g, beta, qb, kb, vb

def attend(q, k, v):
    s = jnp.einsum("bqkgd,bskd->bkgqs", q, k, preferred_element_type=F32) * (B_HEAD_DIM ** -0.5)
    p = jax.nn.softmax(s, axis=-1).astype(v.dtype)
    return jnp.einsum("bkgqs,bskd->bqkgd", p, v)

def latent_attention_blocks(q, k, v):
    bsz, n_tok = q.shape[:2]
    nb = n_tok // Q_BLOCK
    qb = q.reshape(bsz, nb, Q_BLOCK, *q.shape[2:]).swapaxes(0, 1)
    o = lax.map(lambda blk: attend(blk, k, v), qb)
    return o.swapaxes(0, 1).reshape(bsz, n_tok, B_WIDTH)

def hybrid_mixer(a_lat, a_ctx, w_in, conv_w, a_log, dt_bias, out_norm, q_norm, k_norm, w_out, cos, sin, ctx_out):
    bsz, n_tok, _ = a_lat.shape
    n_ctx = a_ctx.shape[1]
    qa_l, ka_l, va_l, za_l, g_l, be_l, qb_l, kb_l, vb_l = split_hybrid_projection(
        a_lat @ w_in, conv_w, a_log, dt_bias, q_norm, k_norm)
    qa_c, ka_c, va_c, za_c, g_c, be_c, qb_c, kb_c, vb_c = split_hybrid_projection(
        a_ctx @ w_in, conv_w, a_log, dt_bias, q_norm, k_norm)

    zeros = jnp.zeros((bsz, A_HEADS, A_HEAD_DIM, A_HEAD_DIM), F32)
    o_ctx_a, s_fwd, s_bwd = bidirectional_delta(qa_c, ka_c, va_c, g_c, be_c, zeros, zeros, ctx_out)
    o_lat_a, _, _ = bidirectional_delta(qa_l, ka_l, va_l, g_l, be_l, s_fwd, s_bwd, True)

    def delta_readout(o, z, n):
        y = rms_norm(o, out_norm) * jax.nn.silu(z.astype(F32))
        return y.reshape(bsz, n, A_WIDTH).astype(a_lat.dtype)

    qb_l = apply_axial_rope(qb_l, cos, sin)
    kb_l = apply_axial_rope(kb_l, cos, sin)
    k_all = jnp.concatenate([kb_c, kb_l], axis=1)
    v_all = jnp.concatenate([vb_c, vb_l], axis=1)
    group = lambda t: t.reshape(*t.shape[:2], B_KV_HEADS, B_GROUP, B_HEAD_DIM)
    o_lat_b = latent_attention_blocks(group(qb_l), k_all, v_all)

    y_lat = jnp.concatenate([delta_readout(o_lat_a, za_l, n_tok), o_lat_b.astype(a_lat.dtype)], axis=-1) @ w_out
    y_ctx = None
    if ctx_out:
        o_ctx_b = attend(group(qb_c), kb_c, vb_c).reshape(bsz, n_ctx, B_WIDTH)
        y_ctx = jnp.concatenate([delta_readout(o_ctx_a, za_c, n_ctx), o_ctx_b.astype(a_ctx.dtype)], axis=-1) @ w_out
    return y_lat, y_ctx

def conformer_conv(h, w_in, b_in, dw_w, dw_b, ln_g, ln_b, w_out, b_out):
    val, gate = jnp.split(h @ w_in + b_in, 2, axis=-1)
    u = val * jax.nn.sigmoid(gate)
    u = depthwise_conv_centred(u, dw_w) + dw_b
    u = jax.nn.silu(layer_norm(u, ln_g, ln_b))
    return u @ w_out + b_out

def swiglu_ffn(h, w_in, w_out):
    gate, up = jnp.split(h @ w_in, 2, axis=-1)
    return (jax.nn.silu(gate) * up) @ w_out

def first_inputs(seed: int = 0) -> dict:
    key = jax.random.key(seed)
    ks = iter(jax.random.split(key, 40))
    D = D_MODEL

    def nrm(shape, scale):
        return jax.random.normal(next(ks), shape, F32) * scale

    def gain(shape):
        return 1.0 + nrm(shape, 0.05)

    a_log = jnp.log(jax.random.uniform(next(ks), (N_EVEN, 2, A_HEADS), F32, 1.0, 16.0))
    dt = jnp.exp(jax.random.uniform(next(ks), (N_EVEN, 2, A_HEADS), F32, math.log(1e-3), math.log(1e-1)))
    dt_bias = dt + jnp.log(-jnp.expm1(-dt))
    return {
        "x": nrm((BATCH, SEQ, D), 1.0),
        "c": nrm((BATCH, D), 1.0),
        "ctx": nrm((BATCH, CTX_LEN, D), 1.0),
        "c_ctx": nrm((D,), 1.0),
        "w_mod": nrm((DEPTH, D, 6 * D), 0.5 * D ** -0.5),
        "b_mod": nrm((DEPTH, 6 * D), 0.02),
        "g_mix_pre": gain((DEPTH, D)),
        "g_mix_post": gain((DEPTH, D)),
        "g_ffn_pre": gain((DEPTH, D)),
        "g_ffn_post": gain((DEPTH, D)),
        "w_ffn_in": nrm((DEPTH, D, 2 * FFN_HIDDEN), D ** -0.5),
        "w_ffn_out": nrm((DEPTH, FFN_HIDDEN, D), FFN_HIDDEN ** -0.5),
        "hyb_w_in": nrm((N_EVEN, D, HYB_IN_WIDTH), D ** -0.5),
        "hyb_conv_w": nrm((N_EVEN, SHORT_CONV_W, 3 * A_WIDTH), SHORT_CONV_W ** -0.5),
        "hyb_a_log": a_log,
        "hyb_dt_bias": dt_bias,
        "hyb_out_norm": gain((N_EVEN, A_HEAD_DIM)),
        "hyb_q_norm": gain((N_EVEN, B_HEAD_DIM)),
        "hyb_k_norm": gain((N_EVEN, B_HEAD_DIM)),
        "hyb_w_out": nrm((N_EVEN, MIX_WIDTH, D), MIX_WIDTH ** -0.5),
        "conf_w_in": nrm((N_ODD, D, 2 * CONF_WIDTH), D ** -0.5),
        "conf_b_in": nrm((N_ODD, 2 * CONF_WIDTH), 0.02),
        "conf_dw_w": nrm((N_ODD, CONF_KERNEL, CONF_WIDTH), CONF_KERNEL ** -0.5),
        "conf_dw_b": nrm((N_ODD, CONF_WIDTH), 0.02),
        "conf_ln_g": gain((N_ODD, CONF_WIDTH)),
        "conf_ln_b": nrm((N_ODD, CONF_WIDTH), 0.02),
        "conf_w_out": nrm((N_ODD, CONF_WIDTH, D), CONF_WIDTH ** -0.5),
        "conf_b_out": nrm((N_ODD, D), 0.02),
    }

def first_block(x, c, ctx, c_ctx, w_mod, b_mod, g_mix_pre, g_mix_post, g_ffn_pre, g_ffn_post, w_ffn_in, w_ffn_out,
              hyb_w_in, hyb_conv_w, hyb_a_log, hyb_dt_bias, hyb_out_norm, hyb_q_norm, hyb_k_norm, hyb_w_out,
              conf_w_in, conf_b_in, conf_dw_w, conf_dw_b, conf_ln_g, conf_ln_b, conf_w_out, conf_b_out):
    cos, sin = axial_rope_tables(x.shape[1])
    h, hc = x, ctx
    for layer in range(DEPTH):
        is_hybrid = layer % 2 == 0
        idx = layer // 2
        advance_ctx = any(j % 2 == 0 for j in range(layer + 1, DEPTH))
        sh1, sc1, gt1, sh2, sc2, gt2 = ada_terms(c[:, None, :], w_mod[layer], b_mod[layer])
        a = modulate(rms_norm(h, g_mix_pre[layer]), sh1, sc1)
        if is_hybrid or advance_ctx:
            csh1, csc1, cgt1, csh2, csc2, cgt2 = ada_terms(c_ctx, w_mod[layer], b_mod[layer])
            ac = modulate(rms_norm(hc, g_mix_pre[layer]), csh1, csc1)
        if is_hybrid:
            y, yc = hybrid_mixer(a, ac, hyb_w_in[idx], hyb_conv_w[idx], hyb_a_log[idx], hyb_dt_bias[idx],
                                 hyb_out_norm[idx], hyb_q_norm[idx], hyb_k_norm[idx], hyb_w_out[idx],
                                 cos, sin, advance_ctx)
        else:
            conf = (conf_w_in[idx], conf_b_in[idx], conf_dw_w[idx], conf_dw_b[idx],
                    conf_ln_g[idx], conf_ln_b[idx], conf_w_out[idx], conf_b_out[idx])
            y = conformer_conv(a, *conf)
            yc = conformer_conv(ac, *conf) if advance_ctx else None
        h = h + gt1 * rms_norm(y, g_mix_post[layer])
        f = swiglu_ffn(modulate(rms_norm(h, g_ffn_pre[layer]), sh2, sc2), w_ffn_in[layer], w_ffn_out[layer])
        h = h + gt2 * rms_norm(f, g_ffn_post[layer])
        if advance_ctx:
            hc = hc + cgt1 * rms_norm(yc, g_mix_post[layer])
            fc = swiglu_ffn(modulate(rms_norm(hc, g_ffn_pre[layer]), csh2, csc2), w_ffn_in[layer], w_ffn_out[layer])
            hc = hc + cgt2 * rms_norm(fc, g_ffn_post[layer])
    return h


DEPTH_2 = 1

CHUNK = 64
S5_WIDTH = 512
S5_GROUP = 16
S5_GROUPS = S5_WIDTH // S5_GROUP
S5_STATE = 64
CONV_WIDTH = 512
CONV_K = 3
ATTN_HEADS = 8
HEAD_DIM = 64
ATTN_WIDTH = ATTN_HEADS * HEAD_DIM
N_BRANCH = 3
MIX_WIDTH_2 = S5_WIDTH + CONV_WIDTH + ATTN_WIDTH
D_FF = 4 * D_MODEL
IN_WIDTH = S5_WIDTH + 3 * CONV_WIDTH + 3 * ATTN_WIDTH + ATTN_HEADS + N_BRANCH * D_MODEL
NEG_INF = -1e30


def rmsnorm(x, g):
    xf = x.astype(jnp.float32)
    y = xf * lax.rsqrt(jnp.mean(xf * xf, axis=-1, keepdims=True) + EPS)
    return (y * g.astype(jnp.float32)).astype(x.dtype)

def s5_mixer(u, a_re, a_im, log_dt, b_re, b_im, c_re, c_im, d_skip, w_glu):
    bsz, L, _ = u.shape
    f32 = jnp.float32
    uf = u.astype(f32).reshape(bsz, L, S5_GROUPS, S5_GROUP)
    lam = lax.complex(jnp.minimum(a_re.astype(f32), -1e-4), a_im.astype(f32))
    dt = jnp.exp(log_dt.astype(f32))[:, None]
    a_bar = jnp.exp(lam * dt)
    b = lax.complex(b_re.astype(f32), b_im.astype(f32))
    b_bar = ((a_bar - 1.0) / lam)[..., None] * b
    bu = lax.complex(jnp.einsum('gph,blgh->blgp', jnp.real(b_bar), uf),
                     jnp.einsum('gph,blgh->blgp', jnp.imag(b_bar), uf))
    a_seq = jnp.broadcast_to(a_bar, bu.shape)

    def combine(left, right):
        a_l, s_l = left
        a_r, s_r = right
        return a_r * a_l, a_r * s_l + s_r

    _, states = lax.associative_scan(combine, (a_seq, bu), axis=1)
    y = (jnp.einsum('ghp,blgp->blgh', c_re.astype(f32), jnp.real(states))
         - jnp.einsum('ghp,blgp->blgh', c_im.astype(f32), jnp.imag(states))
         + d_skip.astype(f32) * uf)
    y = jax.nn.gelu(y)
    y = y * jax.nn.sigmoid(jnp.einsum('blgh,ghk->blgk', y, w_glu.astype(f32)))
    return y.reshape(bsz, L, S5_WIDTH).astype(u.dtype)

def short_conv_mixer(x_in, gate_b, gate_c, conv_w):
    L = x_in.shape[1]
    v = gate_c * x_in
    vp = jnp.pad(v, ((0, 0), (CONV_K - 1, 0), (0, 0)))
    conv = vp[:, 0:L] * conv_w[0]
    for tap in range(1, CONV_K):
        conv = conv + vp[:, tap:tap + L] * conv_w[tap]
    return gate_b * conv

def forgetting_attention(q, k, v, f_logit, b_f):
    bsz, L, _ = q.shape
    q = q.reshape(bsz, L, ATTN_HEADS, HEAD_DIM)
    k = k.reshape(bsz, L, ATTN_HEADS, HEAD_DIM)
    v = v.reshape(bsz, L, ATTN_HEADS, HEAD_DIM)
    log_f = jax.nn.log_sigmoid((f_logit + b_f).astype(jnp.float32))
    cum = jnp.cumsum(log_f, axis=1).transpose(0, 2, 1)
    scale = HEAD_DIM ** -0.5
    outs = []
    for blk in range(L // Q_BLOCK):
        q0 = blk * Q_BLOCK
        kend = q0 + Q_BLOCK
        s = jnp.einsum('bqhd,bkhd->bhqk', q[:, q0:kend], k[:, :kend]).astype(jnp.float32) * scale
        s = s + cum[:, :, q0:kend, None] - cum[:, :, None, :kend]
        q_pos = q0 + jnp.arange(Q_BLOCK)
        k_pos = jnp.arange(kend)
        s = jnp.where(k_pos[None, :] <= q_pos[:, None], s, NEG_INF)
        p = jax.nn.softmax(s, axis=-1)
        outs.append(jnp.einsum('bhqk,bkhd->bqhd', p.astype(v.dtype), v[:, :kend]))
    return jnp.concatenate(outs, axis=1).reshape(bsz, L, ATTN_WIDTH)

def hybrid_layer(x, g_pre_mix, w_in, b_gate, a_re, a_im, log_dt, b_re, b_im, c_re, c_im,
                 d_skip, w_glu, conv_w, b_f, w_branch, w_out, g_post_mix, g_pre_mlp,
                 w_ff1, w_ff2, g_post_mlp):
    bsz, L, _ = x.shape
    h = rmsnorm(x, g_pre_mix)
    proj = jnp.einsum('bld,dn->bln', h, w_in)
    widths = [S5_WIDTH, CONV_WIDTH, CONV_WIDTH, CONV_WIDTH, ATTN_WIDTH, ATTN_WIDTH,
              ATTN_WIDTH, ATTN_HEADS, N_BRANCH * D_MODEL]
    offsets = np.cumsum(widths)[:-1].tolist()
    (u_s5, x_conv, b_conv, c_conv, q, k, v, f_logit, gate_logits) = jnp.split(proj, offsets, axis=-1)

    y_a = s5_mixer(u_s5, a_re, a_im, log_dt, b_re, b_im, c_re, c_im, d_skip, w_glu)
    y_b = short_conv_mixer(x_conv, b_conv, c_conv, conv_w)
    y_c = forgetting_attention(q, k, v, f_logit, b_f)

    gates = jax.nn.sigmoid((gate_logits + b_gate).astype(jnp.float32)).astype(x.dtype)
    gates = gates.reshape(bsz, L, N_BRANCH, D_MODEL)
    wa = w_branch[:S5_WIDTH]
    wb = w_branch[S5_WIDTH:S5_WIDTH + CONV_WIDTH]
    wc = w_branch[S5_WIDTH + CONV_WIDTH:]
    merged = (gates[:, :, 0] * jnp.einsum('blc,cd->bld', y_a, wa)
              + gates[:, :, 1] * jnp.einsum('blc,cd->bld', y_b, wb)
              + gates[:, :, 2] * jnp.einsum('blc,cd->bld', y_c, wc))
    mix = jnp.einsum('bld,de->ble', merged, w_out)
    x = x + rmsnorm(mix, g_post_mix)

    h = rmsnorm(x, g_pre_mlp)
    ff = jnp.einsum('blf,fd->bld', jnp.square(jax.nn.relu(jnp.einsum('bld,df->blf', h, w_ff1))), w_ff2)
    return x + rmsnorm(ff, g_post_mlp)

def second_inputs(seed: int = 0) -> dict:
    key = jax.random.key(seed)
    ks = jax.random.split(key, 24)
    f32 = jnp.float32
    nrm = lambda k, shape, s: (jax.random.normal(k, shape, f32) * s)
    G, P, H = S5_GROUPS, S5_STATE, S5_GROUP
    x = jax.random.normal(ks[0], (BATCH, SEQ, D_MODEL), f32)
    g_pre_mix = 1.0 + nrm(ks[1], (DEPTH_2, D_MODEL), 0.05)
    w_in = nrm(ks[2], (DEPTH_2, D_MODEL, IN_WIDTH), D_MODEL ** -0.5)
    b_gate = nrm(ks[3], (DEPTH_2, N_BRANCH * D_MODEL), 0.01)
    n_idx = jnp.arange(P, dtype=f32)
    s5_a_re = -0.5 + nrm(ks[4], (DEPTH_2, G, P), 0.01)
    s5_a_im = math.pi * n_idx + nrm(ks[5], (DEPTH_2, G, P), 0.01)
    s5_log_dt = jax.random.uniform(ks[6], (DEPTH_2, G), f32, math.log(1e-3), math.log(1e-1))
    s5_b_re = nrm(ks[7], (DEPTH_2, G, P, H), (2.0 * H) ** -0.5)
    s5_b_im = nrm(ks[8], (DEPTH_2, G, P, H), (2.0 * H) ** -0.5)
    s5_c_re = nrm(ks[9], (DEPTH_2, G, H, P), (2.0 * P) ** -0.5)
    s5_c_im = nrm(ks[10], (DEPTH_2, G, H, P), (2.0 * P) ** -0.5)
    s5_d = nrm(ks[11], (DEPTH_2, G, H), 1.0)
    s5_w_glu = nrm(ks[12], (DEPTH_2, G, H, H), H ** -0.5)
    conv_w = nrm(ks[13], (DEPTH_2, CONV_K, CONV_WIDTH), CONV_K ** -0.5)
    fox_b_f = jnp.linspace(1.0, 6.0, ATTN_HEADS, dtype=f32)[None, :] + nrm(ks[14], (DEPTH_2, ATTN_HEADS), 0.1)
    w_branch = nrm(ks[15], (DEPTH_2, MIX_WIDTH_2, D_MODEL), S5_WIDTH ** -0.5)
    w_out = nrm(ks[16], (DEPTH_2, D_MODEL, D_MODEL), D_MODEL ** -0.5)
    g_post_mix = 1.0 + nrm(ks[17], (DEPTH_2, D_MODEL), 0.05)
    g_pre_mlp = 1.0 + nrm(ks[18], (DEPTH_2, D_MODEL), 0.05)
    w_ff1 = nrm(ks[19], (DEPTH_2, D_MODEL, D_FF), D_MODEL ** -0.5)
    w_ff2 = nrm(ks[20], (DEPTH_2, D_FF, D_MODEL), D_FF ** -0.5)
    g_post_mlp = 1.0 + nrm(ks[21], (DEPTH_2, D_MODEL), 0.05)
    return {"x": x, "g_pre_mix": g_pre_mix, "w_in": w_in, "b_gate": b_gate,
            "s5_a_re": s5_a_re, "s5_a_im": s5_a_im, "s5_log_dt": s5_log_dt,
            "s5_b_re": s5_b_re, "s5_b_im": s5_b_im, "s5_c_re": s5_c_re, "s5_c_im": s5_c_im,
            "s5_d": s5_d, "s5_w_glu": s5_w_glu, "conv_w": conv_w, "fox_b_f": fox_b_f,
            "w_branch": w_branch, "w_out": w_out, "g_post_mix": g_post_mix,
            "g_pre_mlp": g_pre_mlp, "w_ff1": w_ff1, "w_ff2": w_ff2, "g_post_mlp": g_post_mlp}

def second_block(x, g_pre_mix, w_in, b_gate, s5_a_re, s5_a_im, s5_log_dt, s5_b_re, s5_b_im,
              s5_c_re, s5_c_im, s5_d, s5_w_glu, conv_w, fox_b_f, w_branch, w_out,
              g_post_mix, g_pre_mlp, w_ff1, w_ff2, g_post_mlp):
    for layer in range(DEPTH_2):
        x = hybrid_layer(x, g_pre_mix[layer], w_in[layer], b_gate[layer],
                         s5_a_re[layer], s5_a_im[layer], s5_log_dt[layer],
                         s5_b_re[layer], s5_b_im[layer], s5_c_re[layer], s5_c_im[layer],
                         s5_d[layer], s5_w_glu[layer], conv_w[layer], fox_b_f[layer],
                         w_branch[layer], w_out[layer], g_post_mix[layer], g_pre_mlp[layer],
                         w_ff1[layer], w_ff2[layer], g_post_mlp[layer])
    return x


def setup_inputs(seed=0):
    out = dict(first_inputs(seed))
    for name, value in second_inputs(seed + 1).items():
        if name != "x":
            out[name + "_2"] = value
    return out


def reference(
    x, c, ctx, c_ctx, w_mod, b_mod, g_mix_pre, g_mix_post, g_ffn_pre, g_ffn_post, w_ffn_in,
    w_ffn_out, hyb_w_in, hyb_conv_w, hyb_a_log, hyb_dt_bias, hyb_out_norm, hyb_q_norm,
    hyb_k_norm, hyb_w_out, conf_w_in, conf_b_in, conf_dw_w, conf_dw_b, conf_ln_g, conf_ln_b,
    conf_w_out, conf_b_out, g_pre_mix_2, w_in_2, b_gate_2, s5_a_re_2, s5_a_im_2, s5_log_dt_2,
    s5_b_re_2, s5_b_im_2, s5_c_re_2, s5_c_im_2, s5_d_2, s5_w_glu_2, conv_w_2, fox_b_f_2,
    w_branch_2, w_out_2, g_post_mix_2, g_pre_mlp_2, w_ff1_2, w_ff2_2, g_post_mlp_2,
):
    x = first_block(
        x, c, ctx, c_ctx, w_mod, b_mod, g_mix_pre, g_mix_post, g_ffn_pre, g_ffn_post, w_ffn_in,
        w_ffn_out, hyb_w_in, hyb_conv_w, hyb_a_log, hyb_dt_bias, hyb_out_norm, hyb_q_norm,
        hyb_k_norm, hyb_w_out, conf_w_in, conf_b_in, conf_dw_w, conf_dw_b, conf_ln_g, conf_ln_b,
        conf_w_out, conf_b_out,
    )
    return second_block(
        x, g_pre_mix_2, w_in_2, b_gate_2, s5_a_re_2, s5_a_im_2, s5_log_dt_2, s5_b_re_2,
        s5_b_im_2, s5_c_re_2, s5_c_im_2, s5_d_2, s5_w_glu_2, conv_w_2, fox_b_f_2, w_branch_2,
        w_out_2, g_post_mix_2, g_pre_mlp_2, w_ff1_2, w_ff2_2, g_post_mlp_2,
    )


_drawn_inputs = setup_inputs


def setup_inputs(seed=0):
    import zlib

    import numpy as np

    out = dict(_drawn_inputs(seed))
    spreads = {}
    factors = {'hyb_out_norm': 9.218,
     'hyb_q_norm': 8.0,
     'hyb_k_norm': 8.0,
     'conf_b_in': 6.629,
     'conf_dw_b': 4.382,
     'conf_ln_b': 7.177,
     'conf_b_out': 4.943,
     'b_gate_2': 8.0,
     's5_a_re_2': 64.0,
     's5_a_im_2': 34.496,
     's5_log_dt_2': 37.712,
     's5_b_re_2': 46.912,
     's5_b_im_2': 48.6,
     's5_c_re_2': 48.84,
     's5_c_im_2': 48.08}
    for name, (base, spread) in spreads.items():
        noise = np.random.default_rng([zlib.crc32(name.encode()), seed]).standard_normal(out[name].shape)
        drawn = base * np.exp(spread * noise) if base else spread * noise
        out[name] = __import__('jax').numpy.asarray(drawn.astype(out[name].dtype))
    for name, factor in factors.items():
        out[name] = (out[name] * factor).astype(out[name].dtype)
    return out
```

```python
from contextlib import ExitStack

import numpy as np

import concourse.bass as bass
from concourse import mybir

F32 = mybir.dt.float32
BF16 = mybir.dt.bfloat16
ALU = mybir.AluOpType
ACT = mybir.ActivationFunctionType
AXX = mybir.AxisListType.X

P = 128
D = 1024
T = 256
KT = D // P
TT = T // P
EPS = 1e-6
HD = 128
NH = 4
CONV_A = 5
AH, AHD = 8, 64
CONF_K = 31
FFN_H = 2816
NF = FFN_H // P
NF2 = 4 * D // P
HYB_T = 1296
HYB_TC = HYB_T // 4
CTX_T = 272
V2C = 260
BIG = 1.0e30
LEVELS = 7
S5T = 16
HALF_PI = float(np.pi / 2)
PI = float(np.float32(np.pi))
TWO_PI = float(2 * np.pi)
TWO_PI_PARTS = [6.28125, 0.0019350051879882812, float(2 * np.pi - 6.28125 - 0.0019350051879882812)]
ROUND = 12582912.0

MOD_C = 384
NMOD = 6 * D // MOD_C
MOD_CTX = 6
MOD0_PE = (0, 2, 4, 9, 13)
SUMS = {key: n for n, key in enumerate([(0, j) for j in range(NMOD) if j not in MOD0_PE]
                                       + [(1, j) for j in range(NMOD)])}

STREAM = [
    ("mod0", NMOD, 8 * MOD_C), ("hyb_f", 4, 3072), ("hyb_t", 4, 8 * HYB_TC), ("mod1", NMOD, 8 * MOD_C),
    ("hyb_o", 4, 2048), ("ffn0", NF, 3072), ("conf_i", 8, 2048), ("conf_o", 4, 2048),
    ("ffn1", NF, 3072), ("in_a", 4, 3072), ("in_v", 2, 8 * V2C), ("in_b", 4, 3072),
    ("in_g", 8, 3072), ("branch", 4, 3072), ("out2", 4, 2048), ("ff", NF2, 2048),
]
SLOTS = 4
SLOT = 3072
ORDERED = [("mod0", _j) for _j in range(NMOD)]
for _j in range(8):
    ORDERED += [("hyb_f", _j) if _j < 4 else ("hyb_t", _j - 4), ("mod1", 2 * _j), ("mod1", 2 * _j + 1)]
ORDERED += [(_name, _j) for _name, _chunks, _ in STREAM[4:] for _j in range(_chunks)]
CHUNK = {key: _n for _n, key in enumerate(ORDERED)}
FIRST = {_name: CHUNK[_name, 0] for _name, _, _ in STREAM}

COLS = [
    ("cond", 16), ("b_mod", 96), ("g_mix_pre", 16), ("g_mix_post", 16), ("g_ffn_pre", 16),
    ("g_ffn_post", 16), ("conf_b_in", 16), ("conf_dw_w", 8 * CONF_K), ("conf_dw_b", 8),
    ("conf_ln_g", 8), ("conf_ln_b", 8), ("hyb_conv", 12 * CONV_A), ("g_pre_mix_2", 8),
    ("b_gate_2", 24), ("conv_w_2", 12), ("g_post_mix_2", 8), ("g_pre_mlp_2", 8),
    ("g_post_mlp_2", 8), ("s5_d", 4), ("a_re", 16), ("a_im", 16), ("log_dt", 16),
]
ROWS = [("a_log", 8), ("dt_bias", 8), ("b_f", 8), ("out_norm", HD), ("qk_norm", 640)]
CONSTS = [
    ("ident", P), ("ones", P), ("le", P), ("lt", P), ("ge", P), ("gt", P), ("neg_f", P),
    ("neg_b", P), ("levels", 2 * LEVELS * P), ("cos", TT * AHD), ("sin", TT * AHD), ("tvec", 32),
]


def offsets(table):
    at, out = 0, {}
    for name, n in table:
        out[name] = (at, n)
        at += n
    return out, at


COL_AT, NCOLS = offsets(COLS)
ROW_AT, NROWS = offsets(ROWS)
CONST_AT, NCONSTS = offsets(CONSTS)


def constants():
    i = np.arange(P)
    a, b = i[:, None], i[None, :]
    out = {
        "ident": a == b, "ones": np.ones((P, P)), "le": a <= b, "lt": a < b, "ge": a >= b,
        "gt": a > b,
        "neg_f": np.where(b >= a, 0.0, -BIG), "neg_b": np.where(b <= a, 0.0, -BIG),
    }
    masks = []
    for direction in range(2):
        for level in range(LEVELS):
            w = 1 << level
            m = (a // (2 * w) == b // (2 * w)) & ((a // w) % 2 == 0) & ((b // w) % 2 == 1)
            masks.append(m.T if direction else m)
    out["levels"] = np.stack(masks, 1).reshape(P, -1)
    tok = np.arange(T)
    inv = np.float32(10000.0) ** (-np.arange(16, dtype=np.float32) / np.float32(16))
    row = (tok // 64).astype(np.float32)[:, None] * inv
    col = (tok % 64).astype(np.float32)[:, None] * inv
    ang = np.concatenate([row, row, col, col], -1).astype(np.float32)
    sign = np.where((np.arange(AHD) % 32) < 16, -1.0, 1.0)
    for name, v in (("cos", np.cos(ang)), ("sin", np.sin(ang) * sign)):
        out[name] = v.reshape(TT, P, AHD).transpose(1, 0, 2).reshape(P, -1)
    out["tvec"] = np.broadcast_to(np.concatenate([np.arange(16), 16 * np.arange(16)]), (P, 32))
    return np.concatenate([np.asarray(out[n], np.float32) for n, _ in CONSTS], 1)


class Chain:

    def __init__(self, engine, sem):
        self.engine, self.sem, self.n = engine, sem, 0

    def mark(self, ins):
        self.n += 1
        ins.then_inc(self.sem, 1)

    def sync(self):
        self.engine.wait_ge(self.sem, self.n)

    def __call__(self, ins):
        self.mark(ins)
        self.sync()


class Banks:

    def __init__(self):
        self.n = [0] * 8

    def take(self, bank):
        self.n[bank] += 1
        return bank, self.n[bank] - 1

    def turn(self, n, banks=(0, 1, 2, 3)):
        return [self.take(banks[i % len(banks)]) for i in range(n)]


BANKS = Banks()
USE = {}


def take_y(name):
    before = BANKS.n[4:7]
    USE[name] = BANKS.take(7), before


USE["norm0"] = BANKS.turn(4)
USE["norm1"] = BANKS.turn(4)
USE["hyb_f"] = BANKS.turn(12)
USE["hyb_t"] = BANKS.turn(10)
USE["att_qk"] = BANKS.turn(3)
NATT = AH * TT
USE["att_s"] = BANKS.turn(NATT, (0, 1, 2))
USE["att_t"] = BANKS.turn(NATT, (3, 4))
USE["att_o"] = BANKS.turn(AH // 2, (5,))
USE["to_tok"] = BANKS.turn(6, (0, 1, 2, 3, 4, 5)) + BANKS.turn(4, (6, 7))
USE["to_feat"] = BANKS.turn(6, (0, 1, 2, 3, 4, 5))
USE["gates"] = BANKS.take(6)
USE["decay"] = BANKS.turn(8)
USE["kq"] = BANKS.turn(2, (4, 5))
USE["kk"] = BANKS.turn(4, (6, 7))
USE["x1"] = BANKS.turn(8, range(8))
for _l in range(1, LEVELS):
    USE["p", _l] = BANKS.turn(8, range(8))
    USE["q", _l] = BANKS.turn(8, range(8))
    if _l < LEVELS - 1:
        USE["t", _l] = BANKS.turn(8, range(8))
for _s in range(4):
    for _d in range(2):
        if _s:
            USE["ks", _s, _d] = BANKS.take(_d)
    for _d in range(2):
        USE["vn", _s, _d] = BANKS.take(2 + _d)
        if _s >= 2:
            USE["os", _s, _d] = BANKS.take(4 + _d)
            USE["oi", _s, _d] = BANKS.take(6 + _d)
        if _s < 3:
            USE["ds", _s, _d] = BANKS.take(_d)
USE["y_t"] = BANKS.turn(2, (0, 1))
USE["row", 0] = BANKS.turn(2, (2, 3))
take_y(("y", 0))
USE["norm2"] = BANKS.turn(4)
USE["row", 1] = BANKS.turn(2, (0, 1))
USE["ffn0"] = BANKS.turn(NF)
take_y(("y", 1))
USE["norm3"] = BANKS.turn(4, (2, 3, 0, 1))
USE["conf_i"] = BANKS.turn(8)
USE["ln"] = BANKS.turn(2, (0, 1))
USE["row", 2] = BANKS.turn(2, (2, 3))
take_y(("y", 2))
USE["norm4"] = BANKS.turn(4)
USE["row", 3] = BANKS.turn(2, (0, 1))
USE["ffn1"] = BANKS.turn(NF)
take_y(("y", 3))
USE["norm5"] = BANKS.turn(4, (2, 3, 0, 1))
USE["in_a"] = BANKS.turn(12)
USE["in_v"] = BANKS.turn(4)
USE["b_bar"] = BANKS.turn(2, (4, 5))
USE["cum"] = BANKS.take(6)
USE["cum_k"] = BANKS.turn(4, (7,))
USE["in_b"] = BANKS.turn(12)
USE["in_g"] = BANKS.turn(24)
USE["s5_u"] = BANKS.turn(S5T, (4, 5))
USE["s5_y"], USE["glu"] = [], []
for _b in range(4):
    USE["s5_y"].append(BANKS.take(6))
    USE["glu"].append(BANKS.take(7))
USE["fa_s"] = BANKS.turn(NATT, (4, 5))
USE["fa_t"] = BANKS.turn(NATT, (7,))
USE["fa_o"] = BANKS.turn(AH // 2, (6,))
USE["branch"] = BANKS.turn(16)
USE["row", 4] = BANKS.turn(2, (0, 1))
take_y(("y", 4))
USE["norm6"] = BANKS.turn(4, (2, 3, 0, 1))
USE["row", 5] = BANKS.turn(2, (2, 3))
USE["ff"] = BANKS.turn(NF2)
take_y(("y", 5))

DONE = []
CHUNKS_OF = {_name: _chunks for _name, _chunks, _ in STREAM}
_used = 0
for _name, _j in ORDERED:
    _chunks = CHUNKS_OF[_name]
    if _name in ("mod0", "mod1") and (int(_name[3]), _j) in SUMS:
        DONE.append(("sums", SUMS[int(_name[3]), _j] + 1))
        continue
    if _name in ("hyb_f", "in_a", "in_b", "in_g"):
        _u = USE[_name][3 * _j + 2]
    elif _name == "hyb_t":
        _u = USE[_name][9 if _j == 3 else 2 * _j + 1]
    elif _name == "in_v":
        _u = USE[_name][2 * _j + 1]
    elif _name == "conf_i":
        _u = USE[_name][_j]
    elif _name == "branch":
        _u = USE[_name][4 * _j + 3]
    elif _j == _chunks - 1:
        _u = USE["y", {"hyb_o": 0, "ffn0": 1, "conf_o": 2, "ffn1": 3, "out2": 4, "ff": 5}[_name]][0]
    else:
        _u = None
    if _u is None:
        _used += 1
        DONE.append(("used", _used))
    else:
        DONE.append((_u[0], _u[1] + 1))


def used_before(name):
    return max([n for s, n in DONE[:FIRST[name]] if s == "used"], default=0)

ORDER = ((2, 3, 0, 1), (3, 2, 1, 0))


def build(nc, w, cols_in, rows_in, consts_in, b_out_in, c_bd_in, glu_in, b_in, x_in, ctx_in, out):
    ctx = ExitStack()
    with ctx:
        def sb(name, n, dt=F32):
            return ctx.enter_context(nc.sbuf_tensor(name, [P, n], dt))

        def sem(name):
            return ctx.enter_context(nc.semaphore(name))

        def view(t, at, *dims):
            n = int(np.prod(dims))
            v = t[:, at:at + n]
            if len(dims) == 2:
                return v.rearrange("p (a b) -> p a b", a=dims[0])
            if len(dims) == 3:
                return v.rearrange("p (a b c) -> p a b c", a=dims[0], b=dims[1])
            return v

        def bc_in(ap, n):
            return ap.unsqueeze(2).to_broadcast([ap.shape[0], ap.shape[1], n])

        def bc_out(ap, n):
            return ap.unsqueeze(1).to_broadcast([ap.shape[0], n, ap.shape[1]])

        ring = sb("ring", SLOTS * SLOT)
        h = view(sb("h", TT * D), 0, TT, D)
        ybuf_t = sb("ybuf", TT * D)
        nrm_t = sb("nrm", TT * D)
        ybuf, nrm = view(ybuf_t, 0, TT, D), view(nrm_t, 0, TT, D)
        aT_t = sb("aT", KT * 2 * T)
        aT = view(aT_t, 0, KT, 2 * T)
        consts = sb("consts", NCONSTS)
        cols = sb("cols", NCOLS)
        rows = sb("rows", NROWS)
        rowbc = sb("rowbc", D)
        diag = sb("diag", D)
        arena = sb("arena", 16384)
        tok_t = sb("tok", TT * (HYB_T - 512) + TT * CTX_T)
        z_t = sb("z", TT * 512)
        o_t = sb("o", 1024)
        yT_t = sb("yT", KT * T)
        yT = view(yT_t, 0, KT, T)
        sg, hT = view(arena, 0, 2, T), view(arena, 2 * T, 2, T)
        small = sb("small", 700)
        cond = sb("cond", 16)
        mod_t = sb("mod", 2 * 96)
        ngain = view(sb("ngain", 7 * KT), 0, 7, KT)
        nshift = view(sb("nshift", 7 * KT), 0, 7, KT)
        pcol = view(sb("pcol", 6 * KT), 0, 6, KT)
        zeros = sb("zeros", 512, BF16)
        brow = tok_t[:, 0:D]
        psum = ctx.enter_context(nc.psum_tensor("psum", [P, 8 * 512], F32))

        def bank(use):
            b = use[0] if isinstance(use, tuple) else use
            return psum[:, 512 * b:512 * b + 512]

        Y = psum[:, 2048:4096].rearrange("p (t n) -> p t n", t=TT)

        def slot(c):
            s = c % SLOTS
            return ring[:, s * SLOT:(s + 1) * SLOT]

        def col(name):
            at, n = COL_AT[name]
            return cols[:, at:at + n]

        def row(name):
            at, n = ROW_AT[name]
            return rows[:, at:at + n]

        def const(name):
            at, n = CONST_AT[name]
            return consts[:, at:at + n]

        macs, macs_ctx = view(yT_t, 0, 4, MOD_C), view(z_t, 0, 2, MOD_C)
        ident, ones = const("ident"), const("ones")
        levels = const("levels").rearrange("p (d l n) -> p d l n", d=2, l=LEVELS)
        cos_t = const("cos").rearrange("p (t n) -> p t n", t=TT)
        sin_t = const("sin").rearrange("p (t n) -> p t n", t=TT)
        modT = view(mod_t, 0, 2, 48, 2)

        _at = [0]

        def stat(n):
            _at[0] += n
            assert _at[0] <= 700
            return small[:, _at[0] - n:_at[0]]

        nss, nms, nsd, nrs = stat(14), stat(14), stat(14), stat(14)
        pss, pms, psd, prs = stat(12), stat(12), stat(12), stat(12)

        cv = view(arena, 0, 12, 2, T)
        cin = view(arena, 8192, 12, 2, T + 4)
        zgate = view(z_t, 0, TT, 512)
        ptok = view(tok_t, 0, TT, HYB_T - 512)
        pctx = view(tok_t, TT * (HYB_T - 512), TT, CTX_T)
        qk = view(arena, 8192, TT, 640)
        rot_a = view(arena, 9472, TT, 640)
        rot_b = view(arena, 10752, TT, 640)
        kctx = view(arena, 12032, TT, P)
        att_sq = arena[:, 10752:10752 + 1536]
        att_p = view(arena, 12288, 3, 512)
        att_pT = view(arena, 13824, 2, 4, T)
        att_r, att_ss = stat(24), stat(24)
        att_max, att_sum = stat(NATT), stat(NATT)
        att_inv = stat(NATT)
        qbT = view(rowbc, 0, 4, T)
        kbT = diag[:, 0:512]
        X = view(arena, 0, 8, 512)
        XT = view(arena, 4096, 8, 512)
        UT = view(arena, 8192, 8, 512)
        BP = view(arena, 12288, 8, 512)
        sq_kq = view(arena, 12288, 6, 512)
        kT = view(aT_t, 0, 2, NH, T)
        qT = view(aT_t, 2048, NH, T)
        S = view(aT_t, 3072, 2, 512)
        intraT = view(nrm_t, 0, 4, 512)
        vtok = view(ybuf_t, 0, 4, 512)
        ktok = view(tok_t, 0, 4, 512)
        o_sum = view(o_t, 0, TT, 512)
        qtok = o_sum
        r_st = view(arena, 12288, 2, 512)
        vn_st = view(arena, 12288 + 1024, 2, 512)
        kt_st = view(arena, 12288 + 2048, 2, 512)
        tmp_st = view(arena, 12288 + 3072, 2, 512)
        ymix = view(tok_t, 0, TT, 512)
        kq_ss, kq_r = stat(24), stat(24)
        ba = view(small, _at[0], 4, 16)
        stat(64)
        beta_t = stat(32)
        beta = beta_t.rearrange("p (s e) -> p s e", s=4)
        g_t, g_a, g_b = stat(32), stat(32), stat(32)
        g = g_t.rearrange("p (s e) -> p s e", s=4)
        na8 = stat(8)
        ngc = stat(32).rearrange("p (s e) -> p s e", s=4)
        eg = stat(32).rearrange("p (s e) -> p s e", s=4)
        etail = stat(32).rearrange("p (s e) -> p s e", s=4)
        etot = stat(32).rearrange("p (s e) -> p s e", s=4)
        ro_ss, ro_r = stat(8), stat(8)

        cu = view(arena, 0, KT, T + CONF_K - 1)
        cc = view(arena, 2304, KT, T)
        csq = view(arena, 4352, KT, T)
        csig = view(arena, 6400, 2, T)
        crs = arena[:, 6912:6912 + T]
        cout = csq

        ring_ready = [sem(f"ring_ready{s}") for s in range(SLOTS)]
        ring_used = sem("ring_used")
        bank_full = [sem(f"bank_full{b}") for b in range(8)]
        bank_free = [sem(f"bank_free{b}") for b in range(8)]
        x_loaded, ctx_loaded = sem("x_loaded"), sem("ctx_loaded")
        cols_loaded, consts_loaded = sem("cols_loaded"), sem("consts_loaded")
        rows_loaded, late_loaded, brow_loaded = sem("rows_loaded"), sem("late_loaded"), sem("brow_loaded")
        sums_ready = sem("sums_ready")
        mac = sem("mac")
        mod_mm = sem("mod_mm")
        cond_ready = sem("cond_ready")
        zeros_ready = sem("zeros_ready")
        margins = sem("margins")
        mod_ready = sem("mod_ready")
        norm_ss, norm_ms, norm_sd, norm_x = (sem(f"norm_{x}") for x in ("ss", "ms", "sd", "x"))
        post_ss, post_ms, post_sd = (sem(f"post_{x}") for x in ("ss", "ms", "sd"))
        h_ready = sem("h_ready")
        diag_ready = sem("diag_ready")
        act_on = sem("act_on")
        stored = sem("stored")
        act_c, dve_c, pool_c = sem("act_chain"), sem("dve_chain"), sem("pool_chain")


        conv_done, silu_done, zgate_ready = sem("conv_done"), sem("silu_done"), sem("zgate_ready")
        att_sq_ready, att_ms, att_sd, att_rope = sem("att_sq"), sem("att_ms"), sem("att_sd"), sem("att_rope")
        att_rs, att_mx, att_norm, att_half = sem("att_rs"), sem("att_mx"), sem("att_norm"), sem("att_half")
        kq_sq, kq_ms, kq_sd = sem("kq_sq"), sem("kq_ms"), sem("kq_sd")
        ba_ready, sp_in, sp_ready, g_ready = sem("ba_ready"), sem("sp_in"), sem("sp_ready"), sem("g_ready")
        gtri_ready, dsum, dmask, dec_ready = sem("gtri_ready"), sem("dsum"), sem("dmask"), sem("dec_ready")
        ut_part, ut_ready, xt_first = sem("ut_part"), sem("ut_ready"), sem("xt_first")
        blocks_ready = sem("blocks_ready")
        resid_ready, ktail_ready = sem("resid_ready"), sem("ktail_ready")
        ro_ms, ro_sd, y_mixed = sem("ro_ms"), sem("ro_sd"), sem("y_mixed")
        csig_ready, conv31, csq_ready, csq_done = sem("csig_ready"), sem("conv31"), sem("csq_ready"), sem("csq_done")
        ln_sd, ln_x, conf_out = sem("ln_sd"), sem("ln_x"), sem("conf_out")
        s5_par, s5_mag, s5_arg, s5_trig = sem("s5_par"), sem("s5_mag"), sem("s5_arg"), sem("s5_trig")
        bbar_ready, logf_in, logf_sp, logf_ready = sem("bbar_ready"), sem("logf_in"), sem("logf_sp"), sem("logf_ready")
        cdiag_ready, s5_tab, masked = sem("cdiag_ready"), sem("s5_tab"), sem("masked")
        s5_n = sem("s5_n")
        s5_state, s5_part = sem("s5_state"), sem("s5_part")
        gelu_done, ya_done, yb_done = sem("gelu_done"), sem("ya_done"), sem("yb_done")
        half_ready = sem("half_ready")
        fa_mx, fa_exp, fa_norm, fa_half = sem("fa_mx"), sem("fa_exp"), sem("fa_norm"), sem("fa_half")
        gates_ready, merged = sem("gates_ready"), sem("merged")

        uT, q2T, k2T = (view(arena, 1024 * n, 4, T) for n in range(3))
        v2 = view(arena, 3072, TT, 2 * V2C)
        cin2 = view(arena, 4112, 12, T + 2)
        gT = view(arena, 7208, 24, T)
        y_c = view(arena, 13352, 4, T)
        small_trig = view(arena, 14376, 2, S5T, 32)
        glu = view(arena, 15400, 4, P)
        bbd = view(arena, 7208, 2, 4, P)
        trig_tmp = view(arena, 8232, 6, 512)
        cdiag = view(arena, 11304, 2, 512)
        y_a, y_b = yT[:, 0:4, :], yT[:, 4:8, :]
        mT = view(tok_t, 0, KT, T)
        bT = view(tok_t, 0, 2, 4, P)
        c_bd = view(tok_t, 1024, 2, S5T, 32)
        ck0, ck1 = view(o_t, 0, AH, P), view(ybuf_t, 0, AH, T)
        etab = view(rowbc, 0, 2, 2, T)
        s5_m1, s5_m2 = diag[:, 0:512], diag[:, 512:1024]
        s5_wt, s5_zt = nrm_t[:, 0:512], nrm_t[:, 512:1024]
        s5_n1, s5_n2 = nrm_t[:, 1024:1536], nrm_t[:, 1536:2048]
        s_ri = view(z_t, 0, 2, 2, T)
        etmp = view(yT_t, 1024, 2, T)
        fa_p, fa_pT = view(nrm_t, 0, 3, T), view(nrm_t, 768, 2, 2, T)
        _s5 = [15912]

        def s5v(n=16):
            _s5[0] += n
            assert _s5[0] <= 16384
            return arena[:, _s5[0] - n:_s5[0]]

        lam_re, dt, mag, theta, rk, phi, phi_hi, phi_lo = (s5v() for _ in range(8))
        sin_h, cos_h, sin_t1, cos_t1, num_re, num_im, den, co_re, co_im = (s5v() for _ in range(9))
        s5_a, s5_b, s5_c = (s5v() for _ in range(3))
        logf, lf_z, lf_a = (s5v().rearrange("p (t e) -> p t e", t=2) for _ in range(3))
        cumq = s5v().rearrange("p (t e) -> p t e", t=2)
        fa_max, fa_sum, fa_inv = s5v(), s5v(), s5v()
        bc_arr = view(arena, 12328, 2, 256)
        glu_sig = view(yT_t, 1536, 2, T)
        halfpi, tick, vtick = sb("halfpi", 1), sb("tick", 1), sb("vtick", 1)
        m_ab, m_c = view(nrm_t, 0, 2, 512), view(nrm_t, 1024, 2, T)

        block = ctx.enter_context(nc.Block())

        def wait_free(pe, use):
            if use[1]:
                pe.wait_ge(bank_free[use[0]], use[1])

        def wait_full(eng, use):
            eng.wait_ge(bank_full[use[0]], use[1] + 1)

        def wait_read(eng, use):
            eng.wait_ge(bank_free[use[0]], use[1] + 1)

        def filled(ins, use):
            ins.then_inc(bank_full[use[0]], 1)

        def freed(ins, use):
            ins.then_inc(bank_free[use[0]], 1)

        @block.sync
        def _(sp):
            def load(c, name, j, i=0):
                width = w[name].shape[2]
                part = w[name][j, :, :] if isinstance(i, int) else \
                    w[name][bass.ds(j + i, 1), :, :].rearrange("a p n -> p (a n)")
                sp.dma_start(slot(c)[:, 0:width], part).then_inc(ring_ready[c % SLOTS], 16)

            def wait_used(c, i=0):
                if c >= SLOTS:
                    who, count = DONE[c - SLOTS]
                    if who in ("used", "sums"):
                        sp.wait_ge(ring_used if who == "used" else sums_ready, count + SLOTS * i)
                    else:
                        sp.wait_ge(bank_full[who], count + i)

            for c in range(FIRST["hyb_o"]):
                wait_used(c)
                load(c, *ORDERED[c])
            for name, n, _ in STREAM[4:]:
                c0 = FIRST[name]
                head = min(n, SLOTS)
                for j in range(head):
                    wait_used(c0 + j)
                    load(c0 + j, name, j)
                turns = (n - head) // SLOTS
                if turns > 1:
                    with sp.Fori(0, turns) as i:
                        for s in range(SLOTS):
                            wait_used(c0 + head + s, i)
                            load(c0 + head + s, name, head + s, SLOTS * i)
                    head += turns * SLOTS
                for j in range(head, n):
                    wait_used(c0 + j)
                    load(c0 + j, name, j)
            for t in range(TT):
                sp.wait_ge(h_ready, 10 + t + 1)
                sp.dma_start(out[t * P:(t + 1) * P, :], h[:, t, :]).then_inc(stored, 16)
            sp.wait_ge(stored, 16 * TT)

        @block.tensor
        def _(pe):
            mm = nc.tensor.matmul

            def wait_ring(c, i=0):
                pe.wait_ge(ring_ready[c % SLOTS], 16 * (c // SLOTS + 1) + 16 * i)

            def transposes(use, parts):
                wait_free(pe, use)
                for n, part in enumerate(parts):
                    last = nc.tensor.transpose(bank(use)[:, n * P:(n + 1) * P], part, ident)
                filled(last, use)

            def norm(i):
                pe.wait_ge(norm_x, 2 * (i + 1))
                src = ybuf if i == 0 else nrm
                for kp, use in enumerate(USE[f"norm{i}"]):
                    transposes(use, [src[:, t, k * P:(k + 1) * P]
                                     for k in (2 * kp, 2 * kp + 1) for t in range(TT)])

            def wait_aT(i):
                for use in USE[f"norm{i}"]:
                    wait_read(pe, use)

            def mod(layer, j):
                own = layer == 0 and j in MOD0_PE
                c = CHUNK[f"mod{layer}", j]
                if own:
                    wait_ring(c)
                else:
                    n = SUMS[layer, j]
                    pe.wait_ge(sums_ready, n + 1)
                for b in range(3):
                    at = 3584 - 512 * layer + 2 * (3 * j + b)
                    if own:
                        for k in range(KT):
                            last = mm(psum[:, at:at + 2], slot(c)[:, k * MOD_C + b * P:k * MOD_C + (b + 1) * P],
                                      cond[:, 2 * k:2 * k + 2], start=(k == 0), stop=(k == KT - 1))
                        continue
                    if layer == 0 and j < MOD_CTX:
                        mm(psum[:, at + 1:at + 2], macs_ctx[:, n % 2, b * P:(b + 1) * P], ones[:, 0:1], start=True, stop=True)
                    last = mm(psum[:, at:at + 1], macs[:, n % 4, b * P:(b + 1) * P], ones[:, 0:1], start=True, stop=True)
                last.then_inc(ring_used if own else mod_mm, 1)

            def feature_block(use, weights, rhs, out_at=0):
                for k in range(KT):
                    last = mm(bank(use)[:, out_at:out_at + rhs(k).shape[1]],
                              weights[:, k * P:(k + 1) * P], rhs(k), start=(k == 0), stop=(k == KT - 1))
                return last

            def row_bc(p):
                pe.wait_ge(diag_ready, p + 1)
                for half, use in enumerate(USE["row", p]):
                    wait_free(pe, use)
                    filled(mm(bank(use), ones, diag[:, half * 512:half * 512 + 512], start=True, stop=True), use)

            def wait_y(p):
                (b, n), before = USE["y", p]
                if n:
                    pe.wait_ge(bank_free[b], n)
                for q, count in enumerate(before):
                    if count:
                        pe.wait_ge(bank_free[4 + q], count)

            def out_rows(c0, lhs, p, wait=None, bias=False):
                wait_y(p)
                if bias:
                    for t in range(TT):
                        for half in range(2):
                            mm(Y[:, t, half * 512:half * 512 + 512], ones[0:1, :],
                               brow[0:1, half * 512:half * 512 + 512], start=True, stop=False)
                for c in range(4):
                    wait_ring(c0 + c)
                    for kk in range(2):
                        k = 2 * c + kk
                        if wait:
                            wait(k)
                        for t in range(TT):
                            for half in range(2):
                                at = kk * D + half * 512
                                last = mm(Y[:, t, half * 512:half * 512 + 512],
                                          lhs[:, k, t * P:(t + 1) * P], slot(c0 + c)[:, at:at + 512],
                                          start=(k == 0 and not bias), stop=(k == KT - 1))
                    if c < 3:
                        last.then_inc(ring_used, 1)
                    else:
                        filled(last, USE["y", p][0])

            def ffn(name, n, p, gated):
                c0, uses, at_out = FIRST[name], USE[name], (2 if gated else 1) * D
                wait_y(p)
                pe.wait_ge(zeros_ready, 1)
                for t in range(TT):
                    for half in range(2):
                        mm(Y[:, t, half * 512:half * 512 + 512], zeros[:, 0:P], zeros[:, :], start=True, stop=False)

                def block_in(c, use, i=0):
                    wait_ring(c, i)
                    if isinstance(i, int):
                        wait_free(pe, use)
                    else:
                        pe.wait_ge(bank_free[use[0]], use[1] + i)
                    last = feature_block(use, slot(c)[:, 0:D], lambda k: aT[:, k, 0:T])
                    if gated:
                        last = feature_block(use, slot(c)[:, D:2 * D], lambda k: aT[:, k, 0:T], T)
                    filled(last, use)

                def block_out(c, use, parity, i=0, stop=False):
                    pe.wait_ge(bank_free[use[0]], use[1] + 1 + i)
                    for t in range(TT):
                        for half in range(2):
                            last = mm(Y[:, t, half * 512:half * 512 + 512], hT[:, parity, t * P:(t + 1) * P],
                                      slot(c)[:, at_out + half * 512:at_out + half * 512 + 512],
                                      start=False, stop=stop)
                    if stop:
                        filled(last, USE["y", p][0])
                    else:
                        last.then_inc(ring_used, 1)

                for j in range(2):
                    block_in(c0 + j, uses[j])
                    if j:
                        block_out(c0, uses[0], 0)
                turns = (n - 2) // SLOTS
                with pe.Fori(0, turns) as i:
                    for q in range(SLOTS):
                        j = 2 + q
                        block_in(c0 + j, uses[j], i)
                        block_out(c0 + j - 1, uses[j - 1], (j - 1) % 2, i)
                for j in range(2 + SLOTS * turns, n):
                    block_in(c0 + j, uses[j])
                    block_out(c0 + j - 1, uses[j - 1], (j - 1) % 2)
                block_out(c0 + n - 1, uses[n - 1], (n - 1) % 2, 0, True)

            pe.wait_ge(consts_loaded, 16)
            pe.wait_ge(cond_ready, 1)
            held = []
            for j in range(NMOD):
                if j in MOD0_PE:
                    mod(0, j)
                else:
                    held.append(j)
                if len(held) > 1:
                    mod(0, held.pop(0))
            mod(0, held[0])
            norm(0)
            norm(1)
            wait_aT(0)
            wait_aT(1)

            for c in range(4):
                wait_ring(CHUNK["hyb_f", c])
                for b in range(3):
                    use = USE["hyb_f"][3 * c + b]
                    wait_free(pe, use)
                    width = 2 * T if 3 * c + b < 8 else T
                    last = feature_block(use, slot(CHUNK["hyb_f", c])[:, b * D:(b + 1) * D], lambda k: aT[:, k, 0:width])
                    filled(last, use)
                if c:
                    mod(1, 2 * c - 2)
                    mod(1, 2 * c - 1)

            uses = iter(USE["hyb_t"])
            for c in range(4):
                wait_ring(CHUNK["hyb_t", c])
                for tile in range(TT if c < 3 else 2 * TT):
                    use = next(uses)
                    wait_free(pe, use)
                    wt = slot(CHUNK["hyb_t", c])
                    for k in range(KT):
                        last = mm(bank(use)[:, 0:HYB_TC], aT[:, k, tile * P:(tile + 1) * P],
                                  wt[:, k * HYB_TC:(k + 1) * HYB_TC], start=(k == 0), stop=(k == KT - 1))
                    filled(last, use)
                mod(1, 2 * c + 6)
                mod(1, 2 * c + 7)
            mod(1, 14)
            mod(1, 15)

            pe.wait_ge(att_rope, 1)
            for t in range(TT):
                transposes(USE["att_qk"][t], [rot_a[:, t, m * P:(m + 1) * P] for m in range(4)])
            transposes(USE["att_qk"][2], [kctx[:, 0, :], kctx[:, 1, :], rot_a[:, 0, 512:640], rot_a[:, 1, 512:640]])
            for use in USE["att_qk"]:
                wait_read(pe, use)
            pe.wait_ge(mod_ready, 1)
            for n in range(NATT + 4):
                if n < NATT:
                    a, t = n // 2, n % 2
                    q0 = 64 * (a % 2)
                    use = USE["att_s"][n]
                    wait_free(pe, use)
                    filled(mm(bank(use), qbT[q0:q0 + 64, a // 2, t * P:(t + 1) * P], kbT[q0:q0 + 64, :],
                              start=True, stop=True), use)
                if 2 <= n < NATT + 2:
                    m = n - 2
                    pe.wait_ge(att_norm, m + 1)
                    transposes(USE["att_t"][m], [att_p[:, m % 3, kb * P:(kb + 1) * P] for kb in range(4)])
                if n >= 4 and n % 2 == 1:
                    a = (n - 4) // 2
                    wait_read(pe, USE["att_t"][2 * a + 1])
                    use = USE["att_o"][a // 2]
                    if a % 2 == 0:
                        wait_free(pe, use)
                    q0 = 64 * (a % 2)
                    for kb in range(4):
                        v = pctx[:, kb, 128 + q0:192 + q0] if kb < 2 else ptok[:, kb - 2, 640 + q0:704 + q0]
                        last = mm(bank(use)[q0:q0 + 64, 0:T], v, att_pT[:, a % 2, kb, :],
                                  start=(kb == 0), stop=(kb == 3))
                    if a % 2:
                        filled(last, use)
                    else:
                        last.then_inc(att_half, 1)

            pe.wait_ge(silu_done, 12)
            for n in range(4):
                seq, t = (n // 2, n % 2)
                transposes(USE["to_tok"][n], [cv[:, hh, seq, t * P:(t + 1) * P] for hh in range(NH)])
            for t in range(TT):
                transposes(USE["to_tok"][4 + t], [cv[:, 8 + hh, 0, t * P:(t + 1) * P] for hh in range(NH)])
            pe.wait_ge(mod_ready, 2)
            for n in range(4):
                seq, t = (n // 2, n % 2)
                transposes(USE["to_tok"][6 + n], [cv[:, 4 + hh, seq, t * P:(t + 1) * P] for hh in range(NH)])
            for n in range(6):
                wait_read(pe, USE["to_tok"][n])
                src = ktok[:, n, :] if n < 4 else qtok[:, n - 4, :]
                transposes(USE["to_feat"][n], [src[:, hh * P:(hh + 1) * P] for hh in range(NH)])
            use = USE["gates"]
            pe.wait_ge(g_ready, 1)
            wait_free(pe, use)
            for n, (name, d) in enumerate((("le", 0), ("ge", 1), ("gt", 0), ("lt", 1))):
                mm(bank(use)[:, 16 * n:16 * n + 16], const(name), g[:, :, 4 * d:4 * d + 4], start=True, stop=True)
            filled(mm(bank(use)[:, 64:96], ones, g_t, start=True, stop=True), use)
            for n in range(8):
                pe.wait_ge(gtri_ready, n + 1)
                use = USE["decay"][n]
                wait_free(pe, use)
                filled(mm(bank(use), ones, X[:, n, :], start=True, stop=True), use)
            for n in range(6):
                wait_read(pe, USE["to_feat"][n])

            def per_head(use, lhs, rhs, start=True, stop=True):
                for hh in range(NH):
                    last = mm(bank(use)[:, hh * P:(hh + 1) * P], lhs(hh), rhs(hh), start=True, stop=True)
                return last

            def feat(x, st, hh):
                return x[:, hh, (st % 2) * P:(st % 2 + 1) * P]

            for t in range(TT):
                use = USE["kq"][t]
                wait_free(pe, use)
                filled(per_head(use, lambda hh: feat(kT[:, 0], t, hh), lambda hh: feat(qT, t, hh)), use)
            for st in range(4):
                use = USE["kk"][st]
                wait_free(pe, use)
                kk = lambda hh: feat(kT[:, st // 2], st, hh)
                filled(per_head(use, kk, kk), use)
            hs = lambda x, n: (lambda hh: x[:, n, hh * P:(hh + 1) * P])
            for n in range(8):
                pe.wait_ge(xt_first, n + 1)
                transposes(USE["x1"][n], [XT[:, n, hh * P:(hh + 1) * P] for hh in range(NH)])
            for level in range(1, LEVELS):
                for n in range(8):
                    wait_read(pe, USE["x1"][n] if level == 1 else USE["t", level - 1][n])
                    pe.wait_ge(blocks_ready, 8 * (level - 1) + n + 1)
                    use = USE["p", level][n]
                    wait_free(pe, use)
                    filled(per_head(use, hs(BP, n), hs(X, n)), use)
                for n in range(8):
                    wait_read(pe, USE["p", level][n])
                    use = USE["q", level][n]
                    if level < LEVELS - 1:
                        filled(per_head(use, hs(XT, n), hs(BP, n)), use)
                    else:
                        filled(per_head(use, hs(BP, n), hs(XT, n)), use)
                if level < LEVELS - 1:
                    for n in range(8):
                        wait_read(pe, USE["q", level][n])
                        transposes(USE["t", level][n], [X[:, n, hh * P:(hh + 1) * P] for hh in range(NH)])
            for n in range(8):
                wait_read(pe, USE["q", LEVELS - 1][n])
            for s in range(4):
                for d in range(2):
                    st = ORDER[d][s]
                    if s:
                        wait_read(pe, USE["ds", s - 1, d])
                        use = USE["ks", s, d]
                        wait_free(pe, use)
                        filled(per_head(use, lambda hh: feat(kT[:, st // 2], st, hh),
                                        lambda hh: S[:, d, hh * P:(hh + 1) * P]), use)
                for d in range(2):
                    st = ORDER[d][s]
                    n = 4 * d + st
                    if s >= 2:
                        use = USE["os", s, d]
                        wait_free(pe, use)
                        filled(per_head(use, lambda hh: feat(qT, st, hh),
                                        lambda hh: S[:, d, hh * P:(hh + 1) * P]), use)
                    pe.wait_ge(resid_ready, 2 * s + d + 1)
                    use = USE["vn", s, d]
                    wait_free(pe, use)
                    filled(per_head(use, hs(XT, n), hs(r_st, d)), use)
                for d in range(2):
                    st = ORDER[d][s]
                    wait_read(pe, USE["vn", s, d])
                    if s < 3:
                        pe.wait_ge(ktail_ready, 2 * s + d + 1)
                        use = USE["ds", s, d]
                        wait_free(pe, use)
                        filled(per_head(use, hs(kt_st, d), hs(vn_st, d)), use)
                    if s >= 2:
                        use = USE["oi", s, d]
                        wait_free(pe, use)
                        filled(per_head(use, hs(intraT, 2 * d + st), hs(vn_st, d)), use)
            pe.wait_ge(y_mixed, 2)
            for t in range(TT):
                transposes(USE["y_t"][t], [ymix[:, t, hh * P:(hh + 1) * P] for hh in range(NH)])
            row_bc(0)
            for use in USE["y_t"] + USE["att_o"]:
                wait_read(pe, use)
            out_rows(FIRST["hyb_o"], yT, 0)
            norm(2)
            row_bc(1)
            wait_aT(2)
            ffn("ffn0", NF, 1, True)

            norm(3)
            wait_aT(3)
            c0 = FIRST["conf_i"]
            for c in range(8):
                wait_ring(c0 + c)
                use = USE["conf_i"][c]
                wait_free(pe, use)
                feature_block(use, slot(c0 + c)[:, 0:D], lambda k: aT[:, k, 0:T])
                filled(feature_block(use, slot(c0 + c)[:, D:2 * D], lambda k: aT[:, k, 0:T], T), use)
            for n, src in enumerate((cc, csq)):
                use = USE["ln"][n]
                wait_free(pe, use)
                for k in range(KT):
                    pe.wait_ge((conv31, csq_done)[n], k + 1)
                    last = mm(bank(use)[:, 0:T], ones, src[:, k, :], start=(k == 0), stop=(k == KT - 1))
                filled(last, use)
            row_bc(2)
            pe.wait_ge(brow_loaded, 16)
            out_rows(FIRST["conf_o"], cout, 2, lambda k: pe.wait_ge(conf_out, k + 1), True)
            norm(4)
            row_bc(3)
            wait_aT(4)
            ffn("ffn1", NF, 3, True)

            norm(5)
            wait_aT(5)
            in_a = FIRST["in_a"]
            for c in range(4):
                wait_ring(in_a + c)
                for b in range(3):
                    use = USE["in_a"][3 * c + b]
                    wait_free(pe, use)
                    filled(feature_block(use, slot(in_a + c)[:, b * D:(b + 1) * D], lambda k: aT[:, k, 0:T]), use)
            for c in range(2):
                in_v = FIRST["in_v"] + c
                wait_ring(in_v)
                for t in range(TT):
                    use = USE["in_v"][2 * c + t]
                    wait_free(pe, use)
                    for k in range(KT):
                        last = mm(bank(use)[:, 0:V2C], aT[:, k, t * P:(t + 1) * P],
                                  slot(in_v)[:, k * V2C:(k + 1) * V2C], start=(k == 0), stop=(k == KT - 1))
                    filled(last, use)

            def rest():
                for name, n in (("in_b", 12), ("in_g", 24)):
                    for b in range(n):
                        c = FIRST[name] + b // 3
                        if b % 3 == 0:
                            wait_ring(c)
                        use = USE[name][b]
                        wait_free(pe, use)
                        filled(feature_block(use, slot(c)[:, (b % 3) * D:(b % 3 + 1) * D], lambda k: aT[:, k, 0:T]), use)
                        yield
            filler = rest()
            pe.wait_ge(bbar_ready, 1)
            for n in range(2):
                transposes(USE["b_bar"][n], [bbd[:, n, blk, :] for blk in range(4)])
            pe.wait_ge(logf_ready, 1)
            use = USE["cum"]
            wait_free(pe, use)
            mm(bank(use)[:, 0:8], const("le"), logf[:, 0, :], start=True, stop=True)
            mm(bank(use)[:, 8:16], ones, logf[:, 0, :], start=True, stop=False)
            filled(mm(bank(use)[:, 8:16], const("le"), logf[:, 1, :], start=False, stop=True), use)
            for n in range(4):
                pe.wait_ge(cdiag_ready, n + 1)
                use = USE["cum_k"][n]
                wait_free(pe, use)
                filled(mm(bank(use), ones, cdiag[:, n % 2, :], start=True, stop=True), use)
            for use in USE["b_bar"]:
                wait_read(pe, use)

            def s5_in(i):
                use = USE["s5_u"][i]
                wait_free(pe, use)
                r0, blk = 32 * (i % 4), i // 4
                for part in range(2):
                    last = mm(bank(use)[:, part * T:(part + 1) * T], bT[r0:r0 + 32, part, blk, :],
                              uT[r0:r0 + 32, blk, :], start=True, stop=True)
                filled(last, use)

            pe.wait_ge(late_loaded, 48)
            for use in USE["in_a"][0:4]:
                wait_read(pe, use)
            s5_in(0)
            for i in range(S5T):
                next(filler)
                if i + 1 < S5T:
                    s5_in(i + 1)
                pe.wait_ge(s5_state, i + 1)
                r0, blk = 32 * (i % 4), i // 4
                use = USE["s5_y"][blk]
                if i % 4 == 0:
                    wait_free(pe, use)
                for part in range(2):
                    last = mm(bank(use)[r0:r0 + 32, 0:T], c_bd[:, part, i, :], s_ri[:, i % 2, part, :],
                              start=(part == 0), stop=(part == 1))
                if i % 4 == 3:
                    filled(last, use)
                else:
                    last.then_inc(s5_part, 1)
                if i % 4 == 3:
                    next(filler)
                    pe.wait_ge(gelu_done, blk + 1)
                    use = USE["glu"][blk]
                    wait_free(pe, use)
                    filled(mm(bank(use)[:, 0:T], glu[:, blk, :], y_a[:, blk, :], start=True, stop=True), use)

            for use in USE["in_a"] + USE["in_v"]:
                wait_read(pe, use)
            for n in range(NATT + 4):
                if n < NATT:
                    a, t = n // 2, n % 2
                    q0 = 64 * (a % 2)
                    use = USE["fa_s"][n]
                    wait_free(pe, use)
                    filled(mm(bank(use)[:, 0:(t + 1) * P], q2T[q0:q0 + 64, a // 2, t * P:(t + 1) * P],
                              k2T[q0:q0 + 64, a // 2, 0:(t + 1) * P], start=True, stop=True), use)
                    next(filler, None)
                if 2 <= n < NATT + 2:
                    m = n - 2
                    pe.wait_ge(fa_norm, m + 1)
                    transposes(USE["fa_t"][m], [fa_p[:, m % 3, kb * P:(kb + 1) * P] for kb in range(m % 2 + 1)])
                if n >= 4 and n % 2 == 1:
                    a = (n - 4) // 2
                    wait_read(pe, USE["fa_t"][2 * a + 1])
                    use = USE["fa_o"][a // 2]
                    if a % 2 == 0:
                        wait_free(pe, use)
                    q0 = 64 * (a % 2)
                    v = lambda kb: v2[:, kb, a * AHD:(a + 1) * AHD]
                    mm(bank(use)[q0:q0 + 64, 0:T], v(0), fa_pT[:, a % 2, 0, :], start=True, stop=False)
                    last = mm(bank(use)[q0:q0 + 64, P:T], v(1), fa_pT[:, a % 2, 1, P:T], start=False, stop=True)
                    if a % 2:
                        filled(last, use)
                    else:
                        last.then_inc(fa_half, 1)
            for _ in filler:
                pass

            pe.wait_ge(ya_done, 4)
            pe.wait_ge(yb_done, 4)
            for use in USE["fa_o"]:
                wait_read(pe, use)
            ys = (y_a, y_b, y_c)
            for j in range(8):
                c = FIRST["branch"] + j // 2
                if j % 2 == 0:
                    wait_ring(c)
                at = (j % 2) * 12 * P
                for part in range(2):
                    use = USE["branch"][2 * j + part]
                    wait_free(pe, use)
                    for br in ((0, 1), (2,))[part]:
                        for k in range(4):
                            wat = at + (4 * br + k) * P
                            last = mm(bank(use)[:, (br % 2) * T:(br % 2 + 1) * T], slot(c)[:, wat:wat + P],
                                      ys[br][:, k, :], start=(k == 0), stop=(k == 3))
                    filled(last, use)
            row_bc(4)
            out_rows(FIRST["out2"], mT, 4, lambda k: pe.wait_ge(merged, k + 1))
            norm(6)
            row_bc(5)
            wait_aT(6)
            ffn("ff", NF2, 5, False)

        @block.scalar
        def _(act):
            fn = nc.scalar.activation
            ch = Chain(act, act_c)

            act.dma_start(cols[:, :], cols_in).then_inc(cols_loaded, 16)
            act.dma_start(ybuf_t[:, :].rearrange("p (t n) -> p t n", t=TT), ctx_in.rearrange("(t p) n -> p t n", p=P)).then_inc(ctx_loaded, 16)
            act.dma_start(h, x_in.rearrange("(t p) n -> p t n", p=P)).then_inc(x_loaded, 16)
            act.dma_start(consts[:, :], consts_in).then_inc(consts_loaded, 16)
            act.dma_start(rows[:, :], rows_in).then_inc(rows_loaded, 16)
            act.wait_ge(cols_loaded, 16)
            fn(cond[:, :], col("cond"), ACT.Silu).then_inc(cond_ready, 1)

            def norm_stats(i):
                src = ybuf if i == 0 else h
                for t in range(TT):
                    if i == 0:
                        act.wait_ge(ctx_loaded, 16)
                    elif i == 1:
                        act.wait_ge(x_loaded, 16)
                    else:
                        act.wait_ge(h_ready, 2 * (i - 2) + t + 1)
                    fn(nrm[:, t, :], src[:, t, :], ACT.Square,
                       accum_out=nss[:, 2 * i + t:2 * i + t + 1]).then_inc(norm_ss, 1)
                act.wait_ge(norm_ms, i + 1)
                fn(nsd[:, 2 * i:2 * i + 2], nms[:, 2 * i:2 * i + 2], ACT.Sqrt).then_inc(norm_sd, 1)

            def norm_evac(i):
                at = T if i == 0 else 0
                for kp in (1, 3):
                    use = USE[f"norm{i}"][kp]
                    wait_full(act, use)
                    for j in range(2):
                        k = 2 * kp + j
                        last = fn(aT[:, k, at:at + T], bank(use)[:, j * T:(j + 1) * T], ACT.Identity,
                                  scale=ngain[:, i, k:k + 1], bias=nshift[:, i, k:k + 1])
                    freed(last, use)

            def row_copy(p):
                for half, use in enumerate(USE["row", p]):
                    wait_full(act, use)
                    freed(fn(rowbc[:, half * 512:half * 512 + 512], bank(use), ACT.Copy), use)

            def post_stats(p):
                use = USE["y", p][0]
                wait_full(act, use)
                for t in range(TT):
                    fn(ybuf[:, t, :], Y[:, t, :], ACT.Square,
                       accum_out=pss[:, 2 * p + t:2 * p + t + 1]).then_inc(post_ss, 1)
                act.wait_ge(post_ms, p + 1)
                fn(psd[:, 2 * p:2 * p + 2], pms[:, 2 * p:2 * p + 2], ACT.Sqrt).then_inc(post_sd, 1)

            def ffn(name, n, func, stage):
                uses = USE[name]

                def one(j, i=0):
                    act.wait_ge(bank_full[uses[j][0]], uses[j][1] + 1 + i)
                    if j >= 2:
                        act.wait_ge(bank_free[uses[j - 2][0]], uses[j - 2][1] + 1 + i)
                    fn(sg[:, j % 2, :], bank(uses[j])[:, 0:T], func).then_inc(act_on, 1)

                for j in range(2):
                    one(j)
                turns = (n - 2) // SLOTS
                with act.Fori(0, turns) as i:
                    for q in range(SLOTS):
                        one(2 + q, i)
                for j in range(2 + SLOTS * turns, n):
                    one(j)

            norm_stats(0)
            norm_stats(1)
            act.wait_ge(mod_ready, 1)
            norm_evac(0)
            norm_evac(1)
            act.wait_ge(margins, 1)
            for b, use in enumerate(USE["hyb_f"]):
                wait_full(act, use)
                n = 2 if b < 8 else 1
                freed(fn(cin[:, b, 0:n, 2:T + 2], bank(use)[:, 0:n * T].rearrange("p (s t) -> p s t", s=n), ACT.Copy), use)
            uses = iter(USE["hyb_t"])
            for c in range(4):
                for t in range(TT):
                    use = next(uses)
                    wait_full(act, use)
                    at = c * HYB_TC
                    cut = min(max(512 - at, 0), HYB_TC)
                    if cut:
                        last = fn(zgate[:, t, at:at + cut], bank(use)[:, 0:cut], ACT.Copy)
                    if cut < HYB_TC:
                        last = fn(ptok[:, t, at + cut - 512:at - 512 + HYB_TC], bank(use)[:, cut:HYB_TC], ACT.Copy)
                    freed(last, use)
            for t in range(TT):
                use = next(uses)
                wait_full(act, use)
                freed(fn(pctx[:, t, :], bank(use)[:, HYB_TC - CTX_T:HYB_TC], ACT.Copy), use)
            for b in range(12):
                act.wait_ge(conv_done, b // 4 + 1)
                n = 2 if b < 8 else 1
                fn(cv[:, b, 0:n, :], cv[:, b, 0:n, :], ACT.Silu).then_inc(silu_done, 1)
            act.wait_ge(bank_free[USE["hyb_t"][5][0]], USE["hyb_t"][5][1] + 1)
            for t in range(TT):
                fn(zgate[:, t, :], zgate[:, t, :], ACT.Silu).then_inc(zgate_ready, 1)
            act.wait_ge(att_ms, 1)
            fn(att_ss, att_ss, ACT.Sqrt).then_inc(att_sd, 1)
            for n, use in enumerate(USE["att_qk"]):
                wait_full(act, use)
                if n < 2:
                    freed(fn(qbT[:, :, n * P:(n + 1) * P], bank(use).rearrange("p (a b) -> p a b", a=4), ACT.Copy), use)
                else:
                    freed(fn(kbT, bank(use), ACT.Copy), use)
            for n in range(NATT + 5):
                if n < NATT:
                    act.wait_ge(att_mx, n + 1)
                    if n >= 3:
                        wait_full(act, USE["att_t"][n - 3])
                    use = USE["att_s"][n]
                    wait_full(act, use)
                    freed(fn(att_p[:, n % 3, :], bank(use), ACT.Exp, scale=AHD ** -0.5,
                             bias=att_max[:, n:n + 1], accum_out=att_sum[:, n:n + 1]), use)
                if 2 <= n < NATT + 2:
                    m = n - 2
                    a, t = m // 2, m % 2
                    use = USE["att_t"][m]
                    wait_full(act, use)
                    if a >= 2:
                        if a % 2 == 0:
                            act.wait_ge(att_half, a // 2)
                        else:
                            wait_full(act, USE["att_o"][(a - 2) // 2])
                    freed(fn(att_pT[:, a % 2, :, t * P:(t + 1) * P],
                             bank(use).rearrange("p (a b) -> p a b", a=4), ACT.Copy), use)
                if n >= 8 and (n - 8) % 4 == 0:
                    m = (n - 8) // 4
                    use = USE["att_o"][m]
                    wait_full(act, use)
                    freed(fn(yT[:, 4 + m, :], bank(use)[:, 0:T], ACT.Copy), use)
            for n in range(6):
                use = USE["to_tok"][n]
                wait_full(act, use)
                fn(sq_kq[:, n, :], bank(use), ACT.Square).then_inc(kq_sq, 1)
            act.wait_ge(kq_ms, 1)
            fn(kq_ss, kq_ss, ACT.Sqrt).then_inc(kq_sd, 1)
            for n in range(4):
                use = USE["to_tok"][6 + n]
                wait_full(act, use)
                freed(fn(vtok[:, n, :], bank(use), ACT.Copy), use)
            act.wait_ge(ba_ready, 4)
            act.wait_ge(rows_loaded, 16)
            fn(beta, ba[:, :, 0:8], ACT.Sigmoid).then_inc(sp_ready, 1)
            act.wait_ge(sp_in, 1)
            ch(fn(g_a, g_a, ACT.Exp, scale=-1.0))
            ch.mark(fn(na8, row("a_log"), ACT.Exp))
            ch.sync()
            fn(g_a, g_a, ACT.Ln, bias=1.0).then_inc(sp_ready, 1)
            for n, use in enumerate(USE["to_feat"]):
                wait_full(act, use)
                dst = kT[:, n // 2, :, (n % 2) * P:(n % 2 + 1) * P] if n < 4 else qT[:, :, (n - 4) * P:(n - 3) * P]
                freed(fn(dst, bank(use).rearrange("p (a b) -> p a b", a=NH), ACT.Copy), use)
            use = USE["gates"]
            wait_full(act, use)
            act.wait_ge(dsum, 1)
            for n, (dst, d) in enumerate(((eg, 0), (eg, 1), (etail, 0), (etail, 1))):
                fn(dst[:, :, 4 * d:4 * d + 4], bank(use)[:, 16 * n:16 * n + 16].rearrange("p (s e) -> p s e", s=4), ACT.Exp)
            freed(fn(etot, bank(use)[:, 64:96].rearrange("p (s e) -> p s e", s=4), ACT.Exp), use)
            for n in range(8):
                act.wait_ge(dmask, n + 1)
                fn(UT[:, n, :], UT[:, n, :], ACT.Exp).then_inc(dec_ready, 1)
            for n, use in enumerate(USE["x1"]):
                wait_full(act, use)
                freed(fn(X[:, n, :], bank(use), ACT.Copy), use)
            for level in range(1, LEVELS):
                for n, use in enumerate(USE["p", level]):
                    wait_full(act, use)
                    freed(fn(BP[:, n, :], bank(use), ACT.Copy), use)
                if level < LEVELS - 1:
                    for n, use in enumerate(USE["t", level]):
                        wait_full(act, use)
                        freed(fn(XT[:, n, :], bank(use), ACT.Copy), use)
            act.wait_ge(ro_ms, 1)
            fn(ro_ss, ro_ss, ACT.Sqrt).then_inc(ro_sd, 1)
            for t, use in enumerate(USE["y_t"]):
                wait_full(act, use)
                freed(fn(yT[:, 0:4, t * P:(t + 1) * P], bank(use).rearrange("p (a b) -> p a b", a=NH), ACT.Copy), use)
            row_copy(0)
            post_stats(0)
            norm_stats(2)
            norm_evac(2)
            row_copy(1)
            act.dma_start(tok_t[:, 1024:2048], c_bd_in).then_inc(late_loaded, 16)
            act.dma_start(arena[:, 15400:15912], glu_in).then_inc(late_loaded, 16)
            act.dma_start(arena[:, 12328:12840], b_in).then_inc(late_loaded, 16)
            act.dma_start(brow[0:1, :], b_out_in).then_inc(brow_loaded, 16)
            ffn("ffn0", NF, ACT.Silu, 0)
            post_stats(1)
            norm_stats(3)
            norm_evac(3)
            for c in range(8):
                use = USE["conf_i"][c]
                wait_full(act, use)
                if c >= 2:
                    wait_read(act, USE["conf_i"][c - 2])
                fn(csig[:, c % 2, :], bank(use)[:, T:2 * T], ACT.Sigmoid,
                   bias=col("conf_b_in")[:, 8 + c:9 + c]).then_inc(csig_ready, 1)
            for k in range(KT):
                act.wait_ge(ln_x, k + 1)
                fn(csq[:, k, :], cc[:, k, :], ACT.Square).then_inc(csq_done, 1)
            wait_read(act, USE["ln"][1])
            fn(crs, crs, ACT.Sqrt).then_inc(ln_sd, 1)
            for k in range(KT):
                act.wait_ge(csq_ready, k + 1)
                fn(cout[:, k, :], csq[:, k, :], ACT.Silu, scale=col("conf_ln_g")[:, k:k + 1],
                   bias=col("conf_ln_b")[:, k:k + 1]).then_inc(conf_out, 1)
            fn(dt, col("log_dt"), ACT.Exp).then_inc(s5_mag, 1)
            act.wait_ge(s5_par, 1)
            fn(mag, s5_a, ACT.Exp).then_inc(s5_mag, 1)
            act.wait_ge(half_ready, 1)
            act.wait_ge(s5_arg, 1)
            fn(sin_h, phi, ACT.Sin, scale=PI).then_inc(s5_trig, 1)
            fn(cos_h, s5_b, ACT.Sin, scale=-PI, bias=halfpi[:, :]).then_inc(s5_trig, 1)
            act.wait_ge(s5_arg, 2)
            fn(trig_tmp[:, 2, :], trig_tmp[:, 0, :], ACT.Sin, scale=PI).then_inc(s5_trig, 1)
            fn(trig_tmp[:, 3, :], trig_tmp[:, 1, :], ACT.Sin, scale=-PI, bias=halfpi[:, :]).then_inc(s5_trig, 1)
            row_copy(2)
            post_stats(2)
            norm_stats(4)
            norm_evac(4)
            row_copy(3)
            ffn("ffn1", NF, ACT.Silu, 2)
            post_stats(3)
            norm_stats(5)
            norm_evac(5)
            for b, use in enumerate(USE["in_a"]):
                wait_full(act, use)
                dst = (uT, q2T, k2T)[b // 4][:, b % 4, :]
                freed(fn(dst, bank(use)[:, 0:T], ACT.Copy), use)
            for n, use in enumerate(USE["in_v"]):
                wait_full(act, use)
                c, t = n // 2, n % 2
                freed(fn(v2[:, t, c * V2C:(c + 1) * V2C], bank(use)[:, 0:V2C], ACT.Copy), use)
            act.wait_ge(logf_in, 1)
            ch(fn(lf_a, lf_a, ACT.Exp, scale=-1.0))
            fn(lf_a, lf_a, ACT.Ln, bias=1.0).then_inc(logf_sp, 1)

            def rest():
                for b, use in enumerate(USE["in_b"]):
                    wait_full(act, use)
                    freed(fn(cin2[:, b, 2:T + 2], bank(use)[:, 0:T], ACT.Copy), use)
                    yield
                for b, use in enumerate(USE["in_g"]):
                    wait_full(act, use)
                    freed(fn(gT[:, b, :], bank(use)[:, 0:T], ACT.Identity, bias=col("b_gate_2")[:, b:b + 1]), use)
                    yield
            filler = rest()
            for n, use in enumerate(USE["b_bar"]):
                wait_full(act, use)
                freed(fn(bT[:, n, :, :].rearrange("p a b -> p (a b)"), bank(use), ACT.Copy), use)
            for i in range(S5T):
                next(filler)
                if i % 4 == 3:
                    next(filler)
                    blk = i // 4
                    wait_read(act, USE["s5_y"][blk])
                    fn(y_a[:, blk, :], y_a[:, blk, :], ACT.Gelu_apprx_tanh).then_inc(gelu_done, 1)
                    use = USE["glu"][blk]
                    wait_full(act, use)
                    freed(fn(glu_sig[:, blk % 2, :], bank(use)[:, 0:T], ACT.Sigmoid), use)
            for n in range(NATT + 5):
                if n < NATT:
                    next(filler, None)
                    t = n % 2
                    act.wait_ge(fa_mx, n + 1)
                    if n >= 3:
                        wait_full(act, USE["fa_t"][n - 3])
                    width = (t + 1) * P
                    fn(fa_p[:, n % 3, 0:width], fa_p[:, n % 3, 0:width], ACT.Exp, bias=fa_max[:, n:n + 1],
                       accum_out=fa_sum[:, n:n + 1]).then_inc(fa_exp, 1)
                if 2 <= n < NATT + 2:
                    m = n - 2
                    a, t = m // 2, m % 2
                    use = USE["fa_t"][m]
                    wait_full(act, use)
                    if a >= 2:
                        if a % 2 == 0:
                            act.wait_ge(fa_half, a // 2)
                        else:
                            wait_full(act, USE["fa_o"][(a - 2) // 2])
                    freed(fn(fa_pT[:, a % 2, 0:t + 1, t * P:(t + 1) * P],
                             bank(use)[:, 0:(t + 1) * P].rearrange("p (a b) -> p a b", a=t + 1), ACT.Copy), use)
                if n >= 8 and (n - 8) % 4 == 0:
                    m = (n - 8) // 4
                    use = USE["fa_o"][m]
                    wait_full(act, use)
                    freed(fn(y_c[:, m, :], bank(use)[:, 0:T], ACT.Copy), use)
            for _ in filler:
                pass
            wait_read(act, USE["in_g"][23])
            for n in range(8):
                fn(gT[:, 3 * n:3 * n + 3, :], gT[:, 3 * n:3 * n + 3, :], ACT.Sigmoid).then_inc(gates_ready, 1)
            row_copy(4)
            post_stats(4)
            norm_stats(6)
            norm_evac(6)
            row_copy(5)
            ffn("ff", NF2, ACT.Relu, 4)
            post_stats(5)

        @block.vector
        def _(dve):
            v = nc.vector
            tt, ts, stt = v.tensor_tensor, v.tensor_scalar, v.scalar_tensor_tensor
            ch = Chain(dve, dve_c)

            def mod(layer):
                dve.wait_ge(mod_mm, SUMS[layer, NMOD - 1] + 1)
                if layer == 0:
                    dve.wait_ge(ring_used, len(MOD0_PE))
                src = psum[:, 3584 - 512 * layer:3584 - 512 * layer + 96].rearrange("p (n c) -> p n c", c=2)
                b = col("b_mod")[:, 48 * layer:48 * layer + 48]
                m = modT[:, layer, :, :]
                for c in range(2 if layer == 0 else 1):
                    n = 16 if c else 48
                    ch.mark(tt(m[:, 0:n, c], src[:, 0:n, c], b[:, 0:n], ALU.add))
                ch.sync()
                gain = lambda name: col(name)[:, KT * layer:KT * layer + KT]
                todo = [(1 + 2 * layer, 0, "g_mix_pre", 0), (2 + 2 * layer, 24, "g_ffn_pre", 0)]
                if layer == 0:
                    todo.append((0, 0, "g_mix_pre", 1))
                for i, at, name, c in todo:
                    ch.mark(stt(ngain[:, i, :], m[:, at + 8:at + 16, c], 1.0, gain(name), ALU.add, ALU.mult))
                    ch.mark(v.tensor_copy(nshift[:, i, :], m[:, at:at + 8, c]))
                ch.mark(tt(pcol[:, 2 * layer, :], m[:, 16:24, 0], gain("g_mix_post"), ALU.mult))
                ch.mark(tt(pcol[:, 2 * layer + 1, :], m[:, 40:48, 0], gain("g_ffn_post"), ALU.mult))
                if layer == 0:
                    for i, name in ((5, "g_pre_mix_2"), (6, "g_pre_mlp_2")):
                        ch.mark(v.tensor_copy(ngain[:, i, :], col(name)))
                        ch.mark(v.memset(nshift[:, i, :], 0.0))
                    for p, name in ((4, "g_post_mix_2"), (5, "g_post_mlp_2")):
                        ch.mark(v.tensor_copy(pcol[:, p, :], col(name)))
                ch.sync()
                v.memset(vtick[:, :], 0.0).then_inc(mod_ready, 1)

            def mod_sums(layer, j):
                c, n = CHUNK[f"mod{layer}", j], SUMS[layer, j]
                dve.wait_ge(ring_ready[c % SLOTS], 16 * (c // SLOTS + 1))
                if n >= 4:
                    dve.wait_ge(mod_mm, n - 3)
                todo = [(macs[:, n % 4, :], 0, MOD_C)]
                if layer == 0 and j < MOD_CTX:
                    todo.insert(0, (macs_ctx[:, n % 2, :], 1, MOD_C))
                    if n >= 2:
                        dve.wait_ge(mod_mm, n - 1)
                for k in range(KT):
                    for n, (dst, which, width) in enumerate(todo):
                        part = slot(c)[:, k * MOD_C:(k + 1) * MOD_C]
                        value = cond[:, 2 * k + which:2 * k + which + 1]
                        if k == 0:
                            ins = ts(dst, part, value, None, ALU.mult)
                        else:
                            ins = stt(dst, part, value, dst, ALU.mult, ALU.add)
                        if (k, n) == (KT - 1, len(todo) - 1):
                            ins.then_inc(sums_ready, 1)
                        else:
                            ins.then_inc(mac, 1)
                            mac_n[0] += 1
                    if k < KT - 1:
                        dve.wait_ge(mac, mac_n[0])

            mac_n = [0]

            def mean_eps(out, src, n):
                return ts(out, src, 1.0 / n, EPS, ALU.mult, ALU.add)

            def norm_scale(i):
                dve.wait_ge(norm_ss, 2 * (i + 1))
                mean_eps(nms[:, 2 * i:2 * i + 2], nss[:, 2 * i:2 * i + 2], D).then_inc(norm_ms, 1)
                dve.wait_ge(norm_sd, i + 1)
                ch(v.reciprocal(nrs[:, 2 * i:2 * i + 2], nsd[:, 2 * i:2 * i + 2]))
                src, dst = (ybuf, ybuf) if i == 0 else (h, nrm)
                if i == 1:
                    dve.wait_ge(x_loaded, 16)
                for t in range(TT):
                    ts(dst[:, t, :], src[:, t, :], nrs[:, 2 * i + t:2 * i + t + 1], None, ALU.mult).then_inc(norm_x, 1)

            def norm_evac(i):
                at = T if i == 0 else 0
                for kp in (0, 2):
                    use = USE[f"norm{i}"][kp]
                    wait_full(dve, use)
                    for j in range(2):
                        k = 2 * kp + j
                        last = ts(aT[:, k, at:at + T], bank(use)[:, j * T:(j + 1) * T],
                                  ngain[:, i, k:k + 1], nshift[:, i, k:k + 1], ALU.mult, ALU.add)
                    freed(last, use)

            def row_diag(p):
                if p:
                    wait_full(dve, USE["row", p - 1][1])
                tt(view(diag, 0, KT, P), bc_out(ident, KT), bc_in(pcol[:, p, :], P), ALU.mult).then_inc(diag_ready, 1)

            def post(p):
                dve.wait_ge(post_ss, 2 * (p + 1))
                mean_eps(pms[:, 2 * p:2 * p + 2], pss[:, 2 * p:2 * p + 2], D).then_inc(post_ms, 1)
                dve.wait_ge(post_sd, p + 1)
                ch(v.reciprocal(prs[:, 2 * p:2 * p + 2], psd[:, 2 * p:2 * p + 2]))
                for use in USE["row", p]:
                    wait_read(dve, use)
                use = USE["y", p][0]
                for t in range(TT):
                    last = stt(ybuf[:, t, :], Y[:, t, :], prs[:, 2 * p + t:2 * p + t + 1], rowbc[:, :], ALU.mult, ALU.mult)
                    if t == 0:
                        ch(last)
                    else:
                        freed(last, use)
                        wait_read(dve, use)
                    tt(h[:, t, :], h[:, t, :], ybuf[:, t, :], ALU.add).then_inc(h_ready, 1)

            def ffn(name, n, base, second):
                uses, used = USE[name], used_before(name)

                def one(j, i=0):
                    dve.wait_ge(act_on, base + j + 1 + SLOTS * i)
                    if j >= 2:
                        dve.wait_ge(ring_used, used + j - 1 + SLOTS * i)
                    freed(tt(hT[:, j % 2, :], sg[:, j % 2, :], bank(uses[j])[:, second:second + T], ALU.mult), uses[j])

                for j in range(2):
                    one(j)
                turns = (n - 2) // SLOTS
                with dve.Fori(0, turns) as i:
                    for q in range(SLOTS):
                        one(2 + q, i)
                for j in range(2 + SLOTS * turns, n):
                    one(j)

            v.memset(zeros[:, :], 0.0).then_inc(zeros_ready, 1)
            dve.wait_ge(cols_loaded, 16)
            dve.wait_ge(cond_ready, 1)
            for j in range(NMOD):
                if (0, j) in SUMS:
                    mod_sums(0, j)
            mod(0)
            dve.wait_ge(ctx_loaded, 16)
            norm_scale(0)
            norm_scale(1)
            dve.wait_ge(consts_loaded, 16)
            norm_evac(0)
            norm_evac(1)
            for j in range(8):
                mod_sums(1, j)
            taps = col("hyb_conv").rearrange("p (b k) -> p b k", k=CONV_A)
            for grp in range(3):
                n = 2 if grp < 2 else 1
                for b in range(4 * grp, 4 * grp + 4):
                    wait_read(dve, USE["hyb_f"][b])
                    ch.mark(ts(cv[:, b, 0:n, :], cin[:, b, 0:n, 0:T], taps[:, b, 0:1], None, ALU.mult))
                for k in range(1, CONV_A):
                    ch.sync()
                    for b in range(4 * grp, 4 * grp + 4):
                        last = stt(cv[:, b, 0:n, :], cin[:, b, 0:n, k:k + T], taps[:, b, k:k + 1], cv[:, b, 0:n, :], ALU.mult, ALU.add)
                        if k < CONV_A - 1:
                            ch.mark(last)
                last.then_inc(conv_done, 1)
                for j in range(8 + 2 * grp, 10 + 2 * grp):
                    mod_sums(1, j)
            for j in range(14, NMOD):
                mod_sums(1, j)
            dve.wait_ge(att_sq_ready, 4)
            ch.mark(v.reduce_sum(att_ss[:, 0:20], att_sq[:, 0:1280].rearrange("p (a b) -> p a b", b=AHD), axis=AXX))
            ch.mark(v.reduce_sum(att_ss[:, 20:24], att_sq[:, 1280:1536].rearrange("p (a b) -> p a b", b=AHD), axis=AXX))
            ch.sync()
            mean_eps(att_ss, att_ss, AHD).then_inc(att_ms, 1)
            dve.wait_ge(att_sd, 1)
            v.reciprocal(att_r, att_ss).then_inc(att_rs, 1)
            mod(1)

            def att_scale(n):
                wait_read(dve, USE["att_s"][n])
                ch(v.reciprocal(att_inv[:, n:n + 1], att_sum[:, n:n + 1]))
                ts(att_p[:, n % 3, :], att_p[:, n % 3, :], att_inv[:, n:n + 1], None, ALU.mult).then_inc(att_norm, 1)

            for n in range(NATT):
                use = USE["att_s"][n]
                wait_full(dve, use)
                ch(v.reduce_max(att_max[:, n:n + 1], bank(use), axis=AXX))
                ts(att_max[:, n:n + 1], att_max[:, n:n + 1], -(AHD ** -0.5), None, ALU.mult).then_inc(att_mx, 1)
                if n:
                    att_scale(n - 1)
            att_scale(NATT - 1)
            for n in range(6):
                dve.wait_ge(kq_sq, n + 1)
                ch.mark(v.reduce_sum(kq_ss[:, 4 * n:4 * n + 4], sq_kq[:, n, :].rearrange("p (a b) -> p a b", a=NH), axis=AXX))
            ch.sync()
            ts(kq_ss, kq_ss, EPS, None, ALU.add).then_inc(kq_ms, 1)
            dve.wait_ge(kq_sd, 1)
            ch(v.reciprocal(kq_r, kq_ss))
            ch(ts(kq_r[:, 16:24], kq_r[:, 16:24], HD ** -0.5, None, ALU.mult))
            for n in range(6):
                use = USE["to_tok"][n]
                dst = ktok[:, n, :] if n < 4 else qtok[:, n - 4, :]
                freed(tt(dst.rearrange("p (a b) -> p a b", a=NH), bank(use).rearrange("p (a b) -> p a b", a=NH),
                         bc_in(kq_r[:, 4 * n:4 * n + 4], P), ALU.mult), use)
            dve.wait_ge(ba_ready, 4)
            dve.wait_ge(rows_loaded, 16)
            z, za = (x.rearrange("p (s e) -> p s e", s=4) for x in (g_b, g_a))
            ch(tt(z, ba[:, :, 8:16], bc_out(row("dt_bias"), 4), ALU.add))
            stt(za, z, -1.0, z, ALU.mult, ALU.max).then_inc(sp_in, 1)
            dve.wait_ge(sp_ready, 2)
            ch(stt(g_b, g_b, 0.0, g_a, ALU.max, ALU.add))
            ch(tt(g, z, bc_out(na8, 4), ALU.mult))
            ts(g_t, g_t, -1.0, None, ALU.mult).then_inc(g_ready, 1)
            use = USE["gates"]
            wait_full(dve, use)
            for d in range(2):
                last = ts(ngc[:, :, 4 * d:4 * d + 4], bank(use)[:, 16 * d:16 * d + 16].rearrange("p (s e) -> p s e", s=4),
                          -1.0, None, ALU.mult)
            last.then_inc(dsum, 1)
            dve.wait_ge(dsum, 1)
            quad = lambda x: x.rearrange("p (a b) -> p a b", a=NH)
            for n, use in enumerate(USE["decay"]):
                d, st = n // 4, n % 4
                wait_full(dve, use)
                freed(tt(quad(UT[:, n, :]), quad(bank(use)), bc_in(ngc[:, st, 4 * d:4 * d + 4], P), ALU.add), use)
            for t, use in enumerate(USE["kq"]):
                wait_full(dve, use)
                for d in range(2):
                    dve.wait_ge(dec_ready, 4 * d + t + 1)
                    last = tt(intraT[:, 2 * d + t, :], bank(use), UT[:, 4 * d + t, :], ALU.mult)
                freed(last, use)
            for st, use in enumerate(USE["kk"]):
                wait_full(dve, use)
                dve.wait_ge(dec_ready, 8)
                tt(UT[:, st, :], bank(use), UT[:, st, :], ALU.mult).then_inc(ut_part, 1)
                freed(tt(UT[:, 4 + st, :], bank(use), UT[:, 4 + st, :], ALU.mult), use)
            for n in range(8):
                d, st = n // 4, n % 4
                dve.wait_ge(ut_ready, 2 * st + d + 1)
                ch(tt(quad(XT[:, n, :]), quad(UT[:, n, :]), bc_out(levels[:, d, 0, :], NH), ALU.mult))
                tt(quad(XT[:, n, :]), bc_out(ident, NH), quad(XT[:, n, :]), ALU.subtract).then_inc(xt_first, 1)
            for level in range(1, LEVELS):
                dst = X if level < LEVELS - 1 else XT
                for n, use in enumerate(USE["q", level]):
                    wait_full(dve, use)
                    freed(tt(dst[:, n, :], dst[:, n, :], bank(use), ALU.subtract), use)
            row_diag(0)
            wait_read(dve, USE["gates"])
            for s in range(4):
                for d in range(2):
                    st = ORDER[d][s]
                    if s == 0:
                        v.tensor_copy(r_st[:, d, :], vtok[:, st, :]).then_inc(resid_ready, 1)
                        continue
                    use = USE["ks", s, d]
                    wait_full(dve, use)
                    freed(tt(quad(tmp_st[:, d, :]), quad(bank(use)), bc_in(eg[:, st, 4 * d:4 * d + 4], P), ALU.mult), use)
                    wait_read(dve, use)
                    tt(r_st[:, d, :], vtok[:, st, :], tmp_st[:, d, :], ALU.subtract).then_inc(resid_ready, 1)
                for d in range(2):
                    st = ORDER[d][s]
                    use = USE["vn", s, d]
                    wait_full(dve, use)
                    freed(tt(quad(vn_st[:, d, :]), quad(bank(use)), bc_in(beta[:, st, 4 * d:4 * d + 4], P), ALU.mult), use)
                    if 0 < s < 3:
                        ch.mark(tt(quad(S[:, d, :]), quad(S[:, d, :]), bc_in(etot[:, st, 4 * d:4 * d + 4], P), ALU.mult))
                for d in range(2):
                    if s < 3:
                        use = USE["ds", s, d]
                        wait_full(dve, use)
                        if s == 0:
                            freed(v.tensor_copy(S[:, d, :], bank(use)), use)
                        else:
                            ch.sync()
                            freed(tt(S[:, d, :], S[:, d, :], bank(use), ALU.add), use)
                for d in range(2):
                    st = ORDER[d][s]
                    if s >= 2:
                        use = USE["os", s, d]
                        wait_full(dve, use)
                        dst = o_sum[:, st, :] if s == 2 else tmp_st[:, d, :]
                        freed(tt(quad(dst), quad(bank(use)), bc_in(eg[:, st, 4 * d:4 * d + 4], P), ALU.mult), use)
                        wait_read(dve, use)
                        if s == 3:
                            ch(tt(o_sum[:, st, :], o_sum[:, st, :], tmp_st[:, d, :], ALU.add))
                        use = USE["oi", s, d]
                        wait_full(dve, use)
                        freed(tt(o_sum[:, st, :], o_sum[:, st, :], bank(use), ALU.add), use)
                        wait_read(dve, use)
            ch(tt(r_st, o_sum, o_sum, ALU.mult))
            ch(v.reduce_sum(ro_ss, r_st.rearrange("p t (a b) -> p (t a) b", a=NH), axis=AXX))
            mean_eps(ro_ss, ro_ss, HD).then_inc(ro_ms, 1)
            dve.wait_ge(ro_sd, 1)
            ch(v.reciprocal(ro_r, ro_ss))
            dve.wait_ge(zgate_ready, 2)
            for t in range(TT):
                ch(tt(quad(ymix[:, t, :]), quad(o_sum[:, t, :]), bc_in(ro_r[:, 4 * t:4 * t + 4], P), ALU.mult))
                ch(tt(quad(ymix[:, t, :]), quad(ymix[:, t, :]), bc_out(row("out_norm"), NH), ALU.mult))
                tt(ymix[:, t, :], ymix[:, t, :], zgate[:, t, :], ALU.mult).then_inc(y_mixed, 1)
            post(0)
            norm_scale(2)
            row_diag(1)
            norm_evac(2)
            ffn("ffn0", NF, 0, T)
            post(1)
            norm_scale(3)
            norm_evac(3)
            row_diag(2)
            dve.wait_ge(margins, 2)
            dww = col("conf_dw_w").rearrange("p (b k) -> p b k", k=CONF_K)
            for grp in range(4):
                pair = (2 * grp, 2 * grp + 1)
                for c in pair:
                    use = USE["conf_i"][c]
                    dve.wait_ge(csig_ready, c + 1)
                    freed(stt(cu[:, c, 15:15 + T], bank(use)[:, 0:T], col("conf_b_in")[:, c:c + 1], csig[:, c % 2, :],
                              ALU.add, ALU.mult), use)
                for c in pair:
                    wait_read(dve, USE["conf_i"][c])
                    ch.mark(ts(cc[:, c, :], cu[:, c, 0:T], dww[:, c, 0:1], col("conf_dw_b")[:, c:c + 1], ALU.mult, ALU.add))
                for k in range(1, CONF_K):
                    ch.sync()
                    for c in pair:
                        last = stt(cc[:, c, :], cu[:, c, k:k + T], dww[:, c, k:k + 1], cc[:, c, :], ALU.mult, ALU.add)
                        if k < CONF_K - 1:
                            ch.mark(last)
                        else:
                            last.then_inc(conv31, 1)
            use = USE["ln"][0]
            wait_full(dve, use)
            freed(ts(crs, bank(use)[:, 0:T], 1.0 / D, None, ALU.mult), use)
            wait_read(dve, use)
            for k in range(KT):
                tt(cc[:, k, :], cc[:, k, :], crs, ALU.subtract).then_inc(ln_x, 1)
            use = USE["ln"][1]
            wait_full(dve, use)
            freed(mean_eps(crs, bank(use)[:, 0:T], D), use)
            dve.wait_ge(ln_sd, 1)
            ch(v.reciprocal(crs, crs))
            for k in range(KT):
                tt(csq[:, k, :], cc[:, k, :], crs, ALU.mult).then_inc(csq_ready, 1)
            dve.wait_ge(s5_mag, 1)
            ch(ts(lam_re, col("a_re"), -1e-4, None, ALU.min))
            ch.mark(tt(theta, col("a_im"), dt, ALU.mult))
            tt(s5_a, lam_re, dt, ALU.mult).then_inc(s5_par, 1)
            ch.sync()
            ch(ts(rk, theta, 1 / TWO_PI, ROUND, ALU.mult, ALU.add))
            ch(ts(rk, rk, -ROUND, None, ALU.add))
            for part in TWO_PI_PARTS:
                ch(stt(theta, rk, -part, theta, ALU.mult, ALU.add))
            ch(ts(phi, theta, 1 / TWO_PI, None, ALU.mult))
            ch(ts(phi_hi, phi, ROUND / 4096, None, ALU.add))
            ch(ts(phi_hi, phi_hi, -ROUND / 4096, None, ALU.add))
            ch.mark(tt(phi_lo, phi, phi_hi, ALU.subtract))
            stt(s5_b, phi, -1.0, phi, ALU.mult, ALU.max).then_inc(s5_arg, 1)
            ch.sync()
            grid = lambda x: x.rearrange("p (i t) -> p i t", i=S5T)
            tv = bc_out(const("tvec"), S5T)
            f0, f1, f4, f5 = trig_tmp[:, 0, :], trig_tmp[:, 1, :], trig_tmp[:, 4, :], trig_tmp[:, 5, :]
            dve.wait_ge(late_loaded, 48)
            ch.mark(tt(grid(f0), tv, bc_in(phi_hi, 32), ALU.mult))
            ch.mark(tt(grid(f4), tv, bc_in(phi_lo, 32), ALU.mult))
            ch.sync()
            ch(ts(f5, f0, ROUND, None, ALU.add))
            ch(ts(f5, f5, -ROUND, None, ALU.add))
            ch(tt(f0, f0, f5, ALU.subtract))
            ch(tt(f0, f0, f4, ALU.add))
            stt(f1, f0, -1.0, f0, ALU.mult, ALU.max).then_inc(s5_arg, 1)
            dve.wait_ge(s5_trig, 2)
            dve.wait_ge(s5_mag, 2)
            ch.mark(stt(sin_t1, sin_h, 2.0, cos_h, ALU.mult, ALU.mult))
            ch.mark(stt(cos_t1, sin_h, -2.0, sin_h, ALU.mult, ALU.mult))
            ch.mark(tt(den, lam_re, lam_re, ALU.mult))
            ch.mark(tt(s5_c, col("a_im"), col("a_im"), ALU.mult))
            ch.sync()
            ch.mark(ts(cos_t1, cos_t1, 1.0, None, ALU.add))
            ch.mark(tt(den, den, s5_c, ALU.add))
            ch.mark(tt(num_im, mag, sin_t1, ALU.mult))
            ch.sync()
            ch.mark(tt(num_re, mag, cos_t1, ALU.mult))
            ch.mark(v.reciprocal(den, den))
            ch.sync()
            ch(ts(num_re, num_re, -1.0, None, ALU.add))
            ch.mark(tt(co_re, num_re, lam_re, ALU.mult))
            ch.mark(tt(s5_c, num_im, col("a_im"), ALU.mult))
            ch.mark(tt(co_im, num_im, lam_re, ALU.mult))
            ch.mark(tt(s5_b, num_re, col("a_im"), ALU.mult))
            ch.sync()
            ch.mark(tt(co_re, co_re, s5_c, ALU.add))
            ch.mark(tt(co_im, co_im, s5_b, ALU.subtract))
            ch.sync()
            ch.mark(tt(co_re, co_re, den, ALU.mult))
            ch.mark(tt(co_im, co_im, den, ALU.mult))
            ch.sync()
            hg = lambda x: x.rearrange("p (i e) -> p i e", i=S5T)
            br, bi = bc_arr[:, 0, :], bc_arr[:, 1, :]
            w0, w1, w2, w3 = f4[:, 0:256], f4[:, 256:512], f5[:, 0:256], f5[:, 256:512]
            ch.mark(tt(hg(w0), hg(br), bc_in(co_re, 16), ALU.mult))
            ch.mark(tt(hg(w1), hg(bi), bc_in(co_im, 16), ALU.mult))
            ch.mark(tt(hg(w2), hg(bi), bc_in(co_re, 16), ALU.mult))
            ch.mark(tt(hg(w3), hg(br), bc_in(co_im, 16), ALU.mult))
            ch.sync()
            dve.wait_ge(margins, 2)
            for g2 in range(2):
                r = slice(64 * g2, 64 * g2 + 64)
                for part, (x, y, op) in enumerate(((w0, w1, ALU.subtract), (w2, w3, ALU.add))):
                    dst = bbd[r, part, :, :].rearrange("p a (q g e) -> p (a q) g e", q=4, g=2)[:, :, g2, :]
                    ch.mark(tt(dst, hg(x)[r], hg(y)[r], op))
            dve.wait_ge(s5_trig, 4)
            f2, f3 = trig_tmp[:, 2, :], trig_tmp[:, 3, :]
            ch.mark(stt(small_trig[:, 1, :, :].rearrange("p i t -> p (i t)"), f2, 2.0, f3, ALU.mult, ALU.mult))
            ch(stt(small_trig[:, 0, :, :].rearrange("p i t -> p (i t)"), f2, -2.0, f2, ALU.mult, ALU.mult))
            ch(ts(small_trig[:, 0, :, :], small_trig[:, 0, :, :], 1.0, None, ALU.add))
            v.memset(vtick[:, :], 0.0).then_inc(bbar_ready, 1)
            post(2)
            norm_scale(4)
            norm_evac(4)
            row_diag(3)
            ffn("ffn1", NF, NF, T)
            post(3)
            norm_scale(5)
            norm_evac(5)
            for use in USE["in_v"][2:4]:
                wait_read(dve, use)
            ch(tt(lf_z, v2[:, :, 512:520], bc_out(row("b_f"), TT), ALU.add))
            stt(lf_a, lf_z, -1.0, lf_z, ALU.mult, ALU.max).then_inc(logf_in, 1)
            dve.wait_ge(logf_sp, 1)
            stt(logf, lf_z, 0.0, lf_a, ALU.min, ALU.subtract).then_inc(logf_ready, 1)
            use = USE["cum"]
            wait_full(dve, use)
            freed(v.tensor_copy(cumq, bank(use)[:, 0:16].rearrange("p (t e) -> p t e", t=TT)), use)
            wait_read(dve, use)
            for n in range(4):
                if n >= 2:
                    wait_full(dve, USE["cum_k"][n - 2])
                kt, h0 = n // 2, 4 * (n % 2)
                tt(quad(cdiag[:, n % 2, :]), bc_out(ident, 4), bc_in(cumq[:, kt, h0:h0 + 4], P), ALU.mult).then_inc(cdiag_ready, 1)
                use = USE["cum_k"][n]
                wait_full(dve, use)
                b3 = quad(bank(use))
                if kt == 0:
                    ch.mark(tt(ck0[:, h0:h0 + 4, :], b3, bc_in(cumq[:, 0, h0:h0 + 4], P), ALU.subtract))
                freed(tt(ck1[:, h0:h0 + 4, kt * P:(kt + 1) * P], b3, bc_in(cumq[:, 1, h0:h0 + 4], P), ALU.subtract), use)
            for i in range(S5T):
                use = USE["s5_u"][i]
                dve.wait_ge(s5_tab, i + 1)
                if i:
                    dve.wait_ge(s5_state, i)
                wait_full(dve, use)
                two = lambda x: x.rearrange("p (c t) -> p c t", c=2)
                ch.mark(tt(two(s5_m1), two(bank(use)), bc_out(etab[:, i % 2, 0, :], 2), ALU.mult))
                freed(tt(two(s5_m2), two(bank(use)), bc_out(etab[:, i % 2, 1, :], 2), ALU.mult), use)
                ch.sync()
                wait_read(dve, use)
                ch.mark(tt(s5_wt[:, 0:T], s5_m1[:, 0:T], s5_m2[:, T:2 * T], ALU.add))
                ch(tt(s5_wt[:, T:2 * T], s5_m1[:, T:2 * T], s5_m2[:, 0:T], ALU.subtract))
                r = mag[:, i:i + 1].to_broadcast([P, T])
                for part in range(2):
                    ch.mark(v.tensor_tensor_scan(s5_zt[:, part * T:(part + 1) * T], r, s5_wt[:, part * T:(part + 1) * T],
                                                 0.0, ALU.mult, ALU.add))
                ch.sync()
                ch.mark(tt(two(s5_n1), two(s5_zt), bc_out(etab[:, i % 2, 0, :], 2), ALU.mult))
                tt(two(s5_n2), two(s5_zt), bc_out(etab[:, i % 2, 1, :], 2), ALU.mult).then_inc(s5_n, 1)
                ch.sync()
                dve.wait_ge(s5_n, i + 1)
                if i >= 2:
                    if (i - 2) % 4 == 3:
                        wait_full(dve, USE["s5_y"][(i - 2) // 4])
                    else:
                        dve.wait_ge(s5_part, (i - 2) + 1 - (i - 2) // 4)
                ch.mark(tt(s_ri[:, i % 2, 0, :], s5_n1[:, 0:T], s5_n2[:, T:2 * T], ALU.subtract))
                stt(s_ri[:, i % 2, 1, :], s5_n1[:, T:2 * T], -1.0, s5_n2[:, 0:T], ALU.mult, ALU.subtract).then_inc(s5_state, 1)
                if i % 4 == 3:
                    blk = i // 4
                    use = USE["s5_y"][blk]
                    wait_full(dve, use)
                    freed(stt(y_a[:, blk, :], uT[:, blk, :], col("s5_d")[:, blk:blk + 1], bank(use)[:, 0:T], ALU.mult, ALU.add), use)
                    use = USE["glu"][blk]
                    wait_read(dve, use)
                    tt(y_a[:, blk, :], y_a[:, blk, :], glu_sig[:, blk % 2, :], ALU.mult).then_inc(ya_done, 1)

            def fa_scale(n):
                width = (n % 2 + 1) * P
                dve.wait_ge(fa_exp, n + 1)
                ch(v.reciprocal(fa_inv[:, n:n + 1], fa_sum[:, n:n + 1]))
                ts(fa_p[:, n % 3, 0:width], fa_p[:, n % 3, 0:width], fa_inv[:, n:n + 1], None, ALU.mult).then_inc(fa_norm, 1)

            dve.wait_ge(masked, 4)
            for n in range(NATT):
                a, t = n // 2, n % 2
                width = (t + 1) * P
                use = USE["fa_s"][n]
                wait_full(dve, use)
                if n >= 3:
                    wait_full(dve, USE["fa_t"][n - 3])
                bias = ck1[:, a, :] if t else ck0[:, a, :]
                freed(stt(fa_p[:, n % 3, 0:width], bank(use)[:, 0:width], AHD ** -0.5, bias, ALU.mult, ALU.subtract), use)
                wait_read(dve, use)
                ch(v.reduce_max(fa_max[:, n:n + 1], fa_p[:, n % 3, 0:width], axis=AXX))
                ts(fa_max[:, n:n + 1], fa_max[:, n:n + 1], -1.0, None, ALU.mult).then_inc(fa_mx, 1)
                if n:
                    fa_scale(n - 1)
            fa_scale(NATT - 1)
            dve.wait_ge(margins, 3)
            for use in USE["in_b"]:
                wait_read(dve, use)
            cw = col("conv_w_2").rearrange("p (b k) -> p b k", k=3)
            for b in range(4):
                ch.mark(tt(cin2[:, b, 2:T + 2], cin2[:, b, 2:T + 2], cin2[:, 8 + b, 2:T + 2], ALU.mult))
            ch.sync()
            for b in range(4):
                ch.mark(ts(y_b[:, b, :], cin2[:, b, 0:T], cw[:, b, 0:1], None, ALU.mult))
            for k in (1, 2):
                ch.sync()
                for b in range(4):
                    ch.mark(stt(y_b[:, b, :], cin2[:, b, k:k + T], cw[:, b, k:k + 1], y_b[:, b, :], ALU.mult, ALU.add))
            ch.sync()
            for b in range(4):
                tt(y_b[:, b, :], y_b[:, b, :], cin2[:, 4 + b, 2:T + 2], ALU.mult).then_inc(yb_done, 1)
            row_diag(4)
            for j in range(8):
                m_a, m_b = m_ab[:, j % 2, :], m_c[:, j % 2, :]
                if j >= 2:
                    dve.wait_ge(merged, j - 1)
                dve.wait_ge(gates_ready, j + 1)
                u0, u1 = USE["branch"][2 * j], USE["branch"][2 * j + 1]
                wait_full(dve, u0)
                freed(tt(m_a, bank(u0), gT[:, 3 * j:3 * j + 2, :].rearrange("p a t -> p (a t)"), ALU.mult), u0)
                wait_full(dve, u1)
                freed(tt(m_b, bank(u1)[:, 0:T], gT[:, 3 * j + 2, :], ALU.mult), u1)
                wait_read(dve, u0)
                ch(tt(m_a[:, 0:T], m_a[:, 0:T], m_a[:, T:2 * T], ALU.add))
                wait_read(dve, u1)
                tt(mT[:, j, :], m_a[:, 0:T], m_b, ALU.add).then_inc(merged, 1)
            post(4)
            norm_scale(6)
            norm_evac(6)
            row_diag(5)
            ffn("ff", NF2, 2 * NF, 0)
            post(5)

        @block.gpsimd
        def _(pool):
            gp = nc.gpsimd
            tt = gp.tensor_tensor
            ch = Chain(pool, pool_c)
            quad = lambda x: x.rearrange("p (a b) -> p a b", a=NH)

            cin24 = cin.rearrange("p b s t -> p (b s) t")
            ch.mark(gp.memset(cin24[:, :, 0:2], 0.0))
            ch.mark(gp.memset(cin24[:, :, T + 2:T + 4], 0.0))
            gp.memset(halfpi[:, :], HALF_PI).then_inc(half_ready, 1)
            ch.sync()
            gp.memset(tick[:, :], 0.0).then_inc(margins, 1)
            for use in USE["hyb_t"][6:10]:
                wait_read(pool, use)
            for st in range(4):
                src = ptok[:, st, 768:784] if st < 2 else pctx[:, st - 2, 256:272]
                gp.tensor_copy(ba[:, st, :], src).then_inc(ba_ready, 1)
            for use in USE["hyb_t"][0:6]:
                wait_read(pool, use)
            for t in range(TT):
                pool.wait_ge(conv_done, 3)
                x = ptok[:, t, 0:640]
                tt(att_sq[:, 640 * t:640 * t + 640], x, x, ALU.mult).then_inc(att_sq_ready, 1)
            for t in range(TT):
                x = pctx[:, t, 0:128]
                tt(att_sq[:, 1280 + 128 * t:1408 + 128 * t], x, x, ALU.mult).then_inc(att_sq_ready, 1)
            pool.wait_ge(att_rs, 1)
            pool.wait_ge(rows_loaded, 16)
            heads = lambda x: x.rearrange("p (a b) -> p a b", b=AHD)
            for t in range(TT):
                ch.mark(tt(heads(qk[:, t, :]), heads(ptok[:, t, 0:640]), bc_in(att_r[:, 10 * t:10 * t + 10], AHD), ALU.mult))
                ch.mark(tt(heads(kctx[:, t, :]), heads(pctx[:, t, 0:128]), bc_in(att_r[:, 20 + 2 * t:22 + 2 * t], AHD), ALU.mult))
            ch.sync()
            for t in range(TT):
                ch.mark(tt(qk[:, t, :], qk[:, t, :], row("qk_norm"), ALU.mult))
                ch.mark(tt(kctx[:, t, :], kctx[:, t, :], row("qk_norm")[:, 512:640], ALU.mult))
            ch.sync()
            halves = lambda x: x.rearrange("p (a b c d) -> p a b c d", a=10, b=2, c=2)
            for t in range(TT):
                ch.mark(tt(heads(rot_a[:, t, :]), heads(qk[:, t, :]), bc_out(cos_t[:, t, :], 10), ALU.mult))
                for c in range(2):
                    s4 = sin_t[:, t, :].rearrange("p (b c d) -> p b c d", b=2, c=2)[:, :, c, :]
                    ch.mark(tt(halves(rot_b[:, t, :])[:, :, :, c, :], halves(qk[:, t, :])[:, :, :, 1 - c, :],
                               s4.unsqueeze(1).to_broadcast([P, 10, 2, 16]), ALU.mult))
            ch.sync()
            for t in range(TT):
                ch.mark(tt(rot_a[:, t, :], rot_a[:, t, :], rot_b[:, t, :], ALU.add))
            ch.sync()
            gp.memset(tick[:, :], 0.0).then_inc(att_rope, 1)
            pool.wait_ge(g_ready, 1)
            wait_full(pool, USE["to_tok"][9])
            for n in range(8):
                d, st = n // 4, n % 4
                tt(quad(X[:, n, :]), bc_out(const(("le", "ge")[d]), NH), bc_in(g[:, st, 4 * d:4 * d + 4], P), ALU.mult).then_inc(gtri_ready, 1)
            for n in range(8):
                wait_read(pool, USE["decay"][n])
                tt(quad(UT[:, n, :]), quad(UT[:, n, :]), bc_out(const(("neg_f", "neg_b")[n // 4]), NH), ALU.add).then_inc(dmask, 1)
            for st in range(4):
                for d in range(2):
                    if d:
                        wait_read(pool, USE["kk"][st])
                    else:
                        pool.wait_ge(ut_part, st + 1)
                    n = 4 * d + st
                    tt(quad(UT[:, n, :]), quad(UT[:, n, :]), bc_in(beta[:, st, 4 * d:4 * d + 4], P), ALU.mult).then_inc(ut_ready, 1)
            pool.wait_ge(ut_ready, 8)
            for level in range(1, LEVELS):
                for n in range(8):
                    if level > 1:
                        wait_full(pool, USE["q", level - 1][n])
                    tt(quad(BP[:, n, :]), quad(UT[:, n, :]), bc_out(levels[:, n // 4, level, :], NH), ALU.mult).then_inc(blocks_ready, 1)
            wait_full(pool, USE["q", LEVELS - 1][7])
            for s in range(3):
                for d in range(2):
                    st = ORDER[d][s]
                    if s:
                        wait_full(pool, USE["ds", s - 1, d])
                    tt(quad(kt_st[:, d, :]), quad(ktok[:, st, :]), bc_in(etail[:, st, 4 * d:4 * d + 4], P), ALU.mult).then_inc(ktail_ready, 1)
            pool.wait_ge(h_ready, 4)
            ch.mark(gp.memset(cu[:, :, 0:15], 0.0))
            ch.mark(gp.memset(cu[:, :, T + 15:T + 30], 0.0))
            ch.mark(gp.memset(bbd.rearrange("p a b c -> p (a b c)"), 0.0))
            ch.sync()
            gp.memset(tick[:, :], 0.0).then_inc(margins, 1)
            pool.wait_ge(h_ready, 6)
            ch.mark(gp.memset(cin2[:, :, 0:2], 0.0))
            ch.sync()
            gp.memset(tick[:, :], 0.0).then_inc(margins, 1)
            for n in range(4):
                kt, h0 = n // 2, 4 * (n % 2)
                wait_read(pool, USE["cum_k"][n])
                dst = ck1[:, h0:h0 + 4, P:2 * P] if kt else ck0[:, h0:h0 + 4, :]
                tt(dst, dst, bc_out(const("neg_b"), 4), ALU.subtract).then_inc(masked, 1)

            def tables(i):
                grid = lambda x: x.rearrange("p (a b) -> p a b", a=16)
                c_b, c_a = (small_trig[:, 0, i, at:at + 16] for at in (0, 16))
                s_b, s_a = (small_trig[:, 1, i, at:at + 16] for at in (0, 16))
                if i:
                    pool.wait_ge(s5_tab, i)
                for out_at, (x, y, op) in enumerate((((c_a, c_b), (s_a, s_b), ALU.subtract),
                                                     ((s_a, c_b), (c_a, s_b), ALU.add))):
                    ch.mark(tt(grid(etmp[:, 0, :]), bc_in(x[0], 16), bc_out(x[1], 16), ALU.mult))
                    ch.mark(tt(grid(etmp[:, 1, :]), bc_in(y[0], 16), bc_out(y[1], 16), ALU.mult))
                    ch.sync()
                    last = tt(etab[:, i % 2, out_at, :], etmp[:, 0, :], etmp[:, 1, :], op)
                    if out_at == 0:
                        ch(last)
                last.then_inc(s5_tab, 1)

            for i in range(S5T):
                if i >= 2:
                    pool.wait_ge(s5_n, i - 1)
                tables(i)


def lay_out(inputs):
    a = {k: np.asarray(x) for k, x in inputs.items()}

    def stationary(wt, per):
        nb = wt.shape[1] // P
        x = wt.reshape(KT, P, nb, P).transpose(2, 1, 0, 3).reshape(nb // per, per, P, D)
        return x.transpose(0, 2, 1, 3).reshape(nb // per, P, per * D)

    def moving(wt, per):
        x = wt.reshape(wt.shape[0] // P // per, per, P, D)
        return x.transpose(0, 2, 1, 3).reshape(-1, P, per * D)

    def by_columns(wt, width):
        n = wt.shape[1] // width
        return wt.reshape(KT, P, n, width).transpose(2, 1, 0, 3).reshape(n, P, KT * width)

    def cols_of(x):
        return x.reshape(-1, P).T

    w = {}
    for layer in range(2):
        w[f"mod{layer}"] = by_columns(a["w_mod"][layer], MOD_C)
        wi, wo = a["w_ffn_in"][layer], a["w_ffn_out"][layer]
        w[f"ffn{layer}"] = np.concatenate(
            [stationary(wi[:, :FFN_H], 1), stationary(wi[:, FFN_H:], 1), moving(wo, 1)], 2)
    hyb = a["hyb_w_in"][0]
    qkv, z_a, ba_w, q_b, k_b, v_b = np.split(hyb, np.cumsum([1536, 512, 16, 512, 128]), 1)
    pairs = [0, 4, 1, 5, 2, 6, 3, 7]
    q_b = q_b.reshape(D, AH, AHD)[:, pairs].reshape(D, 512)
    w["hyb_f"] = stationary(np.concatenate([qkv[:, 512:1024], qkv[:, 1024:], qkv[:, :512]], 1), 3)
    w["hyb_t"] = by_columns(np.concatenate([z_a, q_b, k_b, v_b, ba_w], 1), HYB_TC)
    wo = a["hyb_w_out"][0]
    w["hyb_o"] = moving(np.concatenate([wo[:512], wo[512:].reshape(AH, AHD, D)[pairs].reshape(512, D)], 0), 2)
    ci = a["conf_w_in"][0].reshape(D, 2, KT, P).transpose(0, 2, 1, 3).reshape(D, 2 * D)
    w["conf_i"] = stationary(ci, 2)
    w["conf_o"] = moving(a["conf_w_out"][0], 2)
    u, xbc, qk, vf, gates = np.split(a["w_in_2"][0], np.cumsum([512, 1536, 1024, 520]), 1)
    w["in_a"] = stationary(np.concatenate([u, qk], 1), 3)
    w["in_v"] = by_columns(vf, V2C)
    w["in_b"] = stationary(xbc, 3)
    w["in_g"] = stationary(gates.reshape(D, 3, KT, P).transpose(0, 2, 1, 3).reshape(D, 3 * D), 3)
    br = a["w_branch_2"][0].reshape(12, P, KT, P).transpose(2, 1, 0, 3).reshape(4, 2, P, 12 * P)
    w["branch"] = br.transpose(0, 2, 1, 3).reshape(4, P, 2 * 12 * P)
    w["out2"] = moving(a["w_out_2"][0], 2)
    w["ff"] = np.concatenate([stationary(a["w_ff1_2"][0], 1), moving(a["w_ff2_2"][0], 1)], 2)

    cond = np.stack([cols_of(a["c"][0]), cols_of(a["c_ctx"])], 2).reshape(P, 16)
    order = [4, 5, 6, 7, 8, 9, 10, 11, 0, 1, 2, 3]
    state = lambda x: x.reshape(S5T, P).T
    packed = {
        "cond": cond, "hyb_conv": a["hyb_conv_w"][0].reshape(CONV_A, 12, P)[:, order].transpose(2, 1, 0),
        "conf_dw_w": a["conf_dw_w"][0].reshape(CONF_K, KT, P).transpose(2, 1, 0),
        "conv_w_2": a["conv_w_2"][0].reshape(3, 4, P).transpose(2, 1, 0), "s5_d": cols_of(a["s5_d_2"][0]),
        "b_gate_2": a["b_gate_2"][0].reshape(3, KT, P).transpose(2, 1, 0),
        "a_re": state(a["s5_a_re_2"][0]), "a_im": state(a["s5_a_im_2"][0]),
        "log_dt": state(np.repeat(a["s5_log_dt_2"][0], 64)),
    }
    for name, n in COLS:
        if name not in packed:
            packed[name] = cols_of(a[name])
    cols = np.concatenate([packed[n].reshape(P, -1) for n, _ in COLS], 1)
    flat = {
        "a_log": a["hyb_a_log"].reshape(-1), "dt_bias": a["hyb_dt_bias"].reshape(-1), "b_f": a["fox_b_f_2"][0],
        "out_norm": a["hyb_out_norm"][0],
        "qk_norm": np.concatenate([np.tile(a["hyb_q_norm"][0], AH), np.tile(a["hyb_k_norm"][0], 2)]),
    }
    rows = np.broadcast_to(np.concatenate([flat[n] for n, _ in ROWS]), (P, NROWS))
    def s5_c(x):
        out = np.zeros((S5T, 2, 64, 2, 16), x.dtype)
        x = x.reshape(S5T, 2, 16, 64)
        for g2 in range(2):
            out[:, g2, :, g2, :] = x[:, g2].transpose(0, 2, 1)
        return out.reshape(S5T, P, 32).transpose(1, 0, 2)

    glu = np.zeros((4, 8, 16, 8, 16), a["s5_w_glu_2"].dtype)
    wg = a["s5_w_glu_2"][0].reshape(4, 8, 16, 16)
    for g8 in range(8):
        glu[:, g8, :, g8, :] = wg[:, g8]
    s5_b = lambda x: x.reshape(S5T, P, 16).transpose(1, 0, 2).reshape(P, 256)
    out = {f"w_{k}": x for k, x in w.items()}
    out.update(
        cols=cols, rows=rows, consts=constants(), b_out=a["conf_b_out"].reshape(1, D),
        c_bd=np.stack([s5_c(a["s5_c_re_2"][0]), s5_c(a["s5_c_im_2"][0])], 1).reshape(P, 1024),
        glu=glu.reshape(4, P, P).transpose(1, 0, 2).reshape(P, 512),
        b_s5=np.concatenate([s5_b(a["s5_b_re_2"][0]), s5_b(a["s5_b_im_2"][0])], 1),
        x=a["x"][0], ctx=a["ctx"][0])
    return {k: np.ascontiguousarray(x) for k, x in out.items()}


def kernel(**inputs):
    import concourse.bacc as bacc
    from concourse.bass_utils import run_bass_kernel_spmd

    arrays = lay_out(inputs)
    nc = bacc.Bacc("TRN2", target_bir_lowering=False, num_devices=1)
    at = {k: nc.dram_tensor(f"in_{k}", x.shape, F32, kind="ExternalInput").ap() for k, x in arrays.items()}
    out = nc.dram_tensor("out_0", (T, D), F32, kind="ExternalOutput").ap()
    build(nc, {name: at[f"w_{name}"] for name, _, _ in STREAM}, at["cols"], at["rows"], at["consts"],
          at["b_out"], at["c_bd"], at["glu"], at["b_s5"], at["x"], at["ctx"], out)
    r = run_bass_kernel_spmd(nc, [{f"in_{k}": x for k, x in arrays.items()}], core_ids=[0])
    return r.results[0]["out_0"].reshape(1, T, D)
```

```python
from contextlib import ExitStack

import numpy as np

import concourse.bass as bass
from concourse import mybir

F32 = mybir.dt.float32
F32R = mybir.dt.float32r
BF16 = mybir.dt.bfloat16
ALU = mybir.AluOpType
ACT = mybir.ActivationFunctionType
AXX = mybir.AxisListType.X

P = 128
D = 1024
T = 256
KT = D // P
TT = T // P
EPS = 1e-6
HD = 128
NH = 4
CONV_A = 5
AH, AHD = 8, 64
CONF_K = 31
CONV_PE = (5, 6, 7)
FFN_H = 2816
NF = FFN_H // P
NF2 = 4 * D // P
HYB_T = 1296
HYB_TC = HYB_T // 4
CTX_T = 272
V2C = 260
BIG = 1.0e30
LEVELS = 7
S5T = 16
HALF_PI = float(np.pi / 2)
PI = float(np.float32(np.pi))
TWO_PI = float(2 * np.pi)
TWO_PI_PARTS = [6.28125, 0.0019350051879882812, float(2 * np.pi - 6.28125 - 0.0019350051879882812)]
ROUND = 12582912.0

MOD_C = 384
NMOD = 6 * D // MOD_C
MOD_CTX = 6
MOD0_PE = (0, 2, 5)
SUMS = {key: n for n, key in enumerate([(0, j) for j in range(NMOD) if j not in MOD0_PE]
                                       + [(1, j) for j in range(NMOD)])}

STREAM = [
    ("mod0", NMOD, 8 * MOD_C), ("hyb_f", 4, 3072), ("hyb_t", 4, 8 * HYB_TC),
    ("hyb_o", 4, 2048), ("ffn0", NF, 3072), ("conf_i", 8, 2048), ("conf_o", 4, 2048),
    ("ffn1", NF, 3072), ("in_a", 4, 3072), ("in_v", 2, 8 * V2C), ("in_b", 4, 3072),
    ("in_g", 8, 3072), ("branch", 4, 3072), ("out2", 4, 2048), ("ff", NF2, 2048),
]
SLOTS = 4
SLOT = 3072
ORDERED = [("mod0", _j) for _j in range(MOD_CTX)]
for _j in range(8):
    ORDERED += [("hyb_f", _j) if _j < 4 else ("hyb_t", _j - 4), ("mod0", MOD_CTX + _j)]
ORDERED += [("mod0", _j) for _j in range(MOD_CTX + 8, NMOD)] + [("hyb_o", _j) for _j in range(4)]
ORDERED += [(_name, _j) for _name, _chunks, _ in STREAM[4:] for _j in range(_chunks)]
CHUNK = {key: _n for _n, key in enumerate(ORDERED)}
FIRST = {_name: CHUNK[_name, 0] for _name, _, _ in STREAM}

COLS = [
    ("cond", 16), ("b_mod", 96), ("g_mix_pre", 16), ("g_mix_post", 16), ("g_ffn_pre", 16),
    ("g_ffn_post", 16), ("conf_b_in", 16), ("conf_dw_w", 8 * CONF_K), ("conf_dw_b", 8),
    ("conf_ln_g", 8), ("conf_ln_b", 8), ("hyb_conv", 12 * CONV_A), ("g_pre_mix_2", 8),
    ("b_gate_2", 24), ("conv_w_2", 12), ("g_post_mix_2", 8), ("g_pre_mlp_2", 8),
    ("g_post_mlp_2", 8), ("s5_d", 4), ("a_re", 16), ("a_im", 16), ("log_dt", 16),
]
ROWS = [("a_log", 8), ("dt_bias", 8), ("b_f", 8), ("out_norm", HD), ("qk_norm", 640)]
CONSTS = [
    ("ident", P), ("ones", P), ("le", P), ("lt", P), ("ge", P), ("gt", P), ("neg_f", P),
    ("neg_b", P), ("levels", 2 * LEVELS * P), ("cos", TT * AHD), ("sin", TT * AHD), ("tvec", 32),
]


def offsets(table):
    at, out = 0, {}
    for name, n in table:
        out[name] = (at, n)
        at += n
    return out, at


COL_AT, NCOLS = offsets(COLS)
ROW_AT, NROWS = offsets(ROWS)
CONST_AT, NCONSTS = offsets(CONSTS)


def constants():
    i = np.arange(P)
    a, b = i[:, None], i[None, :]
    out = {
        "ident": a == b, "ones": np.ones((P, P)), "le": a <= b, "lt": a < b, "ge": a >= b,
        "gt": a > b,
        "neg_f": np.where(b >= a, 0.0, -BIG), "neg_b": np.where(b <= a, 0.0, -BIG),
    }
    masks = []
    for direction in range(2):
        for level in range(LEVELS):
            w = 1 << level
            m = (a // (2 * w) == b // (2 * w)) & ((a // w) % 2 == 0) & ((b // w) % 2 == 1)
            masks.append(m.T if direction else m)
    out["levels"] = np.stack(masks, 1).reshape(P, -1)
    tok = np.arange(T)
    inv = np.float32(10000.0) ** (-np.arange(16, dtype=np.float32) / np.float32(16))
    row = (tok // 64).astype(np.float32)[:, None] * inv
    col = (tok % 64).astype(np.float32)[:, None] * inv
    ang = np.concatenate([row, row, col, col], -1).astype(np.float32)
    sign = np.where((np.arange(AHD) % 32) < 16, -1.0, 1.0)
    for name, v in (("cos", np.cos(ang)), ("sin", np.sin(ang) * sign)):
        out[name] = v.reshape(TT, P, AHD).transpose(1, 0, 2).reshape(P, -1)
    out["tvec"] = np.broadcast_to(np.concatenate([np.arange(16), 16 * np.arange(16)]), (P, 32))
    return np.concatenate([np.asarray(out[n], np.float32) for n, _ in CONSTS], 1)


class Chain:

    def __init__(self, engine, sem):
        self.engine, self.sem, self.n = engine, sem, 0

    def mark(self, ins):
        self.n += 1
        ins.then_inc(self.sem, 1)

    def sync(self):
        self.engine.wait_ge(self.sem, self.n)

    def __call__(self, ins):
        self.mark(ins)
        self.sync()


class Banks:

    def __init__(self):
        self.n = [0] * 8

    def take(self, bank):
        self.n[bank] += 1
        return bank, self.n[bank] - 1

    def turn(self, n, banks=(0, 1, 2, 3)):
        return [self.take(banks[i % len(banks)]) for i in range(n)]


BANKS = Banks()
USE = {}


def take_y(name):
    before = BANKS.n[4:7]
    USE[name] = BANKS.take(7), before


USE["norm0"] = BANKS.turn(4)
USE["norm1"] = BANKS.turn(4, (4, 5, 6, 0))
USE["hyb_f"] = BANKS.turn(12)
USE["hyb_t"] = BANKS.turn(10)
USE["att_qk"] = BANKS.turn(3)
NATT = AH * TT
USE["att_s"] = BANKS.turn(NATT, (0, 1, 2))
USE["att_t"] = BANKS.turn(NATT, (3, 4))
USE["att_o"] = BANKS.turn(AH // 2, (5,))
USE["to_tok"] = BANKS.turn(6, (0, 1, 2, 3, 4, 5)) + BANKS.turn(4, (6, 7))
USE["to_feat"] = BANKS.turn(6, (0, 1, 2, 3, 4, 5))
USE["gates"] = BANKS.take(6)
USE["decay"] = BANKS.turn(8)
USE["kq"] = BANKS.turn(2, (4, 5))
USE["kk"] = BANKS.turn(4, (6, 7))
USE["x1"] = BANKS.turn(8, range(8))
for _l in range(1, LEVELS):
    USE["p", _l] = BANKS.turn(8, range(8))
    USE["q", _l] = BANKS.turn(8, range(8))
    if _l < LEVELS - 1:
        USE["t", _l] = BANKS.turn(8, range(8))
USE["mod1"] = [BANKS.take(7)]
for _s in range(4):
    for _d in range(2):
        if _s:
            USE["ks", _s, _d] = BANKS.take(_d)
    for _d in range(2):
        USE["vn", _s, _d] = BANKS.take(2 + _d)
        if _s >= 2:
            USE["os", _s, _d] = BANKS.take(4 + _d)
            USE["oi", _s, _d] = BANKS.take(6 + _d)
        if _s < 3:
            USE["ds", _s, _d] = BANKS.take(_d)
USE["mod1"].append(BANKS.take(4))
USE["y_t"] = BANKS.turn(2, (0, 1))
USE["row", 0] = BANKS.turn(2, (2, 3))
take_y(("y", 0))
USE["norm2"] = BANKS.turn(4)
USE["row", 1] = BANKS.turn(2, (0, 1))
USE["ffn0"] = BANKS.turn(NF)
take_y(("y", 1))
USE["norm3"] = BANKS.turn(4, (2, 3, 0, 1))
USE["conf_i"] = BANKS.turn(8)
USE["conv31"] = BANKS.turn(3, (2, 3))
USE["ln"] = BANKS.turn(2, (0, 1))
USE["row", 2] = BANKS.turn(2, (2, 3))
take_y(("y", 2))
USE["norm4"] = BANKS.turn(4)
USE["row", 3] = BANKS.turn(2, (0, 1))
USE["ffn1"] = BANKS.turn(NF)
take_y(("y", 3))
USE["norm5"] = BANKS.turn(4, (2, 3, 0, 1))
USE["in_a"] = BANKS.turn(12)
USE["in_v"] = BANKS.turn(4)
USE["b_bar"] = BANKS.turn(2, (4, 5))
USE["in_b"] = BANKS.turn(12)
USE["in_g"] = BANKS.turn(24)
USE["s5_u"] = BANKS.turn(S5T, (4, 5))
USE["s5_y"], USE["glu"], USE["cum_k"] = [], [], []
for _b in range(4):
    if _b == 3:
        USE["cum"] = BANKS.take(7)
        USE["cum_k"] += BANKS.turn(2, (7,))
    USE["s5_y"].append(BANKS.take(6))
    USE["glu"].append(BANKS.take(7))
USE["cum_k"] += BANKS.turn(2, (7,))
USE["fa_s"] = BANKS.turn(NATT, (4, 5))
USE["fa_t"] = BANKS.turn(NATT, (7,))
USE["fa_o"] = BANKS.turn(AH // 2, (6,))
USE["branch"] = BANKS.turn(16)
USE["row", 4] = BANKS.turn(2, (0, 1))
take_y(("y", 4))
USE["norm6"] = BANKS.turn(4, (2, 3, 0, 1))
USE["row", 5] = BANKS.turn(2, (2, 3))
USE["ff"] = BANKS.turn(NF2)
take_y(("y", 5))

FFNS = {"ffn0": (3, 0, 0), "ffn1": (3, 3 * NF, NF - 1), "ff": (2, 6 * NF, 2 * NF - 2)}

DONE = []
CHUNKS_OF = {_name: _chunks for _name, _chunks, _ in STREAM}
_used = 0
for _name, _j in ORDERED:
    _chunks = CHUNKS_OF[_name]
    if _name in FFNS:
        _parts, _before, _ = FFNS[_name]
        DONE.append(("split", _before + _parts * (_j + 1), SLOTS * _parts))
        continue
    if _name == "mod0" and (0, _j) in SUMS:
        DONE.append(("sums", SUMS[0, _j] + 1, SLOTS))
        continue
    if _name in ("hyb_f", "in_a", "in_b", "in_g"):
        _u = USE[_name][3 * _j + 2]
    elif _name == "hyb_t":
        _u = USE[_name][9 if _j == 3 else 2 * _j + 1]
    elif _name == "in_v":
        _u = USE[_name][2 * _j + 1]
    elif _name == "conf_i":
        _u = USE[_name][_j]
    elif _name == "branch":
        _u = USE[_name][4 * _j + 3]
    elif _j == _chunks - 1:
        _u = USE["y", {"hyb_o": 0, "conf_o": 2, "out2": 4}[_name]][0]
    else:
        _u = None
    if _u is None:
        _used += 1
        DONE.append(("used", _used, SLOTS))
    else:
        DONE.append((_u[0], _u[1] + 1, 1))

BLOCKS3 = [(_name, _b) for _name, _n in (("in_a", 12), ("in_v", 4), ("in_b", 12), ("in_g", 24)) for _b in range(_n)]
BESIDE = [2 if _i % 2 else 1 for _i in range(S5T)]

ORDER = ((2, 3, 0, 1), (3, 2, 1, 0))


def build(nc, w, w_mod1, cols_in, rows_in, consts_in, b_out_in, c_bd_in, glu_in, b_in, x_in, ctx_in, out):
    ctx = ExitStack()
    with ctx:
        def sb(name, n, dt=F32):
            return ctx.enter_context(nc.sbuf_tensor(name, [P, n], dt))

        def sb_both(name, n):
            with nc.sbuf_tensor(name, [P, n], F32) as plain:
                pass
            return plain, sb(name + "_r", n, F32R)

        def sem(name):
            return ctx.enter_context(nc.semaphore(name))

        def view(t, at, *dims):
            n = int(np.prod(dims))
            v = t[:, at:at + n]
            if len(dims) == 2:
                return v.rearrange("p (a b) -> p a b", a=dims[0])
            if len(dims) == 3:
                return v.rearrange("p (a b c) -> p a b c", a=dims[0], b=dims[1])
            return v

        def bc_in(ap, n):
            return ap.unsqueeze(2).to_broadcast([ap.shape[0], ap.shape[1], n])

        def bc_out(ap, n):
            return ap.unsqueeze(1).to_broadcast([ap.shape[0], n, ap.shape[1]])

        ring = sb("ring", SLOTS * SLOT)
        h = view(sb("h", TT * D), 0, TT, D)
        ybuf_t = sb("ybuf", TT * D)
        nrm_t = sb("nrm", TT * D)
        ybuf, nrm = view(ybuf_t, 0, TT, D), view(nrm_t, 0, TT, D)
        aT_t, aT_r = sb_both("aT", KT * 2 * T)
        aT = view(aT_t, 0, KT, 2 * T)
        consts = sb("consts", NCONSTS)
        cols = sb("cols", NCOLS)
        rows = sb("rows", NROWS)
        rowbc = sb("rowbc", D)
        diag = sb("diag", D)
        arena, arena_r = sb_both("arena", 16384)
        tok_t = sb("tok", TT * (HYB_T - 512) + TT * CTX_T)
        z_t = sb("z", TT * 512)
        o_t = sb("o", 1024)
        yT_t = sb("yT", KT * T)
        yT = view(yT_t, 0, KT, T)
        x_hi, x_lo = view(aT_r, 0, KT, T), view(aT_r, KT * T, KT, T)
        w_hi = [arena_r[:, at:at + SLOT] for at in (7168, 1024)]
        w_lo = [arena_r[:, at:at + SLOT] for at in (10240, 4096)]
        h_hi, h_lo = view(arena_r, 0, 2, T), view(arena_r, 2 * T, 2, T)
        sg, h_tmp = view(nrm_t, 0, 2, T), nrm_t[:, 2 * T:3 * T]
        small = sb("small", 700)
        cond = sb("cond", 16)
        mod_t = sb("mod", 2 * 96)
        ngain = view(sb("ngain", 7 * KT), 0, 7, KT)
        nshift = view(sb("nshift", 7 * KT), 0, 7, KT)
        pcol = view(sb("pcol", 6 * KT), 0, 6, KT)
        zeros = sb("zeros", 512, BF16)
        brow = tok_t[:, 0:D]
        psum = ctx.enter_context(nc.psum_tensor("psum", [P, 8 * 512], F32))

        def bank(use):
            b = use[0] if isinstance(use, tuple) else use
            return psum[:, 512 * b:512 * b + 512]

        Y = psum[:, 2048:4096].rearrange("p (t n) -> p t n", t=TT)

        def slot(c):
            s = c % SLOTS
            return ring[:, s * SLOT:(s + 1) * SLOT]

        def col(name):
            at, n = COL_AT[name]
            return cols[:, at:at + n]

        def row(name):
            at, n = ROW_AT[name]
            return rows[:, at:at + n]

        def const(name):
            at, n = CONST_AT[name]
            return consts[:, at:at + n]

        macs, macs_ctx = view(yT_t, 0, 4, MOD_C), view(z_t, 0, 2, MOD_C)
        macs1 = ring[:, 2 * SLOT:2 * SLOT + 6 * D]
        ident, ones = const("ident"), const("ones")
        levels = const("levels").rearrange("p (d l n) -> p d l n", d=2, l=LEVELS)
        cos_t = const("cos").rearrange("p (t n) -> p t n", t=TT)
        sin_t = const("sin").rearrange("p (t n) -> p t n", t=TT)
        modT = view(mod_t, 0, 2, 48, 2)

        _at = [0]

        def stat(n):
            _at[0] += n
            assert _at[0] <= 700
            return small[:, _at[0] - n:_at[0]]

        nss, nms, nsd, nrs = stat(14), stat(14), stat(14), stat(14)
        pss, pms, psd, prs = stat(12), stat(12), stat(12), stat(12)

        cv = view(arena, 0, 12, 2, T)
        cin = view(arena, 8192, 12, 2, T + 4)
        zgate = view(z_t, 0, TT, 512)
        ptok = view(tok_t, 0, TT, HYB_T - 512)
        pctx = view(tok_t, TT * (HYB_T - 512), TT, CTX_T)
        qk = view(arena, 8192, TT, 640)
        rot_a = view(arena, 9472, TT, 640)
        rot_b = view(arena, 10752, TT, 640)
        kctx = view(arena, 12032, TT, P)
        att_sq = arena[:, 10752:10752 + 1536]
        att_p = view(arena, 12288, 3, 512)
        att_pT = view(arena, 13824, 2, 4, T)
        att_r, att_ss = stat(24), stat(24)
        att_max, att_sum = stat(NATT), stat(NATT)
        att_inv = stat(NATT)
        qbT = view(rowbc, 0, 4, T)
        kbT = diag[:, 0:512]
        X = view(arena, 0, 8, 512)
        XT = view(arena, 4096, 8, 512)
        UT = view(arena, 8192, 8, 512)
        BP = view(arena, 12288, 8, 512)
        sq_kq = view(arena, 12288, 6, 512)
        kT = view(aT_t, 0, 2, NH, T)
        qT = view(aT_t, 2048, NH, T)
        S = view(aT_t, 3072, 2, 512)
        intraT = view(nrm_t, 0, 4, 512)
        vtok = view(ybuf_t, 0, 4, 512)
        ktok = view(tok_t, 0, 4, 512)
        o_sum = view(o_t, 0, TT, 512)
        qtok = o_sum
        r_st = view(arena, 12288, 2, 512)
        vn_st = view(arena, 12288 + 1024, 2, 512)
        kt_st = view(arena, 12288 + 2048, 2, 512)
        tmp_st = view(arena, 12288 + 3072, 2, 512)
        ymix = view(tok_t, 0, TT, 512)
        kq_ss, kq_r = stat(24), stat(24)
        ba = view(small, _at[0], 4, 16)
        stat(64)
        beta_t = stat(32)
        beta = beta_t.rearrange("p (s e) -> p s e", s=4)
        g_t, g_a, g_b = stat(32), stat(32), stat(32)
        g = g_t.rearrange("p (s e) -> p s e", s=4)
        na8 = stat(8)
        ngc = stat(32).rearrange("p (s e) -> p s e", s=4)
        eg = stat(32).rearrange("p (s e) -> p s e", s=4)
        etail = stat(32).rearrange("p (s e) -> p s e", s=4)
        etot = stat(32).rearrange("p (s e) -> p s e", s=4)
        ro_ss, ro_r = stat(8), stat(8)

        cu = view(arena, 0, KT, T + CONF_K - 1)
        cc = view(arena, 2304, KT, T)
        csq = view(arena, 4352, KT, T)
        csig = view(arena, 6400, 2, T)
        crs = arena[:, 6912:6912 + T]
        tap_diags = [(yT_t[:, :], arena[:, 8232:8232 + (CONF_K - 16) * P]), (ybuf_t[:, :], nrm_t[:, 0:(CONF_K - 16) * P])]
        cout = csq

        ring_ready = [sem(f"ring_ready{s}") for s in range(SLOTS)]
        ring_used = sem("ring_used")
        bank_full = [sem(f"bank_full{b}") for b in range(8)]
        bank_free = [sem(f"bank_free{b}") for b in range(8)]
        x_loaded, ctx_loaded = sem("x_loaded"), sem("ctx_loaded")
        cols_loaded, consts_loaded = sem("cols_loaded"), sem("consts_loaded")
        rows_loaded, late_loaded, brow_loaded = sem("rows_loaded"), sem("late_loaded"), sem("brow_loaded")
        sums_ready = sem("sums_ready")
        mod1_loaded = [sem(f"mod1_loaded{q}") for q in range(2)]
        mac = sem("mac")
        mod_mm = sem("mod_mm")
        cond_ready = sem("cond_ready")
        zeros_ready = sem("zeros_ready")
        margins = sem("margins")
        mod_ready = sem("mod_ready")
        norm_ss, norm_ms, norm_sd, norm_x = (sem(f"norm_{x}") for x in ("ss", "ms", "sd", "x"))
        post_ss, post_ms, post_sd = (sem(f"post_{x}") for x in ("ss", "ms", "sd"))
        h_ready = sem("h_ready")
        diag_ready = sem("diag_ready")
        split_hi = sem("split_hi")
        split_ready = sem("split_ready")
        block_used = sem("block_used")
        x_rounded, x_split = sem("x_rounded"), sem("x_split")
        h_step = sem("h_step")
        act_on = sem("act_on")
        stored = sem("stored")
        act_c, dve_c, pool_c = sem("act_chain"), sem("dve_chain"), sem("pool_chain")


        conv_done, silu_done, zgate_ready = sem("conv_done"), sem("silu_done"), sem("zgate_ready")
        att_sq_ready, att_ms, att_sd, att_rope = sem("att_sq"), sem("att_ms"), sem("att_sd"), sem("att_rope")
        att_rs, att_mx, att_norm, att_half = sem("att_rs"), sem("att_mx"), sem("att_norm"), sem("att_half")
        kq_sq, kq_ms, kq_sd = sem("kq_sq"), sem("kq_ms"), sem("kq_sd")
        ba_ready, sp_in, sp_ready, g_ready = sem("ba_ready"), sem("sp_in"), sem("sp_ready"), sem("g_ready")
        gtri_ready, dsum, dmask, dec_ready = sem("gtri_ready"), sem("dsum"), sem("dmask"), sem("dec_ready")
        ut_part, ut_ready, xt_first = sem("ut_part"), sem("ut_ready"), sem("xt_first")
        blocks_ready = sem("blocks_ready")
        resid_ready, ktail_ready = sem("resid_ready"), sem("ktail_ready")
        ro_ms, ro_sd, y_mixed = sem("ro_ms"), sem("ro_sd"), sem("y_mixed")
        taps_ready = sem("taps_ready")
        csig_ready, conv31, csq_ready, csq_done = sem("csig_ready"), sem("conv31"), sem("csq_ready"), sem("csq_done")
        ln_sd, ln_x, conf_out = sem("ln_sd"), sem("ln_x"), sem("conf_out")
        s5_par, s5_mag, s5_arg, s5_trig = sem("s5_par"), sem("s5_mag"), sem("s5_arg"), sem("s5_trig")
        bbar_ready, logf_in, logf_sp, logf_ready = sem("bbar_ready"), sem("logf_in"), sem("logf_sp"), sem("logf_ready")
        cdiag_ready, s5_tab, masked = sem("cdiag_ready"), sem("s5_tab"), sem("masked")
        s5_n = sem("s5_n")
        s5_state, s5_part = sem("s5_state"), sem("s5_part")
        gelu_done, ya_done, yb_done = sem("gelu_done"), sem("ya_done"), sem("yb_done")
        half_ready = sem("half_ready")
        fa_mx, fa_exp, fa_norm, fa_half = sem("fa_mx"), sem("fa_exp"), sem("fa_norm"), sem("fa_half")
        gates_ready, merged = sem("gates_ready"), sem("merged")

        uT, q2T, k2T = (view(arena, 1024 * n, 4, T) for n in range(3))
        v2 = view(arena, 3072, TT, 2 * V2C)
        cin2 = view(arena, 4112, 12, T + 2)
        gT = view(arena, 7208, 24, T)
        y_c = view(arena, 13352, 4, T)
        small_trig = view(arena, 14376, 2, S5T, 32)
        glu = view(arena, 15400, 4, P)
        bbd = view(arena, 13352, 2, 4, P)
        trig_tmp = view(arena, 8232, 6, 512)
        cdiag = view(arena, 11304, 2, 512)
        y_a, y_b = yT[:, 0:4, :], yT[:, 4:8, :]
        mT = view(tok_t, 0, KT, T)
        bT = view(tok_t, 0, 2, 4, P)
        c_bd = view(tok_t, 1024, 2, S5T, 32)
        ck0, ck1 = view(o_t, 0, AH, P), view(ybuf_t, 0, AH, T)
        etab = view(rowbc, 0, 2, 2, T)
        s5_m1, s5_m2 = diag[:, 0:512], diag[:, 512:1024]
        s5_wt, s5_zt = nrm_t[:, 0:512], nrm_t[:, 512:1024]
        s5_n1, s5_n2 = nrm_t[:, 1024:1536], nrm_t[:, 1536:2048]
        s_ri = view(z_t, 0, 2, 2, T)
        etmp = view(yT_t, 1024, 2, T)
        fa_p, fa_pT = view(nrm_t, 0, 3, T), view(nrm_t, 768, 2, 2, T)
        _s5 = [15912]

        def s5v(n=16):
            _s5[0] += n
            assert _s5[0] <= 16384
            return arena[:, _s5[0] - n:_s5[0]]

        lam_re, dt, mag, theta, rk, phi, phi_hi, phi_lo = (s5v() for _ in range(8))
        sin_h, cos_h, sin_t1, cos_t1, num_re, num_im, den, co_re, co_im = (s5v() for _ in range(9))
        s5_a, s5_b, s5_c = (s5v() for _ in range(3))
        logf, lf_z, lf_a = (s5v().rearrange("p (t e) -> p t e", t=2) for _ in range(3))
        cumq = s5v().rearrange("p (t e) -> p t e", t=2)
        fa_max, fa_sum, fa_inv = s5v(), s5v(), s5v()
        bc_arr = view(arena, 12328, 2, 256)
        glu_sig = view(yT_t, 1536, 2, T)
        halfpi, tick, vtick = sb("halfpi", 1), sb("tick", 1), sb("vtick", 1)
        m_ab, m_c = view(nrm_t, 0, 2, 512), view(nrm_t, 1024, 2, T)

        block = ctx.enter_context(nc.Block())

        def wait_free(pe, use):
            if use[1]:
                pe.wait_ge(bank_free[use[0]], use[1])

        def wait_full(eng, use):
            eng.wait_ge(bank_full[use[0]], use[1] + 1)

        def wait_read(eng, use):
            eng.wait_ge(bank_free[use[0]], use[1] + 1)

        def filled(ins, use):
            ins.then_inc(bank_full[use[0]], 1)

        def freed(ins, use):
            ins.then_inc(bank_free[use[0]], 1)

        @block.sync
        def _(sp):
            def load(c, name, j, i=0):
                width = w[name].shape[2]
                part = w[name][j, :, :] if isinstance(i, int) else \
                    w[name][bass.ds(j + i, 1), :, :].rearrange("a p n -> p (a n)")
                sp.dma_start(slot(c)[:, 0:width], part).then_inc(ring_ready[c % SLOTS], 16)

            def wait_used(c, i=0):
                if c >= SLOTS:
                    who, count, a_turn = DONE[c - SLOTS]
                    done = {"used": ring_used, "sums": sums_ready, "split": split_ready}
                    sp.wait_ge(done[who] if who in done else bank_full[who], count + a_turn * i)

            for c in range(FIRST["hyb_o"]):
                wait_used(c)
                load(c, *ORDERED[c])
            for j in range(NMOD):
                if j < 2:
                    wait_used(FIRST["hyb_o"] + j)
                else:
                    sp.wait_ge(sums_ready, SUMS[1, j - 2] + 1)
                sp.dma_start(slot(j % 2), w_mod1[j, :, :]).then_inc(mod1_loaded[j % 2], 16)
            for name, n, _ in STREAM[3:]:
                c0 = FIRST[name]
                head = min(n, SLOTS)
                for j in range(head):
                    if name == "hyb_o":
                        if j < 2:
                            sp.wait_ge(sums_ready, SUMS[1, NMOD - 2 + j] + 1)
                        else:
                            wait_full(sp, USE["mod1"][1])
                    wait_used(c0 + j)
                    load(c0 + j, name, j)
                turns = (n - head) // SLOTS
                if turns > 1:
                    with sp.Fori(0, turns) as i:
                        for s in range(SLOTS):
                            wait_used(c0 + head + s, i)
                            load(c0 + head + s, name, head + s, SLOTS * i)
                    head += turns * SLOTS
                for j in range(head, n):
                    wait_used(c0 + j)
                    load(c0 + j, name, j)
            for t in range(TT):
                sp.wait_ge(h_ready, 10 + t + 1)
                sp.dma_start(out[t * P:(t + 1) * P, :], h[:, t, :]).then_inc(stored, 16)
            sp.wait_ge(stored, 16 * TT)

        @block.tensor
        def _(pe):
            mm = nc.tensor.matmul

            def wait_ring(c, i=0):
                pe.wait_ge(ring_ready[c % SLOTS], 16 * (c // SLOTS + 1) + 16 * i)

            def transposes(use, parts):
                wait_free(pe, use)
                for n, part in enumerate(parts):
                    last = nc.tensor.transpose(bank(use)[:, n * P:(n + 1) * P], part, ident)
                filled(last, use)

            def norm(i):
                pe.wait_ge(norm_x, 2 * (i + 1))
                src = ybuf if i == 0 else nrm
                for kp, use in enumerate(USE[f"norm{i}"]):
                    transposes(use, [src[:, t, k * P:(k + 1) * P]
                                     for k in (2 * kp, 2 * kp + 1) for t in range(TT)])

            def wait_aT(i):
                for use in USE[f"norm{i}"]:
                    wait_read(pe, use)

            def mod0(j):
                own = j in MOD0_PE
                c = CHUNK["mod0", j]
                if own:
                    wait_ring(c)
                else:
                    n = SUMS[0, j]
                    pe.wait_ge(sums_ready, n + 1)
                for b in range(3):
                    at = 3584 + 2 * (3 * j + b)
                    if own:
                        for k in range(KT):
                            last = mm(psum[:, at:at + 2], slot(c)[:, k * MOD_C + b * P:k * MOD_C + (b + 1) * P],
                                      cond[:, 2 * k:2 * k + 2], start=(k == 0), stop=(k == KT - 1))
                        continue
                    if j < MOD_CTX:
                        mm(psum[:, at + 1:at + 2], macs_ctx[:, n % 2, b * P:(b + 1) * P], ones[:, 0:1], start=True, stop=True)
                    last = mm(psum[:, at:at + 1], macs[:, n % 4, b * P:(b + 1) * P], ones[:, 0:1], start=True, stop=True)
                last.then_inc(ring_used if own else mod_mm, 1)

            def feature_block(use, weights, rhs, out_at=0):
                for k in range(KT):
                    last = mm(bank(use)[:, out_at:out_at + rhs(k).shape[1]],
                              weights[:, k * P:(k + 1) * P], rhs(k), start=(k == 0), stop=(k == KT - 1))
                return last

            def row_bc(p):
                pe.wait_ge(diag_ready, p + 1)
                for half, use in enumerate(USE["row", p]):
                    wait_free(pe, use)
                    filled(mm(bank(use), ones, diag[:, half * 512:half * 512 + 512], start=True, stop=True), use)

            def wait_y(p):
                (b, n), before = USE["y", p]
                if n:
                    pe.wait_ge(bank_free[b], n)
                for q, count in enumerate(before):
                    if count:
                        pe.wait_ge(bank_free[4 + q], count)

            def out_rows(c0, lhs, p, wait=None, bias=False):
                wait_y(p)
                if bias:
                    for t in range(TT):
                        for half in range(2):
                            mm(Y[:, t, half * 512:half * 512 + 512], ones[0:1, :],
                               brow[0:1, half * 512:half * 512 + 512], start=True, stop=False)
                for c in range(4):
                    wait_ring(c0 + c)
                    for kk in range(2):
                        k = 2 * c + kk
                        if wait:
                            wait(k)
                        for t in range(TT):
                            for half in range(2):
                                at = kk * D + half * 512
                                last = mm(Y[:, t, half * 512:half * 512 + 512],
                                          lhs[:, k, t * P:(t + 1) * P], slot(c0 + c)[:, at:at + 512],
                                          start=(k == 0 and not bias), stop=(k == KT - 1))
                    if c < 3:
                        last.then_inc(ring_used, 1)
                    else:
                        filled(last, USE["y", p][0])

            def ffn(name, n, p):
                uses, (parts, before, _) = USE[name], FFNS[name]
                wait_y(p)
                pe.wait_ge(zeros_ready, 1)
                for t in range(TT):
                    for half in range(2):
                        mm(Y[:, t, half * 512:half * 512 + 512], zeros[:, 0:P], zeros[:, :], start=True, stop=False)

                def wait_part(j, part, i):
                    pe.wait_ge(split_ready, before + parts * j + part + 1 + SLOTS * parts * i)

                def block_in(j, i=0):
                    use = uses[j]
                    if isinstance(i, int):
                        wait_free(pe, use)
                    else:
                        pe.wait_ge(bank_free[use[0]], use[1] + i)
                    for part in range(parts - 1):
                        wait_part(j, part, i)
                        into = bank(use)[:, part * T:(part + 1) * T]
                        for k in range(KT):
                            at = part * D + k * P
                            hi, lo = w_hi[j % 2][:, at:at + P], w_lo[j % 2][:, at:at + P]
                            mm(into, hi, x_hi[:, k, :], start=(k == 0), stop=False)
                            mm(into, hi, x_lo[:, k, :], start=False, stop=False)
                            last = mm(into, lo, x_hi[:, k, :], start=False, stop=(k == KT - 1))
                    filled(last, use)

                def block_out(j, i=0, stop=False):
                    use, at = uses[j], (parts - 1) * D
                    wait_part(j, parts - 1, i)
                    pe.wait_ge(bank_free[use[0]], use[1] + 1 + i)
                    for t in range(TT):
                        hi, lo = (x[:, j % 2, t * P:(t + 1) * P] for x in (h_hi, h_lo))
                        for act_part, w_part in ((hi, w_hi), (hi, w_lo), (lo, w_hi)):
                            for half in range(2):
                                last = mm(Y[:, t, half * 512:half * 512 + 512], act_part,
                                          w_part[j % 2][:, at + half * 512:at + half * 512 + 512],
                                          start=False, stop=stop and act_part is lo)
                    if stop:
                        filled(last, USE["y", p][0])
                    else:
                        last.then_inc(block_used, 1)

                for j in range(2):
                    block_in(j)
                    if j:
                        block_out(0)
                turns = (n - 2) // SLOTS
                with pe.Fori(0, turns) as i:
                    for j in range(2, 2 + SLOTS):
                        block_in(j, i)
                        block_out(j - 1, i)
                for j in range(2 + SLOTS * turns, n):
                    block_in(j)
                    block_out(j - 1)
                block_out(n - 1, 0, True)

            pe.wait_ge(cond_ready, 1)
            mod0(0)
            pe.wait_ge(consts_loaded, 16)
            norm(0)
            for j in range(1, MOD_CTX):
                mod0(j)
            norm(1)
            wait_aT(0)
            wait_aT(1)

            for c in range(4):
                wait_ring(CHUNK["hyb_f", c])
                for b in range(3):
                    use = USE["hyb_f"][3 * c + b]
                    wait_free(pe, use)
                    width = 2 * T if 3 * c + b < 8 else T
                    last = feature_block(use, slot(CHUNK["hyb_f", c])[:, b * D:(b + 1) * D], lambda k: aT[:, k, 0:width])
                    filled(last, use)
                if c:
                    mod0(MOD_CTX + c - 1)

            uses = iter(USE["hyb_t"])
            for c in range(4):
                wait_ring(CHUNK["hyb_t", c])
                for tile in range(TT if c < 3 else 2 * TT):
                    use = next(uses)
                    wait_free(pe, use)
                    wt = slot(CHUNK["hyb_t", c])
                    for k in range(KT):
                        last = mm(bank(use)[:, 0:HYB_TC], aT[:, k, tile * P:(tile + 1) * P],
                                  wt[:, k * HYB_TC:(k + 1) * HYB_TC], start=(k == 0), stop=(k == KT - 1))
                    filled(last, use)
                mod0(MOD_CTX + c + 3)
            for j in range(MOD_CTX + 7, NMOD):
                mod0(j)

            pe.wait_ge(att_rope, 1)
            for t in range(TT):
                transposes(USE["att_qk"][t], [rot_a[:, t, m * P:(m + 1) * P] for m in range(4)])
            transposes(USE["att_qk"][2], [kctx[:, 0, :], kctx[:, 1, :], rot_a[:, 0, 512:640], rot_a[:, 1, 512:640]])
            for use in USE["att_qk"]:
                wait_read(pe, use)
            for n in range(NATT + 4):
                if n < NATT:
                    a, t = n // 2, n % 2
                    q0 = 64 * (a % 2)
                    use = USE["att_s"][n]
                    wait_free(pe, use)
                    filled(mm(bank(use), qbT[q0:q0 + 64, a // 2, t * P:(t + 1) * P], kbT[q0:q0 + 64, :],
                              start=True, stop=True), use)
                if 2 <= n < NATT + 2:
                    m = n - 2
                    pe.wait_ge(att_norm, m + 1)
                    transposes(USE["att_t"][m], [att_p[:, m % 3, kb * P:(kb + 1) * P] for kb in range(4)])
                if n >= 4 and n % 2 == 1:
                    a = (n - 4) // 2
                    wait_read(pe, USE["att_t"][2 * a + 1])
                    use = USE["att_o"][a // 2]
                    if a % 2 == 0:
                        wait_free(pe, use)
                    q0 = 64 * (a % 2)
                    for kb in range(4):
                        v = pctx[:, kb, 128 + q0:192 + q0] if kb < 2 else ptok[:, kb - 2, 640 + q0:704 + q0]
                        last = mm(bank(use)[q0:q0 + 64, 0:T], v, att_pT[:, a % 2, kb, :],
                                  start=(kb == 0), stop=(kb == 3))
                    if a % 2:
                        filled(last, use)
                    else:
                        last.then_inc(att_half, 1)

            pe.wait_ge(silu_done, 12)
            for n in range(4):
                seq, t = (n // 2, n % 2)
                transposes(USE["to_tok"][n], [cv[:, hh, seq, t * P:(t + 1) * P] for hh in range(NH)])
            for t in range(TT):
                transposes(USE["to_tok"][4 + t], [cv[:, 8 + hh, 0, t * P:(t + 1) * P] for hh in range(NH)])
            pe.wait_ge(mod_ready, 2)
            for n in range(4):
                seq, t = (n // 2, n % 2)
                transposes(USE["to_tok"][6 + n], [cv[:, 4 + hh, seq, t * P:(t + 1) * P] for hh in range(NH)])
            for n in range(6):
                wait_read(pe, USE["to_tok"][n])
                src = ktok[:, n, :] if n < 4 else qtok[:, n - 4, :]
                transposes(USE["to_feat"][n], [src[:, hh * P:(hh + 1) * P] for hh in range(NH)])
            use = USE["gates"]
            pe.wait_ge(g_ready, 1)
            wait_free(pe, use)
            for n, (name, d) in enumerate((("le", 0), ("ge", 1), ("gt", 0), ("lt", 1))):
                mm(bank(use)[:, 16 * n:16 * n + 16], const(name), g[:, :, 4 * d:4 * d + 4], start=True, stop=True)
            filled(mm(bank(use)[:, 64:96], ones, g_t, start=True, stop=True), use)
            for n in range(8):
                pe.wait_ge(gtri_ready, n + 1)
                use = USE["decay"][n]
                wait_free(pe, use)
                filled(mm(bank(use), ones, X[:, n, :], start=True, stop=True), use)
            for n in range(6):
                wait_read(pe, USE["to_feat"][n])

            def per_head(use, lhs, rhs, start=True, stop=True):
                for hh in range(NH):
                    last = mm(bank(use)[:, hh * P:(hh + 1) * P], lhs(hh), rhs(hh), start=True, stop=True)
                return last

            def feat(x, st, hh):
                return x[:, hh, (st % 2) * P:(st % 2 + 1) * P]

            for t in range(TT):
                use = USE["kq"][t]
                wait_free(pe, use)
                filled(per_head(use, lambda hh: feat(kT[:, 0], t, hh), lambda hh: feat(qT, t, hh)), use)
            for st in range(4):
                use = USE["kk"][st]
                wait_free(pe, use)
                kk = lambda hh: feat(kT[:, st // 2], st, hh)
                filled(per_head(use, kk, kk), use)
            hs = lambda x, n: (lambda hh: x[:, n, hh * P:(hh + 1) * P])
            for n in range(8):
                pe.wait_ge(xt_first, n + 1)
                transposes(USE["x1"][n], [XT[:, n, hh * P:(hh + 1) * P] for hh in range(NH)])
            for level in range(1, LEVELS):
                for n in range(8):
                    wait_read(pe, USE["x1"][n] if level == 1 else USE["t", level - 1][n])
                    pe.wait_ge(blocks_ready, 8 * (level - 1) + n + 1)
                    use = USE["p", level][n]
                    wait_free(pe, use)
                    filled(per_head(use, hs(BP, n), hs(X, n)), use)
                for n in range(8):
                    wait_read(pe, USE["p", level][n])
                    use = USE["q", level][n]
                    if level < LEVELS - 1:
                        filled(per_head(use, hs(XT, n), hs(BP, n)), use)
                    else:
                        filled(per_head(use, hs(BP, n), hs(XT, n)), use)
                if level < LEVELS - 1:
                    for n in range(8):
                        wait_read(pe, USE["q", level][n])
                        transposes(USE["t", level][n], [X[:, n, hh * P:(hh + 1) * P] for hh in range(NH)])
            for n in range(8):
                wait_read(pe, USE["q", LEVELS - 1][n])
            pe.wait_ge(sums_ready, SUMS[1, NMOD - 1] + 1)

            def mod1(b0, b1):
                use = USE["mod1"][b0 // 24]
                if b0 % 24 == 0:
                    wait_free(pe, use)
                for b in range(b0, b1):
                    last = mm(bank(use)[:, b % 24:b % 24 + 1], macs1[:, b * P:(b + 1) * P], ones[:, 0:1], start=True, stop=True)
                if b1 % 24 == 0:
                    filled(last, use)

            for s in range(4):
                for d in range(2):
                    st = ORDER[d][s]
                    if s:
                        wait_read(pe, USE["ds", s - 1, d])
                        use = USE["ks", s, d]
                        wait_free(pe, use)
                        filled(per_head(use, lambda hh: feat(kT[:, st // 2], st, hh),
                                        lambda hh: S[:, d, hh * P:(hh + 1) * P]), use)
                if s < 2:
                    mod1(12 * s, 12 * s + 6)
                for d in range(2):
                    st = ORDER[d][s]
                    n = 4 * d + st
                    if s >= 2:
                        use = USE["os", s, d]
                        wait_free(pe, use)
                        filled(per_head(use, lambda hh: feat(qT, st, hh),
                                        lambda hh: S[:, d, hh * P:(hh + 1) * P]), use)
                    pe.wait_ge(resid_ready, 2 * s + d + 1)
                    use = USE["vn", s, d]
                    wait_free(pe, use)
                    filled(per_head(use, hs(XT, n), hs(r_st, d)), use)
                if s < 2:
                    mod1(12 * s + 6, 12 * s + 12)
                for d in range(2):
                    st = ORDER[d][s]
                    wait_read(pe, USE["vn", s, d])
                    if s < 3:
                        pe.wait_ge(ktail_ready, 2 * s + d + 1)
                        use = USE["ds", s, d]
                        wait_free(pe, use)
                        filled(per_head(use, hs(kt_st, d), hs(vn_st, d)), use)
                    if s >= 2:
                        use = USE["oi", s, d]
                        wait_free(pe, use)
                        filled(per_head(use, hs(intraT, 2 * d + st), hs(vn_st, d)), use)
            mod1(24, 48)
            pe.wait_ge(y_mixed, 2)
            for t in range(TT):
                transposes(USE["y_t"][t], [ymix[:, t, hh * P:(hh + 1) * P] for hh in range(NH)])
            row_bc(0)
            for use in USE["y_t"] + USE["att_o"]:
                wait_read(pe, use)
            out_rows(FIRST["hyb_o"], yT, 0)
            norm(2)
            row_bc(1)
            pe.wait_ge(x_split, 4)
            ffn("ffn0", NF, 1)

            norm(3)
            wait_aT(3)
            c0 = FIRST["conf_i"]
            for c in range(8):
                wait_ring(c0 + c)
                use = USE["conf_i"][c]
                wait_free(pe, use)
                feature_block(use, slot(c0 + c)[:, 0:D], lambda k: aT[:, k, 0:T])
                filled(feature_block(use, slot(c0 + c)[:, D:2 * D], lambda k: aT[:, k, 0:T], T), use)
            for n, c in enumerate(CONV_PE):
                use = USE["conv31"][n]
                wait_read(pe, USE["conf_i"][c])
                pe.wait_ge(taps_ready, 2 * n + 2)
                wait_free(pe, use)
                for k in range(CONF_K):
                    at = P * (k % 16)
                    last = mm(bank(use)[:, 0:T], tap_diags[n % 2][k // 16][:, at:at + P], cu[:, c, k:k + T],
                              start=(k == 0), stop=(k == CONF_K - 1))
                filled(last, use)
            for use in USE["conv31"]:
                wait_read(pe, use)
            for n, src in enumerate((cc, csq)):
                use = USE["ln"][n]
                wait_free(pe, use)
                order = [*CONV_PE, *(k for k in range(KT) if k not in CONV_PE)] if n == 0 else range(KT)
                for i, k in enumerate(order):
                    if n == 0 and i >= len(CONV_PE):
                        pe.wait_ge(conv31, i + 1 - len(CONV_PE))
                    elif n == 1:
                        pe.wait_ge(csq_done, k + 1)
                    last = mm(bank(use)[:, 0:T], ones, src[:, k, :], start=(i == 0), stop=(i == KT - 1))
                filled(last, use)
            row_bc(2)
            pe.wait_ge(brow_loaded, 16)
            out_rows(FIRST["conf_o"], cout, 2, lambda k: pe.wait_ge(conf_out, k + 1), True)
            norm(4)
            row_bc(3)
            pe.wait_ge(x_split, 8)
            ffn("ffn1", NF, 3)

            norm(5)
            wait_aT(5)

            def projections():
                for name, b in BLOCKS3:
                    per = 2 if name == "in_v" else 3
                    c, use = FIRST[name] + b // per, USE[name][b]
                    if b % per == 0:
                        wait_ring(c)
                    wait_free(pe, use)
                    if name == "in_v":
                        t = b % 2
                        for k in range(KT):
                            last = mm(bank(use)[:, 0:V2C], aT[:, k, t * P:(t + 1) * P],
                                      slot(c)[:, k * V2C:(k + 1) * V2C], start=(k == 0), stop=(k == KT - 1))
                        filled(last, use)
                    else:
                        filled(feature_block(use, slot(c)[:, (b % 3) * D:(b % 3 + 1) * D], lambda k: aT[:, k, 0:T]), use)
                    yield
            filler = projections()
            for _ in range(4):
                next(filler)
            pe.wait_ge(bbar_ready, 1)
            for n in range(2):
                transposes(USE["b_bar"][n], [bbd[:, n, blk, :] for blk in range(4)])
            for use in USE["b_bar"]:
                wait_read(pe, use)

            def cum_k(n):
                pe.wait_ge(cdiag_ready, n + 1)
                use = USE["cum_k"][n]
                wait_free(pe, use)
                filled(mm(bank(use), ones, cdiag[:, n % 2, :], start=True, stop=True), use)

            def s5_in(i):
                use = USE["s5_u"][i]
                wait_free(pe, use)
                r0, blk = 32 * (i % 4), i // 4
                for part in range(2):
                    last = mm(bank(use)[:, part * T:(part + 1) * T], bT[r0:r0 + 32, part, blk, :],
                              uT[r0:r0 + 32, blk, :], start=True, stop=True)
                filled(last, use)

            pe.wait_ge(late_loaded, 48)
            for use in USE["in_a"][0:4]:
                wait_read(pe, use)
            s5_in(0)
            for i in range(S5T):
                next(filler)
                if i + 1 < S5T:
                    s5_in(i + 1)
                for _ in range(BESIDE[i] - 1):
                    next(filler)
                pe.wait_ge(s5_state, i + 1)
                r0, blk = 32 * (i % 4), i // 4
                use = USE["s5_y"][blk]
                if i % 4 == 0:
                    wait_free(pe, use)
                for part in range(2):
                    last = mm(bank(use)[r0:r0 + 32, 0:T], c_bd[:, part, i, :], s_ri[:, i % 2, part, :],
                              start=(part == 0), stop=(part == 1))
                if i % 4 == 3:
                    filled(last, use)
                else:
                    last.then_inc(s5_part, 1)
                if i == 13:
                    pe.wait_ge(logf_ready, 1)
                    use = USE["cum"]
                    wait_free(pe, use)
                    mm(bank(use)[:, 0:8], const("le"), logf[:, 0, :], start=True, stop=True)
                    mm(bank(use)[:, 8:16], ones, logf[:, 0, :], start=True, stop=False)
                    filled(mm(bank(use)[:, 8:16], const("le"), logf[:, 1, :], start=False, stop=True), use)
                if i == 14:
                    cum_k(0)
                    cum_k(1)
                if i % 4 == 3:
                    next(filler)
                    pe.wait_ge(gelu_done, blk + 1)
                    use = USE["glu"][blk]
                    wait_free(pe, use)
                    filled(mm(bank(use)[:, 0:T], glu[:, blk, :], y_a[:, blk, :], start=True, stop=True), use)
            cum_k(2)
            cum_k(3)

            for use in USE["in_a"] + USE["in_v"]:
                wait_read(pe, use)
            for n in range(NATT + 4):
                if n < NATT:
                    a, t = n // 2, n % 2
                    q0 = 64 * (a % 2)
                    use = USE["fa_s"][n]
                    wait_free(pe, use)
                    filled(mm(bank(use)[:, 0:(t + 1) * P], q2T[q0:q0 + 64, a // 2, t * P:(t + 1) * P],
                              k2T[q0:q0 + 64, a // 2, 0:(t + 1) * P], start=True, stop=True), use)
                    next(filler, None)
                if 2 <= n < NATT + 2:
                    m = n - 2
                    pe.wait_ge(fa_norm, m + 1)
                    transposes(USE["fa_t"][m], [fa_p[:, m % 3, kb * P:(kb + 1) * P] for kb in range(m % 2 + 1)])
                if n >= 4 and n % 2 == 1:
                    a = (n - 4) // 2
                    wait_read(pe, USE["fa_t"][2 * a + 1])
                    use = USE["fa_o"][a // 2]
                    if a % 2 == 0:
                        wait_free(pe, use)
                    q0 = 64 * (a % 2)
                    v = lambda kb: v2[:, kb, a * AHD:(a + 1) * AHD]
                    mm(bank(use)[q0:q0 + 64, 0:T], v(0), fa_pT[:, a % 2, 0, :], start=True, stop=False)
                    last = mm(bank(use)[q0:q0 + 64, P:T], v(1), fa_pT[:, a % 2, 1, P:T], start=False, stop=True)
                    if a % 2:
                        filled(last, use)
                    else:
                        last.then_inc(fa_half, 1)
            for _ in filler:
                pass

            pe.wait_ge(ya_done, 4)
            pe.wait_ge(yb_done, 4)
            for use in USE["fa_o"]:
                wait_read(pe, use)
            ys = (y_a, y_b, y_c)
            for j in range(8):
                c = FIRST["branch"] + j // 2
                if j % 2 == 0:
                    wait_ring(c)
                at = (j % 2) * 12 * P
                for part in range(2):
                    use = USE["branch"][2 * j + part]
                    wait_free(pe, use)
                    for br in ((0, 1), (2,))[part]:
                        for k in range(4):
                            wat = at + (4 * br + k) * P
                            last = mm(bank(use)[:, (br % 2) * T:(br % 2 + 1) * T], slot(c)[:, wat:wat + P],
                                      ys[br][:, k, :], start=(k == 0), stop=(k == 3))
                    filled(last, use)
            row_bc(4)
            out_rows(FIRST["out2"], mT, 4, lambda k: pe.wait_ge(merged, k + 1))
            norm(6)
            row_bc(5)
            pe.wait_ge(x_split, 12)
            ffn("ff", NF2, 5)

        @block.scalar
        def _(act):
            fn = nc.scalar.activation
            ch = Chain(act, act_c)

            act.dma_start(cols[:, :], cols_in).then_inc(cols_loaded, 16)
            act.dma_start(ybuf_t[:, :].rearrange("p (t n) -> p t n", t=TT), ctx_in.rearrange("(t p) n -> p t n", p=P)).then_inc(ctx_loaded, 16)
            act.dma_start(h, x_in.rearrange("(t p) n -> p t n", p=P)).then_inc(x_loaded, 16)
            act.dma_start(consts[:, :], consts_in).then_inc(consts_loaded, 16)
            act.dma_start(rows[:, :], rows_in).then_inc(rows_loaded, 16)
            act.wait_ge(cols_loaded, 16)
            fn(cond[:, :], col("cond"), ACT.Silu).then_inc(cond_ready, 1)

            def norm_stats(i):
                src = ybuf if i == 0 else h
                for t in range(TT):
                    if i == 0:
                        act.wait_ge(ctx_loaded, 16)
                    elif i == 1:
                        act.wait_ge(x_loaded, 16)
                    else:
                        act.wait_ge(h_ready, 2 * (i - 2) + t + 1)
                    fn(nrm[:, t, :], src[:, t, :], ACT.Square,
                       accum_out=nss[:, 2 * i + t:2 * i + t + 1]).then_inc(norm_ss, 1)
                act.wait_ge(norm_ms, i + 1)
                fn(nsd[:, 2 * i:2 * i + 2], nms[:, 2 * i:2 * i + 2], ACT.Sqrt).then_inc(norm_sd, 1)

            def norm_evac(i):
                at = T if i == 0 else 0
                for kp in (1, 3):
                    use = USE[f"norm{i}"][kp]
                    wait_full(act, use)
                    for j in range(2):
                        k = 2 * kp + j
                        dst = yT[:, k, :] if i in (2, 4, 6) else aT[:, k, at:at + T]
                        last = fn(dst, bank(use)[:, j * T:(j + 1) * T], ACT.Identity,
                                  scale=ngain[:, i, k:k + 1], bias=nshift[:, i, k:k + 1])
                    freed(last, use)
                    if i in (2, 4, 6):
                        wait_read(act, use)
                        fn(x_hi[:, 2 * kp:2 * kp + 2, :], yT[:, 2 * kp:2 * kp + 2, :], ACT.Copy).then_inc(x_rounded, 1)

            def row_copy(p):
                for half, use in enumerate(USE["row", p]):
                    wait_full(act, use)
                    freed(fn(rowbc[:, half * 512:half * 512 + 512], bank(use), ACT.Copy), use)

            def post_stats(p):
                use = USE["y", p][0]
                wait_full(act, use)
                for t in range(TT):
                    fn(ybuf[:, t, :], Y[:, t, :], ACT.Square,
                       accum_out=pss[:, 2 * p + t:2 * p + t + 1]).then_inc(post_ss, 1)
                act.wait_ge(post_ms, p + 1)
                fn(psd[:, 2 * p:2 * p + 2], pms[:, 2 * p:2 * p + 2], ACT.Sqrt).then_inc(post_sd, 1)

            def split(name, j, todo, i=0):
                (parts, _, used), uses, c = FFNS[name], USE[name], CHUNK[name, j]
                for part in todo:
                    if part == 0:
                        act.wait_ge(ring_ready[c % SLOTS], 16 * (c // SLOTS + 1) + 16 * i)
                    if j >= 2 and part == 0:
                        act.wait_ge(bank_full[uses[j - 2][0]], uses[j - 2][1] + 1 + i)
                    if j >= 2 and part == parts - 1:
                        act.wait_ge(block_used, used + j - 1 + SLOTS * i)
                    at = slice(part * D, part * D + D)
                    fn(w_hi[j % 2][:, at], slot(c)[:, at], ACT.Copy).then_inc(split_hi, 1)

            def ffn(name, n, func):
                uses, parts = USE[name], FFNS[name][0]

                def one(j, i=0):
                    if j + 1 < n:
                        split(name, j + 1, range(parts - 1), i)
                    act.wait_ge(bank_full[uses[j][0]], uses[j][1] + 1 + i)
                    if j >= 2:
                        act.wait_ge(bank_free[uses[j - 2][0]], uses[j - 2][1] + 1 + i)
                    fn(sg[:, j % 2, :], bank(uses[j])[:, 0:T], func).then_inc(act_on, 1)
                    if j + 1 < n:
                        split(name, j + 1, [parts - 1], i)

                for j in range(2):
                    one(j)
                turns = (n - 3) // SLOTS
                with act.Fori(0, turns) as i:
                    for q in range(SLOTS):
                        one(2 + q, i)
                for j in range(2 + SLOTS * turns, n):
                    one(j)

            norm_stats(0)
            norm_stats(1)
            act.wait_ge(mod_ready, 1)
            norm_evac(0)
            norm_evac(1)
            act.wait_ge(margins, 1)
            for b, use in enumerate(USE["hyb_f"]):
                wait_full(act, use)
                n = 2 if b < 8 else 1
                freed(fn(cin[:, b, 0:n, 2:T + 2], bank(use)[:, 0:n * T].rearrange("p (s t) -> p s t", s=n), ACT.Copy), use)
            uses = iter(USE["hyb_t"])
            for c in range(4):
                for t in range(TT):
                    use = next(uses)
                    wait_full(act, use)
                    at = c * HYB_TC
                    cut = min(max(512 - at, 0), HYB_TC)
                    if cut:
                        last = fn(zgate[:, t, at:at + cut], bank(use)[:, 0:cut], ACT.Copy)
                    if cut < HYB_TC:
                        last = fn(ptok[:, t, at + cut - 512:at - 512 + HYB_TC], bank(use)[:, cut:HYB_TC], ACT.Copy)
                    freed(last, use)
            for t in range(TT):
                use = next(uses)
                wait_full(act, use)
                freed(fn(pctx[:, t, :], bank(use)[:, HYB_TC - CTX_T:HYB_TC], ACT.Copy), use)
            for b in range(12):
                act.wait_ge(conv_done, b // 4 + 1)
                n = 2 if b < 8 else 1
                fn(cv[:, b, 0:n, :], cv[:, b, 0:n, :], ACT.Silu).then_inc(silu_done, 1)
            act.wait_ge(bank_free[USE["hyb_t"][5][0]], USE["hyb_t"][5][1] + 1)
            for t in range(TT):
                fn(zgate[:, t, :], zgate[:, t, :], ACT.Silu).then_inc(zgate_ready, 1)
            act.wait_ge(att_ms, 1)
            fn(att_ss, att_ss, ACT.Sqrt).then_inc(att_sd, 1)
            for n, use in enumerate(USE["att_qk"]):
                wait_full(act, use)
                if n < 2:
                    freed(fn(qbT[:, :, n * P:(n + 1) * P], bank(use).rearrange("p (a b) -> p a b", a=4), ACT.Copy), use)
                else:
                    freed(fn(kbT, bank(use), ACT.Copy), use)
            for n in range(NATT + 5):
                if n < NATT:
                    act.wait_ge(att_mx, n + 1)
                    if n >= 3:
                        wait_full(act, USE["att_t"][n - 3])
                    use = USE["att_s"][n]
                    wait_full(act, use)
                    freed(fn(att_p[:, n % 3, :], bank(use), ACT.Exp, scale=AHD ** -0.5,
                             bias=att_max[:, n:n + 1], accum_out=att_sum[:, n:n + 1]), use)
                if 2 <= n < NATT + 2:
                    m = n - 2
                    a, t = m // 2, m % 2
                    use = USE["att_t"][m]
                    wait_full(act, use)
                    if a >= 2:
                        if a % 2 == 0:
                            act.wait_ge(att_half, a // 2)
                        else:
                            wait_full(act, USE["att_o"][(a - 2) // 2])
                    freed(fn(att_pT[:, a % 2, :, t * P:(t + 1) * P],
                             bank(use).rearrange("p (a b) -> p a b", a=4), ACT.Copy), use)
                if n >= 8 and (n - 8) % 4 == 0:
                    m = (n - 8) // 4
                    use = USE["att_o"][m]
                    wait_full(act, use)
                    freed(fn(yT[:, 4 + m, :], bank(use)[:, 0:T], ACT.Copy), use)
            for n in range(6):
                use = USE["to_tok"][n]
                wait_full(act, use)
                fn(sq_kq[:, n, :], bank(use), ACT.Square).then_inc(kq_sq, 1)
            act.wait_ge(kq_ms, 1)
            fn(kq_ss, kq_ss, ACT.Sqrt).then_inc(kq_sd, 1)
            for n in range(4):
                use = USE["to_tok"][6 + n]
                wait_full(act, use)
                freed(fn(vtok[:, n, :], bank(use), ACT.Copy), use)
            act.wait_ge(ba_ready, 4)
            act.wait_ge(rows_loaded, 16)
            fn(beta, ba[:, :, 0:8], ACT.Sigmoid).then_inc(sp_ready, 1)
            act.wait_ge(sp_in, 1)
            ch(fn(g_a, g_a, ACT.Exp, scale=-1.0))
            ch.mark(fn(na8, row("a_log"), ACT.Exp))
            ch.sync()
            fn(g_a, g_a, ACT.Ln, bias=1.0).then_inc(sp_ready, 1)
            for n, use in enumerate(USE["to_feat"]):
                wait_full(act, use)
                dst = kT[:, n // 2, :, (n % 2) * P:(n % 2 + 1) * P] if n < 4 else qT[:, :, (n - 4) * P:(n - 3) * P]
                freed(fn(dst, bank(use).rearrange("p (a b) -> p a b", a=NH), ACT.Copy), use)
            use = USE["gates"]
            wait_full(act, use)
            act.wait_ge(dsum, 1)
            for n, (dst, d) in enumerate(((eg, 0), (eg, 1), (etail, 0), (etail, 1))):
                fn(dst[:, :, 4 * d:4 * d + 4], bank(use)[:, 16 * n:16 * n + 16].rearrange("p (s e) -> p s e", s=4), ACT.Exp)
            freed(fn(etot, bank(use)[:, 64:96].rearrange("p (s e) -> p s e", s=4), ACT.Exp), use)
            for n in range(8):
                act.wait_ge(dmask, n + 1)
                fn(UT[:, n, :], UT[:, n, :], ACT.Exp).then_inc(dec_ready, 1)
            for n, use in enumerate(USE["x1"]):
                wait_full(act, use)
                freed(fn(X[:, n, :], bank(use), ACT.Copy), use)
            for level in range(1, LEVELS):
                for n, use in enumerate(USE["p", level]):
                    wait_full(act, use)
                    freed(fn(BP[:, n, :], bank(use), ACT.Copy), use)
                if level < LEVELS - 1:
                    for n, use in enumerate(USE["t", level]):
                        wait_full(act, use)
                        freed(fn(XT[:, n, :], bank(use), ACT.Copy), use)
            act.wait_ge(ro_ms, 1)
            fn(ro_ss, ro_ss, ACT.Sqrt).then_inc(ro_sd, 1)
            for t, use in enumerate(USE["y_t"]):
                wait_full(act, use)
                freed(fn(yT[:, 0:4, t * P:(t + 1) * P], bank(use).rearrange("p (a b) -> p a b", a=NH), ACT.Copy), use)
            row_copy(0)
            split("ffn0", 0, range(3))
            post_stats(0)
            norm_stats(2)
            act.wait_ge(mod_ready, 2)
            norm_evac(2)
            row_copy(1)
            act.dma_start(tok_t[:, 1024:2048], c_bd_in).then_inc(late_loaded, 16)
            act.dma_start(arena[:, 15400:15912], glu_in).then_inc(late_loaded, 16)
            act.dma_start(brow[0:1, :], b_out_in).then_inc(brow_loaded, 16)
            ffn("ffn0", NF, ACT.Silu)
            post_stats(1)
            act.dma_start(arena[:, 12328:12840], b_in).then_inc(late_loaded, 16)
            norm_stats(3)
            act.wait_ge(mod_ready, 3)
            norm_evac(3)
            for c in range(8):
                use = USE["conf_i"][c]
                wait_full(act, use)
                if c >= 2:
                    wait_read(act, USE["conf_i"][c - 2])
                fn(csig[:, c % 2, :], bank(use)[:, T:2 * T], ACT.Sigmoid,
                   bias=col("conf_b_in")[:, 8 + c:9 + c]).then_inc(csig_ready, 1)
            for c, use in zip(CONV_PE, USE["conv31"]):
                wait_full(act, use)
                freed(fn(cc[:, c, :], bank(use)[:, 0:T], ACT.Identity, bias=col("conf_dw_b")[:, c:c + 1]), use)
            for k in range(KT):
                act.wait_ge(ln_x, k + 1)
                fn(csq[:, k, :], cc[:, k, :], ACT.Square).then_inc(csq_done, 1)
            wait_read(act, USE["ln"][1])
            fn(crs, crs, ACT.Sqrt).then_inc(ln_sd, 1)
            for k in range(KT):
                act.wait_ge(csq_ready, k + 1)
                fn(cout[:, k, :], csq[:, k, :], ACT.Silu, scale=col("conf_ln_g")[:, k:k + 1],
                   bias=col("conf_ln_b")[:, k:k + 1]).then_inc(conf_out, 1)
            fn(dt, col("log_dt"), ACT.Exp).then_inc(s5_mag, 1)
            act.wait_ge(s5_par, 1)
            fn(mag, s5_a, ACT.Exp).then_inc(s5_mag, 1)
            act.wait_ge(half_ready, 1)
            act.wait_ge(s5_arg, 1)
            fn(sin_h, phi, ACT.Sin, scale=PI).then_inc(s5_trig, 1)
            fn(cos_h, s5_b, ACT.Sin, scale=-PI, bias=halfpi[:, :]).then_inc(s5_trig, 1)
            act.wait_ge(s5_arg, 2)
            fn(trig_tmp[:, 2, :], trig_tmp[:, 0, :], ACT.Sin, scale=PI).then_inc(s5_trig, 1)
            fn(trig_tmp[:, 3, :], trig_tmp[:, 1, :], ACT.Sin, scale=-PI, bias=halfpi[:, :]).then_inc(s5_trig, 1)
            row_copy(2)
            act.wait_ge(bbar_ready, 1)
            split("ffn1", 0, range(3))
            post_stats(2)
            norm_stats(4)
            norm_evac(4)
            row_copy(3)
            ffn("ffn1", NF, ACT.Silu)
            post_stats(3)
            norm_stats(5)
            norm_evac(5)

            def projections():
                for name, b in BLOCKS3:
                    use = USE[name][b]
                    wait_full(act, use)
                    if name == "in_a":
                        last = fn((uT, q2T, k2T)[b // 4][:, b % 4, :], bank(use)[:, 0:T], ACT.Copy)
                    elif name == "in_v":
                        c, t = b // 2, b % 2
                        last = fn(v2[:, t, c * V2C:(c + 1) * V2C], bank(use)[:, 0:V2C], ACT.Copy)
                    elif name == "in_b":
                        last = fn(cin2[:, b, 2:T + 2], bank(use)[:, 0:T], ACT.Copy)
                    else:
                        last = fn(gT[:, b, :], bank(use)[:, 0:T], ACT.Identity, bias=col("b_gate_2")[:, b:b + 1])
                    freed(last, use)
                    yield
            filler = projections()
            for _ in range(4):
                next(filler)
            for n, use in enumerate(USE["b_bar"]):
                wait_full(act, use)
                freed(fn(bT[:, n, :, :].rearrange("p a b -> p (a b)"), bank(use), ACT.Copy), use)
            for i in range(S5T):
                for _ in range(BESIDE[i]):
                    next(filler)
                if i % 4 == 3:
                    next(filler)
                    blk = i // 4
                    wait_read(act, USE["s5_y"][blk])
                    fn(y_a[:, blk, :], y_a[:, blk, :], ACT.Gelu_apprx_tanh).then_inc(gelu_done, 1)
                    use = USE["glu"][blk]
                    wait_full(act, use)
                    freed(fn(glu_sig[:, blk % 2, :], bank(use)[:, 0:T], ACT.Sigmoid), use)
                if i == 11:
                    act.wait_ge(logf_in, 1)
                    ch(fn(lf_a, lf_a, ACT.Exp, scale=-1.0))
                    fn(lf_a, lf_a, ACT.Ln, bias=1.0).then_inc(logf_sp, 1)
            for n in range(NATT + 5):
                if n < NATT:
                    next(filler, None)
                    t = n % 2
                    act.wait_ge(fa_mx, n + 1)
                    if n >= 3:
                        wait_full(act, USE["fa_t"][n - 3])
                    width = (t + 1) * P
                    fn(fa_p[:, n % 3, 0:width], fa_p[:, n % 3, 0:width], ACT.Exp, bias=fa_max[:, n:n + 1],
                       accum_out=fa_sum[:, n:n + 1]).then_inc(fa_exp, 1)
                if 2 <= n < NATT + 2:
                    m = n - 2
                    a, t = m // 2, m % 2
                    use = USE["fa_t"][m]
                    wait_full(act, use)
                    if a >= 2:
                        if a % 2 == 0:
                            act.wait_ge(fa_half, a // 2)
                        else:
                            wait_full(act, USE["fa_o"][(a - 2) // 2])
                    freed(fn(fa_pT[:, a % 2, 0:t + 1, t * P:(t + 1) * P],
                             bank(use)[:, 0:(t + 1) * P].rearrange("p (a b) -> p a b", a=t + 1), ACT.Copy), use)
                if n >= 8 and (n - 8) % 4 == 0:
                    m = (n - 8) // 4
                    use = USE["fa_o"][m]
                    wait_full(act, use)
                    freed(fn(y_c[:, m, :], bank(use)[:, 0:T], ACT.Copy), use)
            for _ in filler:
                pass
            wait_read(act, USE["in_g"][23])
            for n in range(8):
                fn(gT[:, 3 * n:3 * n + 3, :], gT[:, 3 * n:3 * n + 3, :], ACT.Sigmoid).then_inc(gates_ready, 1)
            row_copy(4)
            act.wait_ge(merged, 8)
            split("ff", 0, range(2))
            post_stats(4)
            norm_stats(6)
            norm_evac(6)
            row_copy(5)
            ffn("ff", NF2, ACT.Relu)
            post_stats(5)

        @block.vector
        def _(dve):
            v = nc.vector
            tt, ts, stt = v.tensor_tensor, v.tensor_scalar, v.scalar_tensor_tensor
            ch = Chain(dve, dve_c)

            def mod(layer, vectors):
                if layer == 0:
                    dve.wait_ge(ring_used, len(MOD0_PE))
                    src = psum[:, 3584:3680].rearrange("p (n c) -> p n c", c=2)
                    dve.wait_ge(mod_mm, SUMS[0, NMOD - 1 if 5 in vectors else MOD_CTX - 2] + 1)
                b = col("b_mod")[:, 48 * layer:48 * layer + 48]
                m = modT[:, layer, :, :]
                early, late = 0 in vectors, 5 in vectors
                n0, n1 = 8 * vectors[0], 8 * vectors[-1] + 8
                if layer:
                    use = USE["mod1"][1]
                    wait_full(dve, use)
                    freed(tt(m[:, 24:48, 0], bank(use)[:, 0:24], b[:, 24:48], ALU.add), use)
                    wait_read(dve, use)
                else:
                    for c in range(2 if early else 1):
                        ch.mark(tt(m[:, n0:n1, c], src[:, n0:n1, c], b[:, n0:n1], ALU.add))
                ch.sync()
                gain = lambda name: col(name)[:, KT * layer:KT * layer + KT]
                todo = []
                if early:
                    todo.append((1 + 2 * layer, 0, "g_mix_pre", 0))
                    if layer == 0:
                        todo.append((0, 0, "g_mix_pre", 1))
                if late:
                    todo.append((2 + 2 * layer, 24, "g_ffn_pre", 0))
                for i, at, name, c in todo:
                    ch.mark(stt(ngain[:, i, :], m[:, at + 8:at + 16, c], 1.0, gain(name), ALU.add, ALU.mult))
                    ch.mark(v.tensor_copy(nshift[:, i, :], m[:, at:at + 8, c]))
                if late:
                    ch.mark(tt(pcol[:, 2 * layer, :], m[:, 16:24, 0], gain("g_mix_post"), ALU.mult))
                    ch.mark(tt(pcol[:, 2 * layer + 1, :], m[:, 40:48, 0], gain("g_ffn_post"), ALU.mult))
                if layer == 0 and late:
                    for i, name in ((5, "g_pre_mix_2"), (6, "g_pre_mlp_2")):
                        ch.mark(v.tensor_copy(ngain[:, i, :], col(name)))
                        ch.mark(v.memset(nshift[:, i, :], 0.0))
                    for p, name in ((4, "g_post_mix_2"), (5, "g_post_mlp_2")):
                        ch.mark(v.tensor_copy(pcol[:, p, :], col(name)))
                ch.sync()
                v.memset(vtick[:, :], 0.0).then_inc(mod_ready, 1)

            def mod_sums(layer, j):
                for _ in mod_steps(layer, j):
                    pass

            def mod_steps(layer, j):
                n = SUMS[layer, j]
                if layer:
                    chunk = slot(j % 2)
                    dve.wait_ge(mod1_loaded[j % 2], 16 * (j // 2 + 1))
                    if j == 0:
                        dve.wait_ge(sums_ready, n)
                    todo = [(macs1[:, j * MOD_C:(j + 1) * MOD_C], 0, MOD_C)]
                else:
                    c = CHUNK["mod0", j]
                    chunk = slot(c)
                    dve.wait_ge(ring_ready[c % SLOTS], 16 * (c // SLOTS + 1))
                    todo = [(macs[:, n % 4, :], 0, MOD_C)]
                    if n >= 4:
                        dve.wait_ge(mod_mm, n - 3)
                    if j < MOD_CTX:
                        todo.insert(0, (macs_ctx[:, n % 2, :], 1, MOD_C))
                        if n >= 2:
                            dve.wait_ge(mod_mm, n - 1)
                for k in range(KT):
                    if k:
                        dve.wait_ge(mac, mac_n[0])
                    for n, (dst, which, width) in enumerate(todo):
                        part = chunk[:, k * MOD_C:(k + 1) * MOD_C]
                        value = cond[:, 2 * k + which:2 * k + which + 1]
                        if k == 0:
                            ins = ts(dst, part, value, None, ALU.mult)
                        else:
                            ins = stt(dst, part, value, dst, ALU.mult, ALU.add)
                        if (k, n) == (KT - 1, len(todo) - 1):
                            ins.then_inc(sums_ready, 1)
                        else:
                            ins.then_inc(mac, 1)
                            mac_n[0] += 1
                    yield

            mac_n = [0]

            def mean_eps(out, src, n):
                return ts(out, src, 1.0 / n, EPS, ALU.mult, ALU.add)

            def norm_scale(i):
                dve.wait_ge(norm_ss, 2 * (i + 1))
                mean_eps(nms[:, 2 * i:2 * i + 2], nss[:, 2 * i:2 * i + 2], D).then_inc(norm_ms, 1)
                dve.wait_ge(norm_sd, i + 1)
                ch(v.reciprocal(nrs[:, 2 * i:2 * i + 2], nsd[:, 2 * i:2 * i + 2]))
                src, dst = (ybuf, ybuf) if i == 0 else (h, nrm)
                if i == 1:
                    dve.wait_ge(x_loaded, 16)
                for t in range(TT):
                    ts(dst[:, t, :], src[:, t, :], nrs[:, 2 * i + t:2 * i + t + 1], None, ALU.mult).then_inc(norm_x, 1)

            def norm_evac(i):
                at = T if i == 0 else 0
                for kp in (0, 2):
                    use = USE[f"norm{i}"][kp]
                    wait_full(dve, use)
                    for j in range(2):
                        k = 2 * kp + j
                        dst = yT[:, k, :] if i in (2, 4, 6) else aT[:, k, at:at + T]
                        last = ts(dst, bank(use)[:, j * T:(j + 1) * T],
                                  ngain[:, i, k:k + 1], nshift[:, i, k:k + 1], ALU.mult, ALU.add)
                    freed(last, use)
                if i in (2, 4, 6):
                    pair = lambda x, kp: x[:, 2 * kp:2 * kp + 2, :]
                    for kp in (0, 2):
                        wait_read(dve, USE[f"norm{i}"][kp])
                        ch.mark(v.tensor_copy(pair(x_hi, kp), pair(yT, kp)))
                    ch.sync()
                    for n, kp in enumerate((0, 2, 1, 3)):
                        if n >= 2:
                            dve.wait_ge(x_rounded, i - 2 + n - 1)
                        tt(pair(x_lo, kp), pair(yT, kp), pair(x_hi, kp).bitcast(F32), ALU.subtract).then_inc(x_split, 1)

            def row_diag(p):
                if p:
                    wait_full(dve, USE["row", p - 1][1])
                tt(view(diag, 0, KT, P), bc_out(ident, KT), bc_in(pcol[:, p, :], P), ALU.mult).then_inc(diag_ready, 1)

            def post(p):
                dve.wait_ge(post_ss, 2 * (p + 1))
                mean_eps(pms[:, 2 * p:2 * p + 2], pss[:, 2 * p:2 * p + 2], D).then_inc(post_ms, 1)
                dve.wait_ge(post_sd, p + 1)
                ch(v.reciprocal(prs[:, 2 * p:2 * p + 2], psd[:, 2 * p:2 * p + 2]))
                for use in USE["row", p]:
                    wait_read(dve, use)
                use = USE["y", p][0]
                for t in range(TT):
                    last = stt(ybuf[:, t, :], Y[:, t, :], prs[:, 2 * p + t:2 * p + t + 1], rowbc[:, :], ALU.mult, ALU.mult)
                    if t == 0:
                        ch(last)
                    else:
                        freed(last, use)
                        wait_read(dve, use)
                    tt(h[:, t, :], h[:, t, :], ybuf[:, t, :], ALU.add).then_inc(h_ready, 1)

            def split(name, j, todo, i=0):
                (parts, before, _), c = FFNS[name], CHUNK[name, j]
                for part in todo:
                    dve.wait_ge(split_hi, before + parts * j + part + 1 + SLOTS * parts * i)
                    at = slice(part * D, part * D + D)
                    tt(w_lo[j % 2][:, at], slot(c)[:, at], w_hi[j % 2][:, at].bitcast(F32), ALU.subtract).then_inc(split_ready, 1)

            def ffn(name, n, base, second):
                uses, (parts, _, used) = USE[name], FFNS[name]

                def one(j, i=0):
                    if j + 1 < n:
                        split(name, j + 1, range(parts - 1), i)
                    dve.wait_ge(act_on, base + j + 1 + SLOTS * i)
                    if j:
                        dve.wait_ge(bank_free[uses[j - 1][0]], uses[j - 1][1] + 1 + i)
                    step = 2 * (base + j) + 2 * SLOTS * i
                    tt(h_tmp, sg[:, j % 2, :], bank(uses[j])[:, second:second + T], ALU.mult).then_inc(h_step, 1)
                    if j >= 2:
                        dve.wait_ge(block_used, used + j - 1 + SLOTS * i)
                    dve.wait_ge(h_step, step + 1)
                    v.tensor_copy(h_hi[:, j % 2, :], h_tmp).then_inc(h_step, 1)
                    dve.wait_ge(h_step, step + 2)
                    freed(tt(h_lo[:, j % 2, :], h_tmp, h_hi[:, j % 2, :].bitcast(F32), ALU.subtract), uses[j])
                    if j + 1 < n:
                        split(name, j + 1, [parts - 1], i)

                for j in range(2):
                    one(j)
                turns = (n - 3) // SLOTS
                with dve.Fori(0, turns) as i:
                    for q in range(SLOTS):
                        one(2 + q, i)
                for j in range(2 + SLOTS * turns, n):
                    one(j)

            v.memset(zeros[:, :], 0.0).then_inc(zeros_ready, 1)
            dve.wait_ge(cols_loaded, 16)
            dve.wait_ge(cond_ready, 1)
            first = [j for j in range(MOD_CTX) if j not in MOD0_PE]
            mod_sums(0, first[0])
            dve.wait_ge(ctx_loaded, 16)
            norm_scale(0)
            norm_scale(1)
            for j in first[1:]:
                mod_sums(0, j)
            mod(0, (0, 1))
            dve.wait_ge(consts_loaded, 16)
            norm_evac(0)
            norm_evac(1)
            for j in range(MOD_CTX, MOD_CTX + 4):
                mod_sums(0, j)
            taps = col("hyb_conv").rearrange("p (b k) -> p b k", k=CONV_A)
            for grp in range(3):
                n = 2 if grp < 2 else 1
                for b in range(4 * grp, 4 * grp + 4):
                    wait_read(dve, USE["hyb_f"][b])
                    ch.mark(ts(cv[:, b, 0:n, :], cin[:, b, 0:n, 0:T], taps[:, b, 0:1], None, ALU.mult))
                for k in range(1, CONV_A):
                    ch.sync()
                    for b in range(4 * grp, 4 * grp + 4):
                        last = stt(cv[:, b, 0:n, :], cin[:, b, 0:n, k:k + T], taps[:, b, k:k + 1], cv[:, b, 0:n, :], ALU.mult, ALU.add)
                        if k < CONV_A - 1:
                            ch.mark(last)
                last.then_inc(conv_done, 1)
                for j in range(MOD_CTX + 4 + 2 * grp, MOD_CTX + 6 + 2 * grp):
                    mod_sums(0, j)
            dve.wait_ge(att_sq_ready, 4)
            ch.mark(v.reduce_sum(att_ss[:, 0:20], att_sq[:, 0:1280].rearrange("p (a b) -> p a b", b=AHD), axis=AXX))
            ch.mark(v.reduce_sum(att_ss[:, 20:24], att_sq[:, 1280:1536].rearrange("p (a b) -> p a b", b=AHD), axis=AXX))
            ch.sync()
            mean_eps(att_ss, att_ss, AHD).then_inc(att_ms, 1)
            dve.wait_ge(att_sd, 1)
            v.reciprocal(att_r, att_ss).then_inc(att_rs, 1)
            mod(0, (2, 3, 4, 5))
            for j in range(3):
                mod_sums(1, j)

            def att_scale(n):
                wait_read(dve, USE["att_s"][n])
                ch(v.reciprocal(att_inv[:, n:n + 1], att_sum[:, n:n + 1]))
                ts(att_p[:, n % 3, :], att_p[:, n % 3, :], att_inv[:, n:n + 1], None, ALU.mult).then_inc(att_norm, 1)

            for n in range(NATT):
                use = USE["att_s"][n]
                wait_full(dve, use)
                ch(v.reduce_max(att_max[:, n:n + 1], bank(use), axis=AXX))
                ts(att_max[:, n:n + 1], att_max[:, n:n + 1], -(AHD ** -0.5), None, ALU.mult).then_inc(att_mx, 1)
                if n:
                    att_scale(n - 1)
            att_scale(NATT - 1)
            for n in range(6):
                dve.wait_ge(kq_sq, n + 1)
                ch.mark(v.reduce_sum(kq_ss[:, 4 * n:4 * n + 4], sq_kq[:, n, :].rearrange("p (a b) -> p a b", a=NH), axis=AXX))
            ch.sync()
            ts(kq_ss, kq_ss, EPS, None, ALU.add).then_inc(kq_ms, 1)
            dve.wait_ge(kq_sd, 1)
            ch(v.reciprocal(kq_r, kq_ss))
            ch(ts(kq_r[:, 16:24], kq_r[:, 16:24], HD ** -0.5, None, ALU.mult))
            for n in range(6):
                use = USE["to_tok"][n]
                dst = ktok[:, n, :] if n < 4 else qtok[:, n - 4, :]
                freed(tt(dst.rearrange("p (a b) -> p a b", a=NH), bank(use).rearrange("p (a b) -> p a b", a=NH),
                         bc_in(kq_r[:, 4 * n:4 * n + 4], P), ALU.mult), use)
            dve.wait_ge(ba_ready, 4)
            dve.wait_ge(rows_loaded, 16)
            z, za = (x.rearrange("p (s e) -> p s e", s=4) for x in (g_b, g_a))
            ch(tt(z, ba[:, :, 8:16], bc_out(row("dt_bias"), 4), ALU.add))
            stt(za, z, -1.0, z, ALU.mult, ALU.max).then_inc(sp_in, 1)
            dve.wait_ge(sp_ready, 2)
            ch(stt(g_b, g_b, 0.0, g_a, ALU.max, ALU.add))
            ch(tt(g, z, bc_out(na8, 4), ALU.mult))
            ts(g_t, g_t, -1.0, None, ALU.mult).then_inc(g_ready, 1)
            use = USE["gates"]
            wait_full(dve, use)
            for d in range(2):
                last = ts(ngc[:, :, 4 * d:4 * d + 4], bank(use)[:, 16 * d:16 * d + 16].rearrange("p (s e) -> p s e", s=4),
                          -1.0, None, ALU.mult)
            last.then_inc(dsum, 1)
            dve.wait_ge(dsum, 1)
            quad = lambda x: x.rearrange("p (a b) -> p a b", a=NH)
            steps = mod_steps(1, 3)
            for n, use in enumerate(USE["decay"]):
                d, st = n // 4, n % 4
                wait_full(dve, use)
                next(steps)
                freed(tt(quad(UT[:, n, :]), quad(bank(use)), bc_in(ngc[:, st, 4 * d:4 * d + 4], P), ALU.add), use)
            for t, use in enumerate(USE["kq"]):
                wait_full(dve, use)
                for d in range(2):
                    dve.wait_ge(dec_ready, 4 * d + t + 1)
                    last = tt(intraT[:, 2 * d + t, :], bank(use), UT[:, 4 * d + t, :], ALU.mult)
                freed(last, use)
            for st, use in enumerate(USE["kk"]):
                wait_full(dve, use)
                dve.wait_ge(dec_ready, 8)
                tt(UT[:, st, :], bank(use), UT[:, st, :], ALU.mult).then_inc(ut_part, 1)
                freed(tt(UT[:, 4 + st, :], bank(use), UT[:, 4 + st, :], ALU.mult), use)
            for n in range(8):
                d, st = n // 4, n % 4
                dve.wait_ge(ut_ready, 2 * st + d + 1)
                ch(tt(quad(XT[:, n, :]), quad(UT[:, n, :]), bc_out(levels[:, d, 0, :], NH), ALU.mult))
                tt(quad(XT[:, n, :]), bc_out(ident, NH), quad(XT[:, n, :]), ALU.subtract).then_inc(xt_first, 1)
            for level in range(1, LEVELS):
                dst = X if level < LEVELS - 1 else XT
                steps = mod_steps(1, 2 * level + 2)
                for n, use in enumerate(USE["q", level]):
                    next(steps)
                    wait_full(dve, use)
                    freed(tt(dst[:, n, :], dst[:, n, :], bank(use), ALU.subtract), use)
                mod_sums(1, 2 * level + 3)
            row_diag(0)
            wait_read(dve, USE["gates"])
            for s in range(4):
                for d in range(2):
                    st = ORDER[d][s]
                    if s == 0:
                        v.tensor_copy(r_st[:, d, :], vtok[:, st, :]).then_inc(resid_ready, 1)
                        continue
                    use = USE["ks", s, d]
                    wait_full(dve, use)
                    freed(tt(quad(tmp_st[:, d, :]), quad(bank(use)), bc_in(eg[:, st, 4 * d:4 * d + 4], P), ALU.mult), use)
                    wait_read(dve, use)
                    tt(r_st[:, d, :], vtok[:, st, :], tmp_st[:, d, :], ALU.subtract).then_inc(resid_ready, 1)
                for d in range(2):
                    st = ORDER[d][s]
                    use = USE["vn", s, d]
                    wait_full(dve, use)
                    freed(tt(quad(vn_st[:, d, :]), quad(bank(use)), bc_in(beta[:, st, 4 * d:4 * d + 4], P), ALU.mult), use)
                    if 0 < s < 3:
                        ch.mark(tt(quad(S[:, d, :]), quad(S[:, d, :]), bc_in(etot[:, st, 4 * d:4 * d + 4], P), ALU.mult))
                for d in range(2):
                    if s < 3:
                        use = USE["ds", s, d]
                        wait_full(dve, use)
                        if s == 0:
                            freed(v.tensor_copy(S[:, d, :], bank(use)), use)
                        else:
                            ch.sync()
                            freed(tt(S[:, d, :], S[:, d, :], bank(use), ALU.add), use)
                if s == 1:
                    use = USE["mod1"][0]
                    wait_full(dve, use)
                    freed(tt(modT[:, 1, 0:24, 0], bank(use)[:, 0:24], col("b_mod")[:, 48:72], ALU.add), use)
                for d in range(2):
                    st = ORDER[d][s]
                    if s >= 2:
                        use = USE["os", s, d]
                        wait_full(dve, use)
                        dst = o_sum[:, st, :] if s == 2 else tmp_st[:, d, :]
                        freed(tt(quad(dst), quad(bank(use)), bc_in(eg[:, st, 4 * d:4 * d + 4], P), ALU.mult), use)
                        wait_read(dve, use)
                        if s == 3:
                            ch(tt(o_sum[:, st, :], o_sum[:, st, :], tmp_st[:, d, :], ALU.add))
                        use = USE["oi", s, d]
                        wait_full(dve, use)
                        freed(tt(o_sum[:, st, :], o_sum[:, st, :], bank(use), ALU.add), use)
                        wait_read(dve, use)
            ch(tt(r_st, o_sum, o_sum, ALU.mult))
            ch(v.reduce_sum(ro_ss, r_st.rearrange("p t (a b) -> p (t a) b", a=NH), axis=AXX))
            mean_eps(ro_ss, ro_ss, HD).then_inc(ro_ms, 1)
            dve.wait_ge(ro_sd, 1)
            ch(v.reciprocal(ro_r, ro_ss))
            dve.wait_ge(zgate_ready, 2)
            for t in range(TT):
                ch(tt(quad(ymix[:, t, :]), quad(o_sum[:, t, :]), bc_in(ro_r[:, 4 * t:4 * t + 4], P), ALU.mult))
                ch(tt(quad(ymix[:, t, :]), quad(ymix[:, t, :]), bc_out(row("out_norm"), NH), ALU.mult))
                tt(ymix[:, t, :], ymix[:, t, :], zgate[:, t, :], ALU.mult).then_inc(y_mixed, 1)
            mod(1, (0, 1, 2, 3, 4, 5))
            split("ffn0", 0, range(3))
            post(0)
            norm_scale(2)
            row_diag(1)
            norm_evac(2)
            ffn("ffn0", NF, 0, T)
            post(1)
            norm_scale(3)
            norm_evac(3)
            row_diag(2)
            dve.wait_ge(margins, 2)
            dww = col("conf_dw_w").rearrange("p (b k) -> p b k", k=CONF_K)

            def glu_in(c):
                use = USE["conf_i"][c]
                dve.wait_ge(csig_ready, c + 1)
                freed(stt(cu[:, c, 15:15 + T], bank(use)[:, 0:T], col("conf_b_in")[:, c:c + 1], csig[:, c % 2, :],
                          ALU.add, ALU.mult), use)

            own = [c for c in range(KT) if c not in CONV_PE]
            ahead = iter(range(2, KT))
            glu_in(0)
            glu_in(1)
            for group in (own[:2], own[2:]):
                for c in group:
                    wait_read(dve, USE["conf_i"][c])
                    ch.mark(ts(cc[:, c, :], cu[:, c, 0:T], dww[:, c, 0:1], col("conf_dw_b")[:, c:c + 1], ALU.mult, ALU.add))
                for k in range(1, CONF_K):
                    ch.sync()
                    for c in group:
                        last = stt(cc[:, c, :], cu[:, c, k:k + T], dww[:, c, k:k + 1], cc[:, c, :], ALU.mult, ALU.add)
                        if k < CONF_K - 1:
                            ch.mark(last)
                        else:
                            last.then_inc(conv31, 1)
                    if k % 7 == 0:
                        for c in ahead:
                            glu_in(c)
                            break
            use = USE["ln"][0]
            wait_full(dve, use)
            freed(ts(crs, bank(use)[:, 0:T], 1.0 / D, None, ALU.mult), use)
            wait_read(dve, use)
            for k in range(KT):
                tt(cc[:, k, :], cc[:, k, :], crs, ALU.subtract).then_inc(ln_x, 1)
            use = USE["ln"][1]
            wait_full(dve, use)
            freed(mean_eps(crs, bank(use)[:, 0:T], D), use)
            dve.wait_ge(ln_sd, 1)
            ch(v.reciprocal(crs, crs))
            for k in range(KT):
                tt(csq[:, k, :], cc[:, k, :], crs, ALU.mult).then_inc(csq_ready, 1)
            dve.wait_ge(s5_mag, 1)
            ch(ts(lam_re, col("a_re"), -1e-4, None, ALU.min))
            ch.mark(tt(theta, col("a_im"), dt, ALU.mult))
            tt(s5_a, lam_re, dt, ALU.mult).then_inc(s5_par, 1)
            ch.sync()
            ch(ts(rk, theta, 1 / TWO_PI, ROUND, ALU.mult, ALU.add))
            ch(ts(rk, rk, -ROUND, None, ALU.add))
            for part in TWO_PI_PARTS:
                ch(stt(theta, rk, -part, theta, ALU.mult, ALU.add))
            ch(ts(phi, theta, 1 / TWO_PI, None, ALU.mult))
            ch(ts(phi_hi, phi, ROUND / 4096, None, ALU.add))
            ch(ts(phi_hi, phi_hi, -ROUND / 4096, None, ALU.add))
            ch.mark(tt(phi_lo, phi, phi_hi, ALU.subtract))
            stt(s5_b, phi, -1.0, phi, ALU.mult, ALU.max).then_inc(s5_arg, 1)
            ch.sync()
            grid = lambda x: x.rearrange("p (i t) -> p i t", i=S5T)
            tv = bc_out(const("tvec"), S5T)
            f0, f1, f4, f5 = trig_tmp[:, 0, :], trig_tmp[:, 1, :], trig_tmp[:, 4, :], trig_tmp[:, 5, :]
            dve.wait_ge(late_loaded, 48)
            ch.mark(tt(grid(f0), tv, bc_in(phi_hi, 32), ALU.mult))
            ch.mark(tt(grid(f4), tv, bc_in(phi_lo, 32), ALU.mult))
            ch.sync()
            ch(ts(f5, f0, ROUND, None, ALU.add))
            ch(ts(f5, f5, -ROUND, None, ALU.add))
            ch(tt(f0, f0, f5, ALU.subtract))
            ch(tt(f0, f0, f4, ALU.add))
            stt(f1, f0, -1.0, f0, ALU.mult, ALU.max).then_inc(s5_arg, 1)
            dve.wait_ge(s5_trig, 2)
            dve.wait_ge(s5_mag, 2)
            ch.mark(stt(sin_t1, sin_h, 2.0, cos_h, ALU.mult, ALU.mult))
            ch.mark(stt(cos_t1, sin_h, -2.0, sin_h, ALU.mult, ALU.mult))
            ch.mark(tt(den, lam_re, lam_re, ALU.mult))
            ch.mark(tt(s5_c, col("a_im"), col("a_im"), ALU.mult))
            ch.sync()
            ch.mark(ts(cos_t1, cos_t1, 1.0, None, ALU.add))
            ch.mark(tt(den, den, s5_c, ALU.add))
            ch.mark(tt(num_im, mag, sin_t1, ALU.mult))
            ch.sync()
            ch.mark(tt(num_re, mag, cos_t1, ALU.mult))
            ch.mark(v.reciprocal(den, den))
            ch.sync()
            ch(ts(num_re, num_re, -1.0, None, ALU.add))
            ch.mark(tt(co_re, num_re, lam_re, ALU.mult))
            ch.mark(tt(s5_c, num_im, col("a_im"), ALU.mult))
            ch.mark(tt(co_im, num_im, lam_re, ALU.mult))
            ch.mark(tt(s5_b, num_re, col("a_im"), ALU.mult))
            ch.sync()
            ch.mark(tt(co_re, co_re, s5_c, ALU.add))
            ch.mark(tt(co_im, co_im, s5_b, ALU.subtract))
            ch.sync()
            ch.mark(tt(co_re, co_re, den, ALU.mult))
            ch.mark(tt(co_im, co_im, den, ALU.mult))
            ch.sync()
            hg = lambda x: x.rearrange("p (i e) -> p i e", i=S5T)
            br, bi = bc_arr[:, 0, :], bc_arr[:, 1, :]
            w0, w1, w2, w3 = f4[:, 0:256], f4[:, 256:512], f5[:, 0:256], f5[:, 256:512]
            ch.mark(tt(hg(w0), hg(br), bc_in(co_re, 16), ALU.mult))
            ch.mark(tt(hg(w1), hg(bi), bc_in(co_im, 16), ALU.mult))
            ch.mark(tt(hg(w2), hg(bi), bc_in(co_re, 16), ALU.mult))
            ch.mark(tt(hg(w3), hg(br), bc_in(co_im, 16), ALU.mult))
            ch.sync()
            dve.wait_ge(margins, 2)
            for g2 in range(2):
                r = slice(64 * g2, 64 * g2 + 64)
                for part, (x, y, op) in enumerate(((w0, w1, ALU.subtract), (w2, w3, ALU.add))):
                    dst = bbd[r, part, :, :].rearrange("p a (q g e) -> p (a q) g e", q=4, g=2)[:, :, g2, :]
                    ch.mark(tt(dst, hg(x)[r], hg(y)[r], op))
            dve.wait_ge(s5_trig, 4)
            f2, f3 = trig_tmp[:, 2, :], trig_tmp[:, 3, :]
            ch.mark(stt(small_trig[:, 1, :, :].rearrange("p i t -> p (i t)"), f2, 2.0, f3, ALU.mult, ALU.mult))
            ch(stt(small_trig[:, 0, :, :].rearrange("p i t -> p (i t)"), f2, -2.0, f2, ALU.mult, ALU.mult))
            ch(ts(small_trig[:, 0, :, :], small_trig[:, 0, :, :], 1.0, None, ALU.add))
            v.memset(vtick[:, :], 0.0).then_inc(bbar_ready, 1)
            split("ffn1", 0, range(3))
            post(2)
            norm_scale(4)
            norm_evac(4)
            row_diag(3)
            ffn("ffn1", NF, NF, T)
            post(3)
            norm_scale(5)
            norm_evac(5)
            def forget(step):
                if step == 0:
                    for use in USE["in_v"][2:4]:
                        wait_read(dve, use)
                    ch(tt(lf_z, v2[:, :, 512:520], bc_out(row("b_f"), TT), ALU.add))
                    stt(lf_a, lf_z, -1.0, lf_z, ALU.mult, ALU.max).then_inc(logf_in, 1)
                elif step == 1:
                    dve.wait_ge(logf_sp, 1)
                    stt(logf, lf_z, 0.0, lf_a, ALU.min, ALU.subtract).then_inc(logf_ready, 1)
                elif step == 2:
                    use = USE["cum"]
                    wait_full(dve, use)
                    freed(v.tensor_copy(cumq, bank(use)[:, 0:16].rearrange("p (t e) -> p t e", t=TT)), use)
                    wait_read(dve, use)
                    keys_diag(0)
                    keys_diag(1)
                else:
                    for n in ((0, 1) if step == 3 else (2, 3)):
                        kt, h0 = n // 2, 4 * (n % 2)
                        use = USE["cum_k"][n]
                        wait_full(dve, use)
                        b3 = quad(bank(use))
                        if kt == 0:
                            ch.mark(tt(ck0[:, h0:h0 + 4, :], b3, bc_in(cumq[:, 0, h0:h0 + 4], P), ALU.subtract))
                        freed(tt(ck1[:, h0:h0 + 4, kt * P:(kt + 1) * P], b3, bc_in(cumq[:, 1, h0:h0 + 4], P), ALU.subtract), use)
                        if step == 3:
                            keys_diag(n + 2)

            def keys_diag(n):
                kt, h0 = n // 2, 4 * (n % 2)
                tt(quad(cdiag[:, n % 2, :]), bc_out(ident, 4), bc_in(cumq[:, kt, h0:h0 + 4], P), ALU.mult).then_inc(cdiag_ready, 1)

            for i in range(S5T):
                use = USE["s5_u"][i]
                dve.wait_ge(s5_tab, i + 1)
                if i:
                    dve.wait_ge(s5_state, i)
                wait_full(dve, use)
                two = lambda x: x.rearrange("p (c t) -> p c t", c=2)
                ch.mark(tt(two(s5_m1), two(bank(use)), bc_out(etab[:, i % 2, 0, :], 2), ALU.mult))
                freed(tt(two(s5_m2), two(bank(use)), bc_out(etab[:, i % 2, 1, :], 2), ALU.mult), use)
                ch.sync()
                wait_read(dve, use)
                ch.mark(tt(s5_wt[:, 0:T], s5_m1[:, 0:T], s5_m2[:, T:2 * T], ALU.add))
                ch(tt(s5_wt[:, T:2 * T], s5_m1[:, T:2 * T], s5_m2[:, 0:T], ALU.subtract))
                r = mag[:, i:i + 1].to_broadcast([P, T])
                for part in range(2):
                    ch.mark(v.tensor_tensor_scan(s5_zt[:, part * T:(part + 1) * T], r, s5_wt[:, part * T:(part + 1) * T],
                                                 0.0, ALU.mult, ALU.add))
                ch.sync()
                ch.mark(tt(two(s5_n1), two(s5_zt), bc_out(etab[:, i % 2, 0, :], 2), ALU.mult))
                tt(two(s5_n2), two(s5_zt), bc_out(etab[:, i % 2, 1, :], 2), ALU.mult).then_inc(s5_n, 1)
                ch.sync()
                dve.wait_ge(s5_n, i + 1)
                if i >= 2:
                    if (i - 2) % 4 == 3:
                        wait_full(dve, USE["s5_y"][(i - 2) // 4])
                    else:
                        dve.wait_ge(s5_part, (i - 2) + 1 - (i - 2) // 4)
                ch.mark(tt(s_ri[:, i % 2, 0, :], s5_n1[:, 0:T], s5_n2[:, T:2 * T], ALU.subtract))
                stt(s_ri[:, i % 2, 1, :], s5_n1[:, T:2 * T], -1.0, s5_n2[:, 0:T], ALU.mult, ALU.subtract).then_inc(s5_state, 1)
                if i % 4 == 3:
                    blk = i // 4
                    use = USE["s5_y"][blk]
                    wait_full(dve, use)
                    freed(stt(y_a[:, blk, :], uT[:, blk, :], col("s5_d")[:, blk:blk + 1], bank(use)[:, 0:T], ALU.mult, ALU.add), use)
                    use = USE["glu"][blk]
                    wait_read(dve, use)
                    tt(y_a[:, blk, :], y_a[:, blk, :], glu_sig[:, blk % 2, :], ALU.mult).then_inc(ya_done, 1)
                if i >= 11:
                    forget(i - 11)

            def fa_scale(n):
                width = (n % 2 + 1) * P
                dve.wait_ge(fa_exp, n + 1)
                ch(v.reciprocal(fa_inv[:, n:n + 1], fa_sum[:, n:n + 1]))
                ts(fa_p[:, n % 3, 0:width], fa_p[:, n % 3, 0:width], fa_inv[:, n:n + 1], None, ALU.mult).then_inc(fa_norm, 1)

            dve.wait_ge(masked, 4)
            for n in range(NATT):
                a, t = n // 2, n % 2
                width = (t + 1) * P
                use = USE["fa_s"][n]
                wait_full(dve, use)
                if n >= 3:
                    wait_full(dve, USE["fa_t"][n - 3])
                bias = ck1[:, a, :] if t else ck0[:, a, :]
                freed(stt(fa_p[:, n % 3, 0:width], bank(use)[:, 0:width], AHD ** -0.5, bias, ALU.mult, ALU.subtract), use)
                wait_read(dve, use)
                ch(v.reduce_max(fa_max[:, n:n + 1], fa_p[:, n % 3, 0:width], axis=AXX))
                ts(fa_max[:, n:n + 1], fa_max[:, n:n + 1], -1.0, None, ALU.mult).then_inc(fa_mx, 1)
                if n:
                    fa_scale(n - 1)
            fa_scale(NATT - 1)
            dve.wait_ge(margins, 3)
            for use in USE["in_b"]:
                wait_read(dve, use)
            cw = col("conv_w_2").rearrange("p (b k) -> p b k", k=3)
            for b in range(4):
                ch.mark(tt(cin2[:, b, 2:T + 2], cin2[:, b, 2:T + 2], cin2[:, 8 + b, 2:T + 2], ALU.mult))
            ch.sync()
            for b in range(4):
                ch.mark(ts(y_b[:, b, :], cin2[:, b, 0:T], cw[:, b, 0:1], None, ALU.mult))
            for k in (1, 2):
                ch.sync()
                for b in range(4):
                    ch.mark(stt(y_b[:, b, :], cin2[:, b, k:k + T], cw[:, b, k:k + 1], y_b[:, b, :], ALU.mult, ALU.add))
            ch.sync()
            for b in range(4):
                tt(y_b[:, b, :], y_b[:, b, :], cin2[:, 4 + b, 2:T + 2], ALU.mult).then_inc(yb_done, 1)
            row_diag(4)
            for j in range(8):
                m_a, m_b = m_ab[:, j % 2, :], m_c[:, j % 2, :]
                if j >= 2:
                    dve.wait_ge(merged, j - 1)
                dve.wait_ge(gates_ready, j + 1)
                u0, u1 = USE["branch"][2 * j], USE["branch"][2 * j + 1]
                wait_full(dve, u0)
                freed(tt(m_a, bank(u0), gT[:, 3 * j:3 * j + 2, :].rearrange("p a t -> p (a t)"), ALU.mult), u0)
                wait_full(dve, u1)
                freed(tt(m_b, bank(u1)[:, 0:T], gT[:, 3 * j + 2, :], ALU.mult), u1)
                wait_read(dve, u0)
                ch(tt(m_a[:, 0:T], m_a[:, 0:T], m_a[:, T:2 * T], ALU.add))
                wait_read(dve, u1)
                tt(mT[:, j, :], m_a[:, 0:T], m_b, ALU.add).then_inc(merged, 1)
            split("ff", 0, range(2))
            post(4)
            norm_scale(6)
            norm_evac(6)
            row_diag(5)
            ffn("ff", NF2, 2 * NF, 0)
            post(5)

        @block.gpsimd
        def _(pool):
            gp = nc.gpsimd
            tt = gp.tensor_tensor
            ch = Chain(pool, pool_c)
            quad = lambda x: x.rearrange("p (a b) -> p a b", a=NH)

            cin24 = cin.rearrange("p b s t -> p (b s) t")
            ch.mark(gp.memset(cin24[:, :, 0:2], 0.0))
            ch.mark(gp.memset(cin24[:, :, T + 2:T + 4], 0.0))
            gp.memset(halfpi[:, :], HALF_PI).then_inc(half_ready, 1)
            ch.sync()
            gp.memset(tick[:, :], 0.0).then_inc(margins, 1)
            for use in USE["hyb_t"][6:10]:
                wait_read(pool, use)
            for st in range(4):
                src = ptok[:, st, 768:784] if st < 2 else pctx[:, st - 2, 256:272]
                gp.tensor_copy(ba[:, st, :], src).then_inc(ba_ready, 1)
            for use in USE["hyb_t"][0:6]:
                wait_read(pool, use)
            for t in range(TT):
                pool.wait_ge(conv_done, 3)
                x = ptok[:, t, 0:640]
                tt(att_sq[:, 640 * t:640 * t + 640], x, x, ALU.mult).then_inc(att_sq_ready, 1)
            for t in range(TT):
                x = pctx[:, t, 0:128]
                tt(att_sq[:, 1280 + 128 * t:1408 + 128 * t], x, x, ALU.mult).then_inc(att_sq_ready, 1)
            pool.wait_ge(att_rs, 1)
            pool.wait_ge(rows_loaded, 16)
            heads = lambda x: x.rearrange("p (a b) -> p a b", b=AHD)
            for t in range(TT):
                ch.mark(tt(heads(qk[:, t, :]), heads(ptok[:, t, 0:640]), bc_in(att_r[:, 10 * t:10 * t + 10], AHD), ALU.mult))
                ch.mark(tt(heads(kctx[:, t, :]), heads(pctx[:, t, 0:128]), bc_in(att_r[:, 20 + 2 * t:22 + 2 * t], AHD), ALU.mult))
            ch.sync()
            for t in range(TT):
                ch.mark(tt(qk[:, t, :], qk[:, t, :], row("qk_norm"), ALU.mult))
                ch.mark(tt(kctx[:, t, :], kctx[:, t, :], row("qk_norm")[:, 512:640], ALU.mult))
            ch.sync()
            halves = lambda x: x.rearrange("p (a b c d) -> p a b c d", a=10, b=2, c=2)
            for t in range(TT):
                ch.mark(tt(heads(rot_a[:, t, :]), heads(qk[:, t, :]), bc_out(cos_t[:, t, :], 10), ALU.mult))
                for c in range(2):
                    s4 = sin_t[:, t, :].rearrange("p (b c d) -> p b c d", b=2, c=2)[:, :, c, :]
                    ch.mark(tt(halves(rot_b[:, t, :])[:, :, :, c, :], halves(qk[:, t, :])[:, :, :, 1 - c, :],
                               s4.unsqueeze(1).to_broadcast([P, 10, 2, 16]), ALU.mult))
            ch.sync()
            for t in range(TT):
                ch.mark(tt(rot_a[:, t, :], rot_a[:, t, :], rot_b[:, t, :], ALU.add))
            ch.sync()
            gp.memset(tick[:, :], 0.0).then_inc(att_rope, 1)
            pool.wait_ge(g_ready, 1)
            wait_full(pool, USE["to_tok"][9])
            for n in range(8):
                d, st = n // 4, n % 4
                tt(quad(X[:, n, :]), bc_out(const(("le", "ge")[d]), NH), bc_in(g[:, st, 4 * d:4 * d + 4], P), ALU.mult).then_inc(gtri_ready, 1)
            for n in range(8):
                wait_read(pool, USE["decay"][n])
                tt(quad(UT[:, n, :]), quad(UT[:, n, :]), bc_out(const(("neg_f", "neg_b")[n // 4]), NH), ALU.add).then_inc(dmask, 1)
            for st in range(4):
                for d in range(2):
                    if d:
                        wait_read(pool, USE["kk"][st])
                    else:
                        pool.wait_ge(ut_part, st + 1)
                    n = 4 * d + st
                    tt(quad(UT[:, n, :]), quad(UT[:, n, :]), bc_in(beta[:, st, 4 * d:4 * d + 4], P), ALU.mult).then_inc(ut_ready, 1)
            pool.wait_ge(ut_ready, 8)
            for level in range(1, LEVELS):
                for n in range(8):
                    if level > 1:
                        wait_full(pool, USE["q", level - 1][n])
                    tt(quad(BP[:, n, :]), quad(UT[:, n, :]), bc_out(levels[:, n // 4, level, :], NH), ALU.mult).then_inc(blocks_ready, 1)
            wait_full(pool, USE["q", LEVELS - 1][7])
            for s in range(3):
                for d in range(2):
                    st = ORDER[d][s]
                    if s:
                        wait_full(pool, USE["ds", s - 1, d])
                    tt(quad(kt_st[:, d, :]), quad(ktok[:, st, :]), bc_in(etail[:, st, 4 * d:4 * d + 4], P), ALU.mult).then_inc(ktail_ready, 1)
            pool.wait_ge(h_ready, 4)
            ch.mark(gp.memset(cu[:, :, 0:15], 0.0))
            ch.mark(gp.memset(cu[:, :, T + 15:T + 30], 0.0))
            def tap_matrices(n):
                for half, dst in enumerate(tap_diags[n % 2]):
                    taps = min(16, CONF_K - 16 * half)
                    at = CONF_K * CONV_PE[n] + 16 * half
                    tt(dst[:, 0:taps * P].rearrange("p (a b) -> p a b", a=taps), bc_out(ident, taps),
                       bc_in(col("conf_dw_w")[:, at:at + taps], P), ALU.mult).then_inc(taps_ready, 1)

            tap_matrices(0)
            for use in USE["norm3"]:
                wait_full(pool, use)
            tap_matrices(1)
            ch.mark(gp.memset(bbd.rearrange("p a b c -> p (a b c)"), 0.0))
            ch.sync()
            gp.memset(tick[:, :], 0.0).then_inc(margins, 1)
            wait_full(pool, USE["conv31"][0])
            tap_matrices(2)
            pool.wait_ge(h_ready, 8)
            ch.mark(gp.memset(cin2[:, :, 0:2], 0.0))
            ch.sync()
            gp.memset(tick[:, :], 0.0).then_inc(margins, 1)

            def tables(i):
                grid = lambda x: x.rearrange("p (a b) -> p a b", a=16)
                c_b, c_a = (small_trig[:, 0, i, at:at + 16] for at in (0, 16))
                s_b, s_a = (small_trig[:, 1, i, at:at + 16] for at in (0, 16))
                if i:
                    pool.wait_ge(s5_tab, i)
                for out_at, (x, y, op) in enumerate((((c_a, c_b), (s_a, s_b), ALU.subtract),
                                                     ((s_a, c_b), (c_a, s_b), ALU.add))):
                    ch.mark(tt(grid(etmp[:, 0, :]), bc_in(x[0], 16), bc_out(x[1], 16), ALU.mult))
                    ch.mark(tt(grid(etmp[:, 1, :]), bc_in(y[0], 16), bc_out(y[1], 16), ALU.mult))
                    ch.sync()
                    last = tt(etab[:, i % 2, out_at, :], etmp[:, 0, :], etmp[:, 1, :], op)
                    if out_at == 0:
                        ch(last)
                last.then_inc(s5_tab, 1)

            for i in range(S5T):
                if i >= 2:
                    pool.wait_ge(s5_n, i - 1)
                tables(i)
            for n in range(4):
                kt, h0 = n // 2, 4 * (n % 2)
                wait_read(pool, USE["cum_k"][n])
                dst = ck1[:, h0:h0 + 4, P:2 * P] if kt else ck0[:, h0:h0 + 4, :]
                tt(dst, dst, bc_out(const("neg_b"), 4), ALU.subtract).then_inc(masked, 1)


def lay_out(inputs):
    a = {k: np.asarray(x) for k, x in inputs.items()}

    def stationary(wt, per):
        nb = wt.shape[1] // P
        x = wt.reshape(KT, P, nb, P).transpose(2, 1, 0, 3).reshape(nb // per, per, P, D)
        return x.transpose(0, 2, 1, 3).reshape(nb // per, P, per * D)

    def moving(wt, per):
        x = wt.reshape(wt.shape[0] // P // per, per, P, D)
        return x.transpose(0, 2, 1, 3).reshape(-1, P, per * D)

    def by_columns(wt, width):
        n = wt.shape[1] // width
        return wt.reshape(KT, P, n, width).transpose(2, 1, 0, 3).reshape(n, P, KT * width)

    def cols_of(x):
        return x.reshape(-1, P).T

    w = {}
    for layer in range(2):
        w[f"mod{layer}"] = by_columns(a["w_mod"][layer], MOD_C)
        wi, wo = a["w_ffn_in"][layer], a["w_ffn_out"][layer]
        w[f"ffn{layer}"] = np.concatenate(
            [stationary(wi[:, :FFN_H], 1), stationary(wi[:, FFN_H:], 1), moving(wo, 1)], 2)
    hyb = a["hyb_w_in"][0]
    qkv, z_a, ba_w, q_b, k_b, v_b = np.split(hyb, np.cumsum([1536, 512, 16, 512, 128]), 1)
    pairs = [0, 4, 1, 5, 2, 6, 3, 7]
    q_b = q_b.reshape(D, AH, AHD)[:, pairs].reshape(D, 512)
    w["hyb_f"] = stationary(np.concatenate([qkv[:, 512:1024], qkv[:, 1024:], qkv[:, :512]], 1), 3)
    w["hyb_t"] = by_columns(np.concatenate([z_a, q_b, k_b, v_b, ba_w], 1), HYB_TC)
    wo = a["hyb_w_out"][0]
    w["hyb_o"] = moving(np.concatenate([wo[:512], wo[512:].reshape(AH, AHD, D)[pairs].reshape(512, D)], 0), 2)
    ci = a["conf_w_in"][0].reshape(D, 2, KT, P).transpose(0, 2, 1, 3).reshape(D, 2 * D)
    w["conf_i"] = stationary(ci, 2)
    w["conf_o"] = moving(a["conf_w_out"][0], 2)
    u, xbc, qk, vf, gates = np.split(a["w_in_2"][0], np.cumsum([512, 1536, 1024, 520]), 1)
    w["in_a"] = stationary(np.concatenate([u, qk], 1), 3)
    w["in_v"] = by_columns(vf, V2C)
    w["in_b"] = stationary(xbc, 3)
    w["in_g"] = stationary(gates.reshape(D, 3, KT, P).transpose(0, 2, 1, 3).reshape(D, 3 * D), 3)
    br = a["w_branch_2"][0].reshape(12, P, KT, P).transpose(2, 1, 0, 3).reshape(4, 2, P, 12 * P)
    w["branch"] = br.transpose(0, 2, 1, 3).reshape(4, P, 2 * 12 * P)
    w["out2"] = moving(a["w_out_2"][0], 2)
    w["ff"] = np.concatenate([stationary(a["w_ff1_2"][0], 1), moving(a["w_ff2_2"][0], 1)], 2)

    cond = np.stack([cols_of(a["c"][0]), cols_of(a["c_ctx"])], 2).reshape(P, 16)
    order = [4, 5, 6, 7, 8, 9, 10, 11, 0, 1, 2, 3]
    state = lambda x: x.reshape(S5T, P).T
    packed = {
        "cond": cond, "hyb_conv": a["hyb_conv_w"][0].reshape(CONV_A, 12, P)[:, order].transpose(2, 1, 0),
        "conf_dw_w": a["conf_dw_w"][0].reshape(CONF_K, KT, P).transpose(2, 1, 0),
        "conv_w_2": a["conv_w_2"][0].reshape(3, 4, P).transpose(2, 1, 0), "s5_d": cols_of(a["s5_d_2"][0]),
        "b_gate_2": a["b_gate_2"][0].reshape(3, KT, P).transpose(2, 1, 0),
        "a_re": state(a["s5_a_re_2"][0]), "a_im": state(a["s5_a_im_2"][0]),
        "log_dt": state(np.repeat(a["s5_log_dt_2"][0], 64)),
    }
    for name, n in COLS:
        if name not in packed:
            packed[name] = cols_of(a[name])
    cols = np.concatenate([packed[n].reshape(P, -1) for n, _ in COLS], 1)
    flat = {
        "a_log": a["hyb_a_log"].reshape(-1), "dt_bias": a["hyb_dt_bias"].reshape(-1), "b_f": a["fox_b_f_2"][0],
        "out_norm": a["hyb_out_norm"][0],
        "qk_norm": np.concatenate([np.tile(a["hyb_q_norm"][0], AH), np.tile(a["hyb_k_norm"][0], 2)]),
    }
    rows = np.broadcast_to(np.concatenate([flat[n] for n, _ in ROWS]), (P, NROWS))
    def s5_c(x):
        out = np.zeros((S5T, 2, 64, 2, 16), x.dtype)
        x = x.reshape(S5T, 2, 16, 64)
        for g2 in range(2):
            out[:, g2, :, g2, :] = x[:, g2].transpose(0, 2, 1)
        return out.reshape(S5T, P, 32).transpose(1, 0, 2)

    glu = np.zeros((4, 8, 16, 8, 16), a["s5_w_glu_2"].dtype)
    wg = a["s5_w_glu_2"][0].reshape(4, 8, 16, 16)
    for g8 in range(8):
        glu[:, g8, :, g8, :] = wg[:, g8]
    s5_b = lambda x: x.reshape(S5T, P, 16).transpose(1, 0, 2).reshape(P, 256)
    out = {f"w_{k}": x for k, x in w.items()}
    out.update(
        cols=cols, rows=rows, consts=constants(), b_out=a["conf_b_out"].reshape(1, D),
        c_bd=np.stack([s5_c(a["s5_c_re_2"][0]), s5_c(a["s5_c_im_2"][0])], 1).reshape(P, 1024),
        glu=glu.reshape(4, P, P).transpose(1, 0, 2).reshape(P, 512),
        b_s5=np.concatenate([s5_b(a["s5_b_re_2"][0]), s5_b(a["s5_b_im_2"][0])], 1),
        x=a["x"][0], ctx=a["ctx"][0])
    return {k: np.ascontiguousarray(x) for k, x in out.items()}


def kernel(**inputs):
    import concourse.bacc as bacc
    from concourse.bass_utils import run_bass_kernel_spmd

    arrays = lay_out(inputs)
    nc = bacc.Bacc("TRN2", target_bir_lowering=False, num_devices=1)
    at = {k: nc.dram_tensor(f"in_{k}", x.shape, F32, kind="ExternalInput").ap() for k, x in arrays.items()}
    out = nc.dram_tensor("out_0", (T, D), F32, kind="ExternalOutput").ap()
    build(nc, {name: at[f"w_{name}"] for name, _, _ in STREAM}, at["w_mod1"], at["cols"], at["rows"], at["consts"],
          at["b_out"], at["c_bd"], at["glu"], at["b_s5"], at["x"], at["ctx"], out)
    r = run_bass_kernel_spmd(nc, [{f"in_{k}": x for k, x in arrays.items()}], core_ids=[0])
    return r.results[0]["out_0"].reshape(1, T, D)
```
